# Optimizing a Trainium2 kernel written in Bass

```python
import math
import jax, jax.numpy as jnp
from jax import lax
import numpy as np

D_MODEL = 1024
BATCH = 1
SEQ = 512
DEPTH = 2

N_A_LAYERS = DEPTH // 2
N_B_LAYERS = DEPTH - N_A_LAYERS

PLE_DIM = 256
D_FF = 4 * D_MODEL
NORM_EPS = 1e-6

RWKV_HEAD = 64
RWKV_HEADS = D_MODEL // RWKV_HEAD
DECAY_LORA = max(32, int(round(D_MODEL ** 0.5 * 1.8 / 32)) * 32)
AAA_LORA = max(32, int(round(D_MODEL ** 0.5 * 1.8 / 32)) * 32)
GATE_LORA = max(32, int(round(0.6 * D_MODEL ** 0.8 / 32)) * 32)
GN_EPS = 64e-5

DIFF_HEAD = 64
DIFF_HEADS = D_MODEL // (2 * DIFF_HEAD)
DIFF_QK = DIFF_HEADS * 2 * DIFF_HEAD
DIFF_V = DIFF_HEADS * 2 * DIFF_HEAD
Q_BLOCK = 128

N_BUCKETS = 32
MAX_DIST = 128

kernel_name = "yoco_rwkv7_diffattn_hybrid"

def rmsnorm(x, g, eps=NORM_EPS):
    xf = x.astype(jnp.float32)
    y = xf * lax.rsqrt(jnp.mean(xf * xf, axis=-1, keepdims=True) + eps)
    return (y * g.astype(jnp.float32)).astype(x.dtype)

def squared_relu_mlp(h, w1, w2):
    return jnp.square(jax.nn.relu(h @ w1)) @ w2

def ple_inject(x, p_i, g, w_up, w_gate):
    gate = jax.nn.sigmoid(rmsnorm(x, g) @ w_gate)
    return x + (p_i @ w_up) * gate

def rwkv7_recurrence(r, w, k, v, a, b):
    Bn, _, H, N = r.shape
    tm = lambda t: jnp.moveaxis(t.astype(jnp.float32), 1, 0)

    def step(S, inp):
        r_t, w_t, k_t, v_t, a_t, b_t = inp
        Sa = jnp.einsum('bhvk,bhk->bhv', S, a_t)
        S = S * w_t[:, :, None, :] + Sa[..., None] * b_t[:, :, None, :] + v_t[..., None] * k_t[:, :, None, :]
        y = jnp.einsum('bhvk,bhk->bhv', S, r_t)
        return S, y

    S0 = jnp.zeros((Bn, H, N, N), jnp.float32)
    _, y = lax.scan(step, S0, (tm(r), tm(w), tm(k), tm(v), tm(a), tm(b)))
    return jnp.moveaxis(y, 0, 1)

def rwkv7_time_mix(h, mix, w_rkvo, w0, w1, w2, a0, a1, a2, g1, g2, k_k, k_a, r_k, ln_w, ln_b):
    Bn, T, C = h.shape
    H, N = RWKV_HEADS, RWKV_HEAD
    heads = lambda t: t.reshape(Bn, T, H, N)
    h_prev = jnp.pad(h[:, :-1], ((0, 0), (1, 0), (0, 0)))
    dx = h_prev - h
    xr = h + dx * mix[0]
    xw = h + dx * mix[1]
    xk = h + dx * mix[2]
    xv = h + dx * mix[3]
    xa = h + dx * mix[4]
    xg = h + dx * mix[5]
    r = xr @ w_rkvo[0]
    k = xk @ w_rkvo[1]
    v = xv @ w_rkvo[2]
    w_log = -jax.nn.softplus(-(w0 + jnp.tanh(xw @ w1) @ w2)) - 0.5
    decay = jnp.exp(-jnp.exp(w_log.astype(jnp.float32)))
    a = jax.nn.sigmoid(a0 + (xa @ a1) @ a2)
    g = jax.nn.sigmoid(xg @ g1) @ g2
    kk = heads((k * k_k).astype(jnp.float32))
    kk = kk / jnp.maximum(jnp.sqrt(jnp.sum(kk * kk, axis=-1, keepdims=True)), 1e-12)
    k = k * (1 + (a - 1) * k_a)
    y = rwkv7_recurrence(heads(r), heads(decay), heads(k), heads(v), -kk, kk * heads(a).astype(jnp.float32))
    mu = jnp.mean(y, axis=-1, keepdims=True)
    var = jnp.mean(jnp.square(y - mu), axis=-1, keepdims=True)
    y = ((y - mu) * lax.rsqrt(var + GN_EPS)).reshape(Bn, T, C)
    y = (y * ln_w.astype(jnp.float32) + ln_b.astype(jnp.float32)).astype(h.dtype)
    bonus = jnp.sum(heads(r) * heads(k) * r_k, axis=-1, keepdims=True) * heads(v)
    y = (y + bonus.reshape(Bn, T, C)) * g
    return y @ w_rkvo[3]

def t5_bucket(rel):
    n = jnp.maximum(rel, 0)
    max_exact = N_BUCKETS // 2
    nf = jnp.maximum(n, 1).astype(jnp.float32)
    large = max_exact + (jnp.log(nf / max_exact) / math.log(MAX_DIST / max_exact)
                         * (N_BUCKETS - max_exact)).astype(jnp.int32)
    large = jnp.minimum(large, N_BUCKETS - 1)
    return jnp.where(n < max_exact, n, large)

def shared_kv(x, kv_norm_g, w_k, w_v, k_norm_g):
    Bn, S, _ = x.shape
    h = rmsnorm(x, kv_norm_g)
    k = rmsnorm((h @ w_k).reshape(Bn, S, DIFF_HEADS, 2, DIFF_HEAD), k_norm_g)
    v = (h @ w_v).reshape(Bn, S, DIFF_HEADS, 2 * DIFF_HEAD)
    return jnp.transpose(k, (0, 2, 3, 1, 4)), jnp.transpose(v, (0, 2, 1, 3))

def diff_attention(h, k, v, rel_bias, w_q, q_norm_g, lam, subln_g, w_o, layer_idx):
    Bn, S, _ = h.shape
    H, d = DIFF_HEADS, DIFF_HEAD
    lambda_init = 0.8 - 0.6 * math.exp(-0.3 * layer_idx)
    lamf = lam.astype(jnp.float32)
    lam_full = (jnp.exp(jnp.sum(lamf[0] * lamf[1])) - jnp.exp(jnp.sum(lamf[2] * lamf[3]))
                + lambda_init)
    q = rmsnorm((h @ w_q).reshape(Bn, S, H, 2, d), q_norm_g)
    nb = S // Q_BLOCK
    qb = jnp.transpose(q.reshape(Bn, nb, Q_BLOCK, H, 2, d), (1, 0, 3, 4, 2, 5))
    k_pos = jnp.arange(S, dtype=jnp.int32)
    scale = d ** -0.5

    def block(args):
        i, q_blk = args
        q_pos = i * Q_BLOCK + jnp.arange(Q_BLOCK, dtype=jnp.int32)
        rel = q_pos[:, None] - k_pos[None, :]
        bias = jnp.transpose(rel_bias[t5_bucket(rel)].astype(jnp.float32), (2, 0, 1))
        logits = jnp.einsum('bhcqd,bhckd->bhcqk', q_blk, k).astype(jnp.float32) * scale
        logits = logits + bias[None, :, None]
        logits = jnp.where(rel >= 0, logits, -jnp.inf)
        probs = jax.nn.softmax(logits, axis=-1)
        attn = probs[:, :, 0] - lam_full * probs[:, :, 1]
        return jnp.einsum('bhqk,bhkv->bhqv', attn.astype(v.dtype), v)

    o = lax.map(block, (jnp.arange(nb, dtype=jnp.int32), qb))
    o = jnp.transpose(o, (1, 0, 3, 2, 4)).reshape(Bn, S, H, 2 * d)
    o = rmsnorm(o, subln_g) * (1 - lambda_init)
    return o.reshape(Bn, S, H * 2 * d) @ w_o

def setup_inputs(seed: int = 0) -> dict:
    key = jax.random.key(seed)
    ks = iter(jax.random.split(key, 40))
    nrm = lambda shape, s: jax.random.normal(next(ks), shape, jnp.float32) * s
    uni = lambda shape, lo, hi: jax.random.uniform(next(ks), shape, jnp.float32, lo, hi)
    D, NA, NB = D_MODEL, N_A_LAYERS, N_B_LAYERS
    return {
        "x": nrm((BATCH, SEQ, D), 1.0),
        "p": nrm((DEPTH, BATCH, SEQ, PLE_DIM), 1.0),
        "norm_g": 1.0 + nrm((DEPTH, 3, D), 0.05),
        "mlp_w1": nrm((DEPTH, D, D_FF), D ** -0.5),
        "mlp_w2": nrm((DEPTH, D_FF, D), D_FF ** -0.5),
        "ple_w_up": nrm((DEPTH, PLE_DIM, D), PLE_DIM ** -0.5),
        "ple_w_gate": nrm((DEPTH, D, D), D ** -0.5),
        "rwkv_mix": uni((NA, 6, D), 0.0, 1.0),
        "rwkv_w_rkvo": nrm((NA, 4, D, D), D ** -0.5),
        "rwkv_w0": uni((NA, D), -4.0, 1.0),
        "rwkv_w1": nrm((NA, D, DECAY_LORA), D ** -0.5),
        "rwkv_w2": nrm((NA, DECAY_LORA, D), 0.5 * DECAY_LORA ** -0.5),
        "rwkv_a0": nrm((NA, D), 0.1),
        "rwkv_a1": nrm((NA, D, AAA_LORA), D ** -0.5),
        "rwkv_a2": nrm((NA, AAA_LORA, D), AAA_LORA ** -0.5),
        "rwkv_g1": nrm((NA, D, GATE_LORA), D ** -0.5),
        "rwkv_g2": nrm((NA, GATE_LORA, D), GATE_LORA ** -0.5),
        "rwkv_k_k": 0.85 + nrm((NA, D), 0.05),
        "rwkv_k_a": 1.0 + nrm((NA, D), 0.05),
        "rwkv_r_k": nrm((NA, RWKV_HEADS, RWKV_HEAD), 0.1),
        "rwkv_ln_w": 1.0 + nrm((NA, D), 0.05),
        "rwkv_ln_b": nrm((NA, D), 0.02),
        "kv_norm_g": 1.0 + nrm((D,), 0.05),
        "w_k_shared": nrm((D, DIFF_QK), D ** -0.5),
        "w_v_shared": nrm((D, DIFF_V), D ** -0.5),
        "k_norm_g": 1.0 + nrm((DIFF_HEAD,), 0.05),
        "diff_w_q": nrm((NB, D, DIFF_QK), D ** -0.5),
        "diff_q_norm_g": 1.0 + nrm((NB, DIFF_HEAD), 0.05),
        "diff_lam": nrm((NB, 4, DIFF_HEAD), 0.1),
        "diff_subln_g": 1.0 + nrm((NB, 2 * DIFF_HEAD), 0.05),
        "diff_w_o": nrm((NB, DIFF_V, D), DIFF_V ** -0.5),
        "rel_bias": nrm((N_BUCKETS, DIFF_HEADS), 0.5),
    }

def reference(x, p, norm_g, mlp_w1, mlp_w2, ple_w_up, ple_w_gate,
              rwkv_mix, rwkv_w_rkvo, rwkv_w0, rwkv_w1, rwkv_w2, rwkv_a0, rwkv_a1, rwkv_a2,
              rwkv_g1, rwkv_g2, rwkv_k_k, rwkv_k_a, rwkv_r_k, rwkv_ln_w, rwkv_ln_b,
              kv_norm_g, w_k_shared, w_v_shared, k_norm_g,
              diff_w_q, diff_q_norm_g, diff_lam, diff_subln_g, diff_w_o, rel_bias):
    k_sh = None
    v_sh = None
    for layer in range(DEPTH):
        if layer < N_A_LAYERS:
            i = layer
            h = rmsnorm(x, norm_g[layer, 0])
            x = x + rwkv7_time_mix(h, rwkv_mix[i], rwkv_w_rkvo[i], rwkv_w0[i], rwkv_w1[i], rwkv_w2[i],
                                   rwkv_a0[i], rwkv_a1[i], rwkv_a2[i], rwkv_g1[i], rwkv_g2[i],
                                   rwkv_k_k[i], rwkv_k_a[i], rwkv_r_k[i], rwkv_ln_w[i], rwkv_ln_b[i])
        else:
            j = layer - N_A_LAYERS
            if j == 0:
                k_sh, v_sh = shared_kv(x, kv_norm_g, w_k_shared, w_v_shared, k_norm_g)
            h = rmsnorm(x, norm_g[layer, 0])
            x = x + diff_attention(h, k_sh, v_sh, rel_bias, diff_w_q[j], diff_q_norm_g[j],
                                   diff_lam[j], diff_subln_g[j], diff_w_o[j], layer)
        x = x + squared_relu_mlp(rmsnorm(x, norm_g[layer, 1]), mlp_w1[layer], mlp_w2[layer])
        x = ple_inject(x, p[layer], norm_g[layer, 2], ple_w_up[layer], ple_w_gate[layer])
    return x


_drawn_inputs = setup_inputs


def setup_inputs(seed=0):
    import zlib

    import numpy as np

    out = dict(_drawn_inputs(seed))
    spreads = {}
    factors = {'rwkv_w1': 2.931,
     'rwkv_w2': 2.918,
     'rwkv_a0': 2.71,
     'rwkv_k_k': 4.864,
     'rwkv_ln_b': 4.792,
     'kv_norm_g': 2.918,
     'k_norm_g': 5.953,
     'diff_q_norm_g': 5.622,
     'diff_lam': 7.351,
     'diff_subln_g': 3.316}
    for name, (base, spread) in spreads.items():
        noise = np.random.default_rng([zlib.crc32(name.encode()), seed]).standard_normal(out[name].shape)
        drawn = base * np.exp(spread * noise) if base else spread * noise
        out[name] = __import__('jax').numpy.asarray(drawn.astype(out[name].dtype))
    for name, factor in factors.items():
        out[name] = (out[name] * factor).astype(out[name].dtype)
    return out
```

```python
import math
from contextlib import ExitStack

import numpy as np

import concourse.bass as bass
from concourse import mybir

F32 = mybir.dt.float32
F32R = mybir.dt.float32r
ALU = mybir.AluOpType
ACT = mybir.ActivationFunctionType
AX = mybir.AxisListType

P = 128
D = 1024
S = 512
CT = D // P
TT = S // P
FF = 4 * D
PLE = 256
HD = 64
CH = 64
QUAD = 4
NQ = CT * S // (CH * QUAD)
LEVELS = 6
BUCKETS, MAX_DIST = 32, 128
LAMBDA_INIT = 0.8 - 0.6 * math.exp(-0.3)
KAPPA = math.exp(-0.5)
NEG = -1.0e30
NORM_EPS, GN_EPS = 1e-6, 64e-5

(V_N00, V_N01, V_N02, V_N10, V_N11, V_N12, V_KV, V_MIX, _1, _2, _3, _4, _5,
 V_W0, V_A0, V_KK, V_KA, V_LNW, V_LNB, V_RK) = range(20)
NV = 20
MIX_R, MIX_W, MIX_K, MIX_V, MIX_A, MIX_G = range(6)

C_ID, C_BONES, C_ONES = 0, 128, 256
C_LVL = 384
C_LVT = C_LVL + LEVELS * P
C_TRS = C_LVT + P
C_SEG = C_TRS + 2 * CH
C_END = C_SEG + S
C_HOT = C_END
C_ALL = C_HOT + 640


def shape_constants():
    c = np.zeros((P, C_ALL), np.float32)
    i = np.arange(P)
    c[:, C_ID:C_ID + P] = np.eye(P)
    c[:, C_BONES:C_BONES + P] = (i[:, None] // HD) == (i[None, :] // HD)
    c[:, C_ONES:C_ONES + P] = 1
    for lv in range(LEVELS):
        b = 1 << lv
        low = ((i[:, None] // (2 * b)) == (i[None, :] // (2 * b))) & ((i[:, None] // b) % 2 == 1) & ((i[None, :] // b) % 2 == 0)
        c[:, C_LVL + lv * P:C_LVL + (lv + 1) * P] = low
        if lv == 0:
            c[:, C_LVT:C_LVT + P] = low.T
    s, t = (i % CH)[:, None], np.arange(CH)[None, :]
    c[:, C_TRS:C_TRS + CH] = s < t
    c[:, C_TRS + CH:C_TRS + 2 * CH] = s <= t
    c[:, C_SEG:C_SEG + S] = (np.arange(S) % CH != 0)[None, :]
    for x in range(640):
        n = x - (P - 1)
        if n < 0:
            c[BUCKETS, C_HOT + x] = 1
            continue
        b = n
        if n >= BUCKETS // 2:
            b = BUCKETS // 2 + int(math.log(n / (BUCKETS // 2)) / math.log(MAX_DIST / (BUCKETS // 2)) * (BUCKETS // 2) + 1e-9)
        c[min(b, BUCKETS - 1), C_HOT + x] = 1
    return c


class Link:

    def __init__(self, eng, sem):
        self.eng, self.sem, self.n = eng, sem, 0

    def mark(self, ins):
        ins.then_inc(self.sem, 1)
        self.n = self.n + 1

    def wait(self):
        self.eng.wait_ge(self.sem, self.n)

    def __call__(self, ins):
        self.mark(ins)
        self.wait()


N_W1, N_A1, N_G1, N_WA2, N_K, N_R, N_V, N_G2, N_WO = 0, 1, 2, 3, 4, 8, 12, 16, 17
L_MLP = (21, 74)
N_KS, N_VS, N_Q, N_DO = 58, 62, 66, 70
N_ALL = 111
X_W, X_A, X_G, X_K, X_R, X_V, X_Y, X_M0, X_P0, X_KV, X_Q, X_O, X_M1, X_P1 = (8 * i for i in range(14))


def trunk(nc, x, p, norm_g, mlp_w1, mlp_w2, ple_w_up, ple_w_gate, rwkv_mix, rwkv_w_rkvo, rwkv_w0, rwkv_w1,
          rwkv_w2, rwkv_a0, rwkv_a1, rwkv_a2, rwkv_g1, rwkv_g2, rwkv_k_k, rwkv_k_a, rwkv_r_k, rwkv_ln_w,
          rwkv_ln_b, kv_norm_g, w_k_shared, w_v_shared, k_norm_g, diff_w_q, diff_q_norm_g, diff_lam,
          diff_subln_g, diff_w_o, rel_bias, consts, out):
    bias_rows = nc.dram_tensor("bias_rows", [8, 640], F32, kind="Internal").ap()
    ctx = ExitStack()
    with ctx:
        slab_bytes = 212800
        base = (nc.sbuf_base + 31) // 32 * 32
        ctx.enter_context(nc.sbuf_tensor("slab", [P, (slab_bytes + 32) // 4], F32))

        def at(name, offset, shape, dtype=F32):
            size = int(np.prod(shape[1:])) * 4
            assert offset + size <= slab_bytes, (name, offset, size)
            return nc.alloc_sbuf_tensor_at(name, shape, dtype, offset=base + offset)

        W_RAW, W_HI, W_LO, XH, XL, XX = 0, 16384, 32768, 49152, 65536, 81920
        ST, HIDH, HIDL, RSTD, TMP, CST = 98432, 180352, 186496, 192640, 194688, 202880
        wraw = at("wraw", W_RAW, [P, 2, 2048])
        whi = at("whi", W_HI, [P, 2, 2048], F32R)
        wlo = at("wlo", W_LO, [P, 2, 2048], F32R)
        xh = at("xh", XH, [P, CT, S], F32R)
        xl = at("xl", XL, [P, CT, S], F32R)
        X = at("X", XX, [P, CT, S + 4])
        lora_h = at("lora_h", HIDH, [P, 3, S], F32R)
        lora_l = at("lora_l", HIDL, [P, 3, S], F32R)
        rstd = at("rstd", RSTD, [P, S])
        tmp = at("tmp", TMP, [P, 4, S])
        cst = at("cst", CST, [P, C_END])
        PV = at("PV", CST + 4 * C_END, [P, CT, NV])
        small = at("small", CST + 4 * C_END + 4 * CT * NV, [P, 224])
        hv = small[:, 0:4]
        nlnw = small[:, 4:12]
        omka = small[:, 12:20]
        gC = small[:, 20:84]
        eps_n, eps_g, eps_0 = small[:, 84:85], small[:, 85:86], small[:, 86:87]
        lamf = small[:, 87:88]
        st_m, st_n, st_l, st_r, st_c = (small[:, 88 + 4 * k:92 + 4 * k] for k in range(5))
        lamw = small[:, 108:112]
        omix = small[:, 112:160]
        omix3 = omix.rearrange("p (c m) -> p c m", m=6)
        subg = small[:, 160:161]
        qg8 = small[:, 161:162]

        St = at("St", ST, [P, 5, CT, S])
        LW, R_, K_, A_, V_ = range(5)
        xtok = at("xtok", ST + 4 * 16384, [P, TT, D])
        vrows = at("vrows", ST + 3 * 16384, [NV, D])
        hrows = at("hrows", ST + 3 * 16384 + 4096, [3, P])
        xtok2 = at("xtok2", ST, [P, TT, D])
        prep_a = at("prep_a", HIDH, [P, S])
        prep_b = at("prep_b", HIDL, [P, S])
        sets = [[at(f"{n}{k}", XH + 14336 * k + o, [P, QUAD, w]) for n, o, w in (
            ("Btok", 0, P), ("Ktok", 2048, P), ("Vtok", 4096, P), ("LakT", 6144, P), ("LrbT", 8192, CH),
            ("LrkT", 9216, CH), ("TiT", 10240, P), ("Abd", 12288, P))] for k in range(2)]
        Pm = at("Pm", XH + 28672, [P, QUAD, P])
        Hs = at("Hs", XH + 30720, [P, 2, P])
        Zs = at("Zs", XH + 31744, [P, P])
        Us = at("Us", XH + 32256, [P, P])
        Hg = at("Hg", HIDH, [P, P])
        Bbd = at("Bbd", TMP, [P, QUAD, P])
        Kbd = at("Kbd", TMP + 2048, [P, QUAD, P])
        Vbd = at("Vbd", TMP + 4096, [P, QUAD, P])
        LabT = at("LabT", TMP + 6144, [P, QUAD, P])
        Ti = at("Ti", RSTD, [P, QUAD, P])
        hid_h = at("hid_h", ST, [P, 16, S], F32R)
        hid_l = at("hid_l", ST + 32768, [P, 16, S], F32R)
        UP = at("UP", ST + 65536, [P, CT, S])
        ptok = at("ptok", ST + 65536, [P, TT, PLE])
        KT = at("KT", ST, [P, CT, S])
        QT = at("QT", ST + 16384, [P, CT, S])
        VT = at("VT", ST + 32768, [P, CT, TT, P])
        strip = at("strip", ST + 49152, [P, 8, S])
        Lg = at("Lg", ST + 65536, [P, 2, S])
        Pr = [at("Pr0", ST + 69632, [P, 2, S]), at("Pr1", HIDH, [P, 2, S])]
        At = at("At", ST + 73728, [P, 2, S])
        ATt = at("ATt", ST + 77824, [P, 2, S])
        hot = at("hot", ST + 65536, [P, 640])
        relb = at("relb", ST + 69632, [P, 8])
        bvec = at("bvec", ST + 73728, [8, 640])
        lrow = at("lrow", HIDH + 4096, [P, 4, HD])
        OT = at("OT", ST, [P, TT, D])

        pb = [ctx.enter_context(nc.psum_tensor(f"pb{i}", [P, S], F32)) for i in range(8)]

        ident = cst[:, C_ID:C_ID + P]
        bones = cst[:, C_BONES:C_BONES + P]
        ones = cst[:, C_ONES:C_ONES + P]

        def lvl(lv):
            return cst[:, C_LVL + lv * P:C_LVL + (lv + 1) * P]

        names = """raw0 raw1 w_hi w_lo pe_step cst_in x_in rows_in hrows_in x2_in p_in lam_in hot_in
            rel_in bvec_out strip_in out_st x_tr xt_cp xt_sq par_tr par_ev small_set gains lam_s lam_e lam_rdy
            h_ready mix_a mix_b x_hi x_ready acc norm_ps norm_rt dense_a dense_v act_link vec_link pool_link
            lora_hi lora_rdy g_cum exps kk_sq kk_ps kk_rt prep
            bd_a bd_p bd_zero sc_mm sc_ev tr_mm tr_ev lab_ev t0 tt0 lv_p lv_pe lv_t lv_te ch z_ev h_ev hg y_mm y_ev
            mu_mm yc_rdy gn_sq gn_ps gn_rt pr_rdy bon_ps y_fin x2_tr x2_cp
            hid_f hid_hi hid_rdy sq_rdy p_tr p_hi p_rdy sig upd far_row bv_mm bv_ev
            qk_sq qk_ps qk_rt qk_n v_tr v_ev s_mm lg nm pexp at_rdy at_tr at_ev o_mm o_sq o_ps o_rt o_f
            fin_tr fin_ev""".split()
        sem = {n: ctx.enter_context(nc.semaphore(n)) for n in names}
        s = type("Sems", (), sem)

        def vec(c, v):
            return PV[:, c, v:v + 1]

        def block_rows(w, m2):
            return w.rearrange("(k p) n -> p k n", p=P)[:, :, bass.ds(m2 * 256, 256)]

        block = ctx.enter_context(nc.Block())

        @block.sync
        def _(sp):
            for t in range(TT):
                sp.dma_start(xtok[:, t, :], x[0, t * P:(t + 1) * P, :]).then_inc(s.x_in, 16)
            raw = (s.raw0, s.raw1)

            def slot_free(n):
                sp.wait_ge(s.w_lo, n - 1)

            def load(n, par, parts):
                for dst, src in parts:
                    sp.dma_start(dst, src).then_inc(raw[par], 16)

            r0 = wraw[:, 0, :]
            r1 = wraw[:, 1, :]

            def cols(r, w, k=CT):
                return r[:, 0:k * w].rearrange("p (k n) -> p k n", n=w)
            w1v = rwkv_w1[0].rearrange("(k p) n -> p k n", p=P)
            a1v = rwkv_a1[0].rearrange("(k p) n -> p k n", p=P)
            g1v = rwkv_g1[0].rearrange("(k p) n -> p k n", p=P)
            load(0, 0, [(cols(r0, P)[:, :, 0:64], w1v), (cols(r0, P)[:, :, 64:128], w1v)])
            load(1, 1, [(cols(r1, P)[:, :, 0:64], a1v), (cols(r1, P)[:, :, 64:128], a1v)])
            slot_free(2)
            load(2, 0, [(cols(r0, 256)[:, :, 0:128], g1v[:, :, 0:128]),
                        (cols(r0, 256)[:, :, 128:256], g1v[:, :, 32:160])])
            slot_free(3)
            load(3, 1, [(r1[0:64, 0:1024], rwkv_w2[0]), (r1[64:128, 0:1024], rwkv_a2[0])])

            def square(w, n0):
                with sp.Fori(0, 2) as i:
                    for h in range(2):
                        sp.wait_ge(s.w_lo, n0 + 2 * i + h - 1)
                        v = block_rows(w, 2 * i + h)
                        for q in range(2):
                            sp.dma_start(cols(wraw[:, (n0 + h) % 2, :], 256)[:, 4 * q:4 * q + 4, :],
                                         v[:, 4 * q:4 * q + 4, :]).then_inc(raw[(n0 + h) % 2], 16)

            def mlp(layer, n0):
                for half in range(2):
                    m0 = n0 + 16 * half
                    with sp.Fori(0, 4) as i:
                        for h in range(2):
                            sp.wait_ge(s.w_lo, m0 + 2 * i + h - 1)
                            v = block_rows(mlp_w1[layer], 8 * half + 2 * i + h)
                            for q in range(2):
                                sp.dma_start(cols(wraw[:, (m0 + h) % 2, :], 256)[:, 4 * q:4 * q + 4, :],
                                             v[:, 4 * q:4 * q + 4, :]).then_inc(raw[(m0 + h) % 2], 16)
                    m0 += 8
                    with sp.Fori(0, 4) as i:
                        for h in range(2):
                            sp.wait_ge(s.w_lo, m0 + 2 * i + h - 1)
                            rows = mlp_w2[layer][half * 2048 + h * 1024:half * 2048 + (h + 1) * 1024, :]
                            v = block_rows(rows, i)
                            for q in range(2):
                                sp.dma_start(cols(wraw[:, (m0 + h) % 2, :], 256)[:, 4 * q:4 * q + 4, :],
                                             v[:, 4 * q:4 * q + 4, :]).then_inc(raw[(m0 + h) % 2], 16)
                    if half == 0:
                        sp.wait_ge(s.hid_rdy, 32 * layer + 16)
                        sp.dma_start(ptok[:, :, :], p[layer, 0].rearrange("(t p) d -> p t d", p=P)).then_inc(s.p_in, 16)

            def up(layer, n):
                slot_free(n)
                v = ple_w_up[layer].rearrange("(k p) n -> p k n", p=P)
                dst = cols(wraw[:, n % 2, :], 1024, 2)
                load(n, n % 2, [(dst[:, k:k + 1, :], v[:, k:k + 1, :]) for k in range(2)])

            square(rwkv_w_rkvo[0, 1], N_K)
            square(rwkv_w_rkvo[0, 0], N_R)
            square(rwkv_w_rkvo[0, 2], N_V)
            slot_free(N_G2)
            load(N_G2, 0, [(r0[:, 0:1024], rwkv_g2[0][0:128, :]), (r0[:, 1024:2048], rwkv_g2[0][32:160, :])])
            square(rwkv_w_rkvo[0, 3], N_WO)
            mlp(0, L_MLP[0])
            up(0, L_MLP[0] + 32)
            square(ple_w_gate[0], L_MLP[0] + 33)
            square(w_k_shared, N_KS)
            sp.wait_ge(s.bv_ev, 2)
            sp.dma_start(bias_rows, bvec[:, :]).then_inc(s.bvec_out, 16)
            sp.wait_ge(s.bvec_out, 16)
            for h in range(8):
                src = bass.AP(bias_rows.tensor, 640 * h, [[1, P], [1, S]])
                sp.dma_start(strip[:, h, :], src).then_inc(s.strip_in, 16)
            square(w_v_shared, N_VS)
            square(diff_w_q[0], N_Q)
            square(diff_w_o[0], N_DO)
            mlp(1, L_MLP[1])
            up(1, L_MLP[1] + 32)
            square(ple_w_gate[1], L_MLP[1] + 33)
            for c in range(CT // 2):
                sp.wait_ge(s.fin_ev, 2 * (c + 1))
                sp.dma_start(out[0].rearrange("(t p) d -> p t d", p=P)[:, :, 256 * c:256 * (c + 1)],
                             OT[:, :, 256 * c:256 * (c + 1)]).then_inc(s.out_st, 16)
            sp.wait_ge(s.out_st, 16 * (CT // 2))

        @block.gpsimd
        def _(pool):
            def low(n, par, rng, first):
                pool.wait_ge(s.w_hi, n + 1)
                if not first:
                    pool.wait_ge(s.pe_step, 8 * (n - 1))
                pool.tensor_tensor(wlo[:, par, rng], wraw[:, par, rng], whi[:, par, rng].bitcast(F32),
                                   ALU.subtract).then_inc(s.w_lo, 1)

            low(0, 0, slice(0, 1024), True)
            low(1, 1, slice(0, 1024), True)
            low(2, 0, slice(0, 2048), False)
            low(3, 1, slice(0, 1024), False)

            def lows(n0, n1):
                assert (n1 - n0) % 2 == 0
                with pool.Fori(0, (n1 - n0) // 2) as i:
                    for h in range(2):
                        low(n0 + 2 * i + h, (n0 + h) % 2, slice(0, 2048), False)

            lows(N_K, N_V + 4)
            low(N_G2, 0, slice(0, 2048), False)
            low(N_WO, 1, slice(0, 2048), False)

            link = Link(pool, s.pool_link)
            pool.wait_ge(s.pe_step, 8 * N_G2)
            pool.wait_ge(s.prep, CT)
            pool.wait_ge(s.dense_v, 8)
            for t in (Bbd, Kbd, Vbd, LabT, sets[0][3], sets[1][3], sets[0][7], sets[1][7]):
                pool.memset(t[:, :, :], 0.0).then_inc(s.bd_zero, 1)
            pool.wait_ge(s.bd_zero, 8)
            for q in range(NQ + 1):
                c, t0 = q // 2, (q % 2) * QUAD * CH
                if q < NQ:
                    Btok, Ktok, Vtok, LakT, LrbT, LrkT, TiT, Abd = sets[q % 2]
                    if q >= 1:
                        pool.wait_ge(s.tr_mm, 4 * q)
                    if q >= 2:
                        pool.wait_ge(s.y_mm, 4 * (q - 1))
                    if q == 0:
                        pool.wait_ge(s.dense_a, 36)
                    for i, (dst, kind) in enumerate(((Vbd, V_), (Abd, LW))):
                        for h in range(2):
                            if q or i or h:
                                pool.wait_ge(s.bd_p, 4 * q + 2 * i + h)
                            pool.tensor_copy(dst[64 * h:64 * h + 64, :, 64 * h:64 * h + 64],
                                             St[64 * h:64 * h + 64, kind, c, t0:t0 + QUAD * CH]
                                             .rearrange("p (u t) -> p u t", t=CH)).then_inc(s.bd_p, 1)
                    pool.wait_ge(s.bd_p, 4 * q + 4)
                    pool.wait_ge(s.sc_ev, 6 * q + 2)
                    link(pool.tensor_tensor(TiT[:, :, :], LabT[:, :, :],
                                            cst[:, None, C_LVT:C_LVT + P].to_broadcast([P, QUAD, P]), ALU.mult))
                    pool.tensor_tensor(TiT[:, :, :], TiT[:, :, :], ident[:, None, :].to_broadcast([P, QUAD, P]),
                                       ALU.add).then_inc(s.tt0, 1)
                    pool.wait_ge(s.tt0, q + 1)

            lows(N_WO + 1, L_MLP[0] + 31)
            low(L_MLP[0] + 31, 0, slice(0, 2048), False)
            low(L_MLP[0] + 32, 1, slice(0, 2048), False)
            lows(L_MLP[0] + 33, N_DO + 4)
            lows(L_MLP[1], L_MLP[1] + 32)
            low(L_MLP[1] + 32, 0, slice(0, 2048), False)
            lows(L_MLP[1] + 33, N_ALL)

        @block.tensor
        def _(pe):
            mm = pe.matmul

            def three(o, n, w, xs, first, last):
                (wh, wl), (ah, al) = w, xs
                mm(o, wh, ah, start=first, stop=False)
                mm(o, wh, al, start=False, stop=False)
                return mm(o, wl, ah, start=False, stop=last)

            def wslice(par, c0):
                return whi[:, par, c0:c0 + P], wlo[:, par, c0:c0 + P]

            def xs(k):
                return xh[:, k, :], xl[:, k, :]

            pe.wait_ge(s.cst_in, 16)
            pe.wait_ge(s.rows_in, 160)
            for c in range(CT):
                pe.transpose(pb[7][:, c * NV:(c + 1) * NV], vrows[:, c * P:(c + 1) * P], ident[0:NV, 0:NV])
            pe.wait_ge(s.hrows_in, 80)
            pe.transpose(pb[7][:, CT * NV:CT * NV + 3], hrows[:, :], ident[0:3, 0:3]).then_inc(s.par_tr, 1)
            pe.wait_ge(s.x_in, 64)
            for c in range(CT):
                if c == 7:
                    pe.wait_ge(s.xt_sq, 1)
                for t in range(TT):
                    ins = pe.transpose(pb[c % 7][:, t * P:(t + 1) * P], xtok[:, t, c * P:(c + 1) * P], ident)
                ins.then_inc(s.x_tr, 1)
            norms = [0]

            def norm_total(bank):
                norms[0] += 1
                pe.wait_ge(s.acc, 8 * norms[0])
                mm(pb[bank][:, :], ones, tmp[:, 3, :], start=True, stop=True).then_inc(s.norm_ps, 1)

            pe.wait_ge(s.xt_sq, 5)
            norm_total(4)

            def dense_block(n, par, pair, width=2, x_base=None, hook=None, rows=None):
                pe.wait_ge(s.w_lo, n + 1)
                for k in range(CT):
                    if x_base is not None:
                        pe.wait_ge(s.x_ready, x_base + k + 1)
                    if hook and k in hook:
                        hook[k]()
                    for m in range(width):
                        ins = three(pb[2 * pair + m][:, :], n, wslice(par, k * P * width + m * P), xs(k),
                                    k == 0, k == CT - 1)
                    ins.then_inc(s.pe_step, 1)

            pe.wait_ge(s.xt_cp, 8)
            pe.wait_ge(s.xt_sq, 8)
            pe.wait_ge(s.par_ev, 2)
            dense_block(0, 0, 0, 1, X_W)
            dense_block(1, 1, 1, 1, X_A)
            pe.wait_ge(s.dense_a, 1)
            dense_block(2, 0, 0, 2, X_G)
            pe.wait_ge(s.w_lo, 4)
            pe.wait_ge(s.lora_rdy, 1)
            for g in range(8):
                if g == 0:
                    pe.wait_ge(s.dense_a, 2)
                elif g == 1:
                    pe.wait_ge(s.dense_a, 4)
                else:
                    pe.wait_ge(s.dense_a, 4 + 2 * (g - 1))
                pair = 1 - g % 2
                r = slice(0, 64) if g < 4 else slice(64, 128)
                for m in range(2):
                    c = (2 * g + m) % 8
                    w = (whi[r, 1, c * P:(c + 1) * P], wlo[r, 1, c * P:(c + 1) * P])
                    ins = three(pb[2 * pair + m][:, :], 3, w, (lora_h[r, 0, :], lora_l[r, 0, :]), True, True)
                ins.then_inc(s.pe_step, 1)

            def kk_total(c):
                def f():
                    pe.wait_ge(s.kk_sq, c + 1)
                    if c >= 2:
                        pe.wait_ge(s.kk_rt, c - 1)
                    mm(pb[4 + c % 2][:, :], bones, tmp[:, c % 2, :], start=True, stop=True).then_inc(s.kk_ps, 1)
                return f

            for t in range(12):
                if t < 2:
                    pe.wait_ge(s.dense_a, 18 + 2 * t)
                elif t < 6:
                    pe.wait_ge(s.dense_a, 20 + 2 * (t - 1))
                elif t < 10:
                    pe.wait_ge(s.dense_v, 2 * (t - 5))
                else:
                    pe.wait_ge(s.dense_a, 28 + 2 * (t - 9))
                dense_block(N_K + t, t % 2, 1 - t % 2, 2, {0: X_K, 4: X_R, 8: X_V}.get(t),
                            {3: kk_total(t - 1)} if 1 <= t <= 8 else None)

            pe.wait_ge(s.dense_a, 36)
            pe.wait_ge(s.prep, CT)
            pe.wait_ge(s.dense_v, 8)
            pe.wait_ge(s.bd_zero, 8)

            for q in range(NQ + 1):
                c = q // 2
                inv = q < NQ
                chain = q >= 1
                if inv:
                    Btok, Ktok, Vtok, LakT, LrbT, LrkT, TiT, Abd = sets[q % 2]
                if chain:
                    o = q - 1
                    oc = o // 2
                    oB, oK, oV, oLak, oLrb, oLrk, oTiT, oA = sets[o % 2]

                def tok(j, qq):
                    return slice((qq % 2) * QUAD * CH + j * CH, (qq % 2) * QUAD * CH + (j + 1) * CH)

                def chain_z(j):
                    J = 4 * o + j
                    if J >= 1:
                        pe.wait_ge(s.h_ev, J)
                    new = J % 8 == 0
                    if j == 0:
                        pe.wait_ge(s.tr_ev, 3 * o + 3)
                        pe.wait_ge(s.sc_ev, 6 * o + 6)
                        pe.wait_ge(s.bd_p, 4 * o + 4)
                    ins = mm(pb[6][:, 0:P], oLak[:, j, :], oV[:, j, :], start=True, stop=new)
                    if not new:
                        ins = mm(pb[6][:, 0:P], oA[:, j, :], Hs[:, J % 2, :], start=False, stop=True)
                    ins.then_inc(s.ch, 1)

                def chain_u(j):
                    J = 4 * o + j
                    pe.wait_ge(s.z_ev, 2 * J + 1)
                    if j == 0:
                        pe.wait_ge(s.lv_te, 9 * o + 9)
                    mm(pb[6][:, 0:P], oTiT[:, j, :], Zs[:, :], start=True, stop=True).then_inc(s.ch, 1)

                def chain_h(j):
                    J = 4 * o + j
                    new = J % 8 == 0
                    pe.wait_ge(s.z_ev, 2 * J + 2)
                    mm(pb[6][:, 0:P], oK[:, j, :], oV[:, j, :], start=True, stop=False)
                    mm(pb[6][:, 0:P], oB[:, j, :], Us[:, :], start=False, stop=True).then_inc(s.ch, 1)
                    if j == 0 and o >= 1:
                        pe.wait_ge(s.y_ev, o)
                    y = pb[7][:, j * CH:(j + 1) * CH]
                    if not new:
                        mm(y, Hs[:, J % 2, :], St[:, R_, oc, tok(j, o)], start=True, stop=False)
                    mm(y, Us[:, :], oLrb[:, j, :], start=new, stop=False)
                    mm(y, oV[:, j, :], oLrk[:, j, :], start=False, stop=True).then_inc(s.y_mm, 1)

                def level_p(lv):
                    if lv == 1:
                        pe.wait_ge(s.t0, q + 1)
                    else:
                        pe.wait_ge(s.lv_te, 9 * q + 2 * (lv - 2) + 1)
                        pe.wait_ge(s.lv_pe, 5 * q + lv - 1)
                    for u in range(QUAD):
                        ins = mm(pb[3][:, u * P:(u + 1) * P], LabT[:, u, :], Ti[:, u, :], start=True, stop=True)
                    ins.then_inc(s.lv_p, 1)

                def level_t(lv):
                    pe.wait_ge(s.lv_pe, 5 * q + lv)
                    if lv == 1:
                        pe.wait_ge(s.tt0, q + 1)
                    else:
                        pe.wait_ge(s.lv_te, 9 * q + 2 * (lv - 1))
                    if lv < LEVELS - 1:
                        for u in range(QUAD):
                            ins = mm(pb[4][:, u * P:(u + 1) * P], TiT[:, u, :], Pm[:, u, :], start=True, stop=True)
                        ins.then_inc(s.lv_t, 1)
                    for u in range(QUAD):
                        ins = mm(pb[5][:, u * P:(u + 1) * P], Pm[:, u, :], TiT[:, u, :], start=True, stop=True)
                    ins.then_inc(s.lv_t, 1)

                def turn(src, nth):
                    for u in range(QUAD):
                        ins = pe.transpose(pb[2][:, u * P:(u + 1) * P], src[:, u, :], ident)
                    ins.then_inc(s.tr_mm, 1)

                if inv:
                    pe.wait_ge(s.bd_a, 4 * (q + 1))
                    if q >= 1:
                        pe.wait_ge(s.sc_ev, 6 * q)
                    for b, src in ((0, Bbd), (1, Kbd)):
                        for u in range(QUAD):
                            ins = mm(pb[b][:, u * P:(u + 1) * P], src[:, u, :], St[:, LW:R_ + 1, c, tok(u, q)],
                                     start=True, stop=True)
                        ins.then_inc(s.sc_mm, 1)
                    if q >= 1:
                        pe.wait_ge(s.tr_ev, 3 * q)
                    turn(Bbd, 0)
                if chain:
                    chain_z(0)
                if inv:
                    pe.wait_ge(s.tr_ev, 3 * q + 1)
                    pe.wait_ge(s.sc_ev, 6 * q + 2)
                    turn(LabT, 1)
                if chain:
                    chain_u(0)
                if inv:
                    pe.wait_ge(s.lab_ev, q + 1)
                    turn(Kbd, 2)
                    level_p(1)
                if chain:
                    chain_h(0)
                if inv:
                    level_t(1)
                for j in range(1, 4):
                    if chain:
                        chain_z(j)
                    if inv:
                        level_p(j + 1)
                    if chain:
                        chain_u(j)
                    if inv:
                        if j == 1:
                            pe.wait_ge(s.tr_ev, 3 * q + 2)
                            pe.wait_ge(s.bd_p, 4 * q + 2)
                            turn(Vbd, 3)
                        level_t(j + 1)
                    if chain:
                        chain_h(j)
                if inv:
                    level_p(5)
                    level_t(5)

            pe.wait_ge(s.y_ev, NQ)
            for c in range(CT):
                if c >= 1:
                    pe.wait_ge(s.yc_rdy, c)
                mm(pb[0][:, :], bones, X[:, c, 4:4 + S], start=True, stop=True).then_inc(s.mu_mm, 1)
                if c >= 1:
                    pe.wait_ge(s.y_fin, c)
                pe.wait_ge(s.pr_rdy, c + 1)
                mm(pb[2][:, :], bones, tmp[:, 2, :], start=True, stop=True).then_inc(s.bon_ps, 1)
                if c == 0:
                    pe.wait_ge(s.w_lo, N_G2 + 1)
                    pe.wait_ge(s.lora_rdy, 3)
                w = (whi[:, 0, c * P:(c + 1) * P], wlo[:, 0, c * P:(c + 1) * P])
                three(pb[3][:, :], N_G2, w, (lora_h[:, 1, :], lora_l[:, 1, :]), True, False)
                w = (whi[96:128, 0, 1024 + c * P:1024 + (c + 1) * P], wlo[96:128, 0, 1024 + c * P:1024 + (c + 1) * P])
                three(pb[3][:, :], N_G2, w, (lora_h[96:128, 2, :], lora_l[96:128, 2, :]), False, True).then_inc(s.pe_step, 1)
                pe.wait_ge(s.gn_sq, c + 1)
                if c >= 1:
                    pe.wait_ge(s.gn_rt, c)
                mm(pb[1][:, :], bones, tmp[:, 1, :], start=True, stop=True).then_inc(s.gn_ps, 1)

            def proj(n0, x_base, ev0):
                for b in range(4):
                    if b >= 2:
                        pe.wait_ge(s.dense_v, ev0 + 2 * (b - 1))
                    dense_block(n0 + b, (n0 + b) % 2, b % 2, 2, x_base if b == 0 else None)

            pe.wait_ge(s.x2_in, 64)
            pe.wait_ge(s.y_fin, 8)
            for c in range(CT):
                if c >= 4:
                    pe.wait_ge(s.x2_cp, c - 3)
                for t in range(TT):
                    ins = pe.transpose(pb[4 + c % 4][:, t * P:(t + 1) * P], xtok2[:, t, c * P:(c + 1) * P], ident)
                ins.then_inc(s.x2_tr, 1)
            proj(N_WO, X_Y, 8)

            def mlp(layer, n0, x_base, ev0):
                for half in range(2):
                    e = ev0 + 24 * half
                    m0 = n0 + 16 * half
                    pe.wait_ge(s.dense_v, e)
                    if half == 0:
                        norm_total(4)
                    with pe.Fori(0, 4) as i:
                        for h in range(2):
                            pe.wait_ge(s.dense_v, e + 2 * (2 * i + h) - 2)
                            dense_block(m0 + 2 * i + h, (m0 + h) % 2, h, 2, x_base if h == 0 else None)
                    m0 += 8
                    e += 16
                    if half == 1:
                        pe.wait_ge(s.p_in, 16 * (layer + 1))
                        for k in range(2):
                            for t in range(TT):
                                ins = pe.transpose(pb[5 + k][:, t * P:(t + 1) * P], ptok[:, t, k * P:(k + 1) * P], ident)
                            ins.then_inc(s.p_tr, 1)
                    pe.wait_ge(s.dense_v, e)
                    with pe.Fori(0, 2) as i:
                        for g in range(2):
                            pe.wait_ge(s.dense_v, e + 2 * (2 * i + g) - 2)
                            for kb in range(2):
                                n = m0 + 4 * i + 2 * g + kb
                                par = (m0 + kb) % 2
                                pe.wait_ge(s.w_lo, n + 1)
                                for k in range(CT):
                                    if g == 0:
                                        pe.wait_ge(s.hid_rdy, 32 * layer + 16 * half + 8 * kb + k + 1)
                                    a = (hid_h[:, 8 * kb + k, :], hid_l[:, 8 * kb + k, :])
                                    for m in range(2):
                                        ins = three(pb[2 * g + m][:, :], n, wslice(par, k * 256 + m * P), a,
                                                    kb == 0 and k == 0, kb == 1 and k == CT - 1)
                                    ins.then_inc(s.pe_step, 1)

            def ple(layer, n, x_base, ev_a, ev0):
                pe.wait_ge(s.w_lo, n + 1)
                pe.wait_ge(s.p_rdy, 2 * (layer + 1))
                pe.wait_ge(s.dense_v, ev0)
                for m in range(CT):
                    if m >= 4:
                        pe.wait_ge(s.dense_a, ev_a + m - 3)
                    for k in range(2):
                        ins = three(pb[m % 4][:, :], n, wslice(n % 2, k * 1024 + m * P), (lora_h[:, k, :], lora_l[:, k, :]),
                                    k == 0, k == 1)
                    ins.then_inc(s.pe_step, 1)
                norm_total(4)
                for b in range(4):
                    if b < 2:
                        pe.wait_ge(s.dense_a, ev_a + 6 + 2 * b)
                    else:
                        pe.wait_ge(s.dense_v, ev0 + 2 * (b - 1))
                    dense_block(n + 1 + b, (n + 1 + b) % 2, b % 2, 2, x_base if b == 0 else None)

            mlp(0, L_MLP[0], X_M0, 16)
            ple(0, L_MLP[0] + 32, X_P0, 36, 64)

            norm_total(4)
            pe.wait_ge(s.far_row, 1)
            pe.wait_ge(s.hot_in, 16)
            pe.wait_ge(s.rel_in, 16)
            mm(pb[5][0:8, 0:S], relb[0:BUCKETS + 1, :], hot[0:BUCKETS + 1, 0:S], start=True, stop=True)
            mm(pb[6][0:8, 0:128], relb[0:BUCKETS + 1, :], hot[0:BUCKETS + 1, S:640], start=True, stop=True).then_inc(s.bv_mm, 1)

            def qk_total(i0):
                def f():
                    for i in (i0, i0 + 1):
                        pe.wait_ge(s.qk_sq, i + 1)
                        if i == 0:
                            pe.wait_ge(s.bv_ev, 2)
                        if i >= 2:
                            pe.wait_ge(s.qk_rt, i - 1)
                        mm(pb[4 + i % 2][:, :], bones, tmp[:, i % 2, :], start=True, stop=True).then_inc(s.qk_ps, 1)
                return f

            def v_turn(i0):
                def f():
                    for i in (i0, i0 + 1):
                        pe.wait_ge(s.dense_v, 80 + i + 1)
                        if i >= 2:
                            pe.wait_ge(s.v_ev, i - 1)
                        for t in range(TT):
                            ins = pe.transpose(pb[6 + i % 2][:, t * P:(t + 1) * P], tmp[:, 2 + i % 2, t * P:(t + 1) * P], ident)
                        ins.then_inc(s.v_tr, 1)
                return f

            for b in range(4):
                pe.wait_ge(s.dense_v, 72 + max(2 * (b - 1), 0))
                dense_block(N_KS + b, b % 2, b % 2, 2, X_KV if b == 0 else None, {5: qk_total(2 * b - 2)} if b else None)
            for b in range(4):
                pe.wait_ge(s.dense_v, 80 + 2 * (b - 1))
                dense_block(N_VS + b, b % 2, b % 2, 2, None, {5: v_turn(2 * b - 2)} if b else {5: qk_total(6)})
            for b in range(4):
                pe.wait_ge(s.dense_v, 88 + 2 * (b - 1))
                dense_block(N_Q + b, b % 2, b % 2, 2, X_Q if b == 0 else None, {5: qk_total(8 + 2 * b - 2)} if b else {5: v_turn(6)})
            pe.wait_ge(s.dense_v, 96)
            qk_total(14)()

            def scores(i):
                h, b = i // 4, i % 4
                w = (b + 1) * P
                if b == 0:
                    pe.wait_ge(s.qk_n, 8 + h + 1)
                if i >= 2:
                    pe.wait_ge(s.lg, 2 * (i - 1))
                for cmp in range(2):
                    r = slice(64 * cmp, 64 * cmp + 64)
                    mm(pb[2 * (i % 2) + cmp][:, 0:w], QT[r, h, b * P:(b + 1) * P], KT[r, h, 0:w],
                       start=True, stop=True).then_inc(s.s_mm, 1)

            def head_total(h):
                pe.wait_ge(s.o_sq, h + 1)
                mm(pb[7][:, :], ones, tmp[:, 0, :], start=True, stop=True).then_inc(s.o_ps, 1)

            pe.wait_ge(s.v_ev, 8)
            pe.wait_ge(s.dense_v, 96)
            pe.wait_ge(s.qk_rt, 16)
            scores(0)
            for i in range(32):
                h, b = i // 4, i % 4
                if i + 1 < 32:
                    scores(i + 1)
                pe.wait_ge(s.at_rdy, i + 1)
                if i >= 1:
                    pe.wait_ge(s.at_ev, i)
                for j in range(b + 1):
                    ins = pe.transpose(pb[4][:, j * P:(j + 1) * P], At[:, i % 2, j * P:(j + 1) * P], ident)
                ins.then_inc(s.at_tr, 1)
                if b == 0 and h >= 2:
                    pe.wait_ge(s.o_f, h - 1)
                if b == 1 and h >= 1:
                    head_total(h - 1)
                pe.wait_ge(s.at_ev, i + 1)
                for j in range(b + 1):
                    ins = mm(pb[5 + h % 2][:, b * P:(b + 1) * P], VT[:, h, j, :], ATt[:, i % 2, j * P:(j + 1) * P],
                             start=(j == 0), stop=(j == b))
                ins.then_inc(s.o_mm, 1)
            head_total(7)
            pe.wait_ge(s.o_f, 8)
            proj(N_DO, X_O, 96)
            mlp(1, L_MLP[1], X_M1, 104)
            ple(1, L_MLP[1] + 32, X_P1, 44, 152)
            for c in range(CT):
                pe.wait_ge(s.upd, 8 + c + 1)
                if c >= 4:
                    pe.wait_ge(s.fin_ev, c - 3)
                for t in range(TT):
                    ins = pe.transpose(pb[4 + c % 4][:, t * P:(t + 1) * P], X[:, c, t * P:(t + 1) * P], ident)
                ins.then_inc(s.fin_tr, 1)

        @block.scalar
        def _(act):
            A = act.activation
            raw = (s.raw0, s.raw1)
            act.dma_start(cst[:, :], consts[:, 0:C_END]).then_inc(s.cst_in, 16)

            def row(a):
                return a.rearrange("(o n) -> o n", o=1)

            for dst, src in ((vrows[0:6, :], norm_g.rearrange("a b n -> (a b) n")), (vrows[6:7, :], row(kv_norm_g)),
                             (vrows[7:13, :], rwkv_mix[0]), (vrows[13:14, :], rwkv_w0), (vrows[14:15, :], rwkv_a0),
                             (vrows[15:16, :], rwkv_k_k), (vrows[16:17, :], rwkv_k_a), (vrows[17:18, :], rwkv_ln_w),
                             (vrows[18:19, :], rwkv_ln_b), (vrows[19:20, :], rwkv_r_k.rearrange("o h n -> o (h n)"))):
                act.dma_start(dst, src).then_inc(s.rows_in, 16)
            for i, src in ((0, row(k_norm_g)), (1, diff_q_norm_g)):
                for h in range(2):
                    act.dma_start(hrows[i:i + 1, h * HD:(h + 1) * HD], src).then_inc(s.hrows_in, 16)
            act.dma_start(hrows[2:3, :], diff_subln_g).then_inc(s.hrows_in, 16)
            act.dma_start(lrow[:, :, :], bass.AP(diff_lam.tensor, diff_lam.offset, [[0, P], [HD, 4], [1, HD]]))\
               .then_inc(s.lam_in, 16)

            def high(n, par, rng=slice(0, 2048), first=False):
                act.wait_ge(raw[par], 16 * (n - par) + 32)
                if not first:
                    act.wait_ge(s.pe_step, 8 * (n - 1))
                A(whi[:, par, rng], wraw[:, par, rng], ACT.Copy).then_inc(s.w_hi, 1)

            def split_high(k, src, gain, free):
                if free is not None:
                    act.wait_ge(s.pe_step, free + k + 1)
                if gain is None:
                    A(xh[:, k, :], src, ACT.Copy).then_inc(s.x_hi, 1)
                else:
                    A(xh[:, k, :], src, ACT.Copy, scale=gain).then_inc(s.x_hi, 1)

            def norm_root(i):
                act.wait_ge(s.norm_ps, i)
                A(rstd[:, :], pb[4][:, :], ACT.Sqrt, bias=eps_n, scale=1.0 / D).then_inc(s.norm_rt, 1)

            for c in range(CT):
                act.wait_ge(s.x_tr, c + 1)
                A(X[:, c, 4:4 + S], pb[c % 7][:, :], ACT.Copy).then_inc(s.xt_cp, 1)
                if c >= 2:
                    act.wait_ge(s.acc, c - 1)
                A(tmp[:, c % 2, :], pb[c % 7][:, :], ACT.Square).then_inc(s.xt_sq, 1)
            high(0, 0, slice(0, 1024), True)
            high(1, 1, slice(0, 1024), True)
            act.wait_ge(s.small_set, 1)
            norm_root(1)
            act.wait_ge(s.lam_s, 1)
            A(lamw[:, 2:4], lamw[:, 0:2], ACT.Exp).then_inc(s.lam_e, 1)

            def mixes(i, mix, free):
                def product(k):
                    if i == 0:
                        act.wait_ge(s.h_ready, k + 1)
                    if 8 * i + k >= 2:
                        act.wait_ge(s.mix_b, 8 * i + k - 1)
                    A(pb[6 + k % 2][:, :], X[:, k, 3:3 + S], ACT.Copy, scale=vec(k, V_MIX + mix)).then_inc(s.mix_a, 1)
                product(0)
                for k in range(CT):
                    if k + 1 < CT:
                        product(k + 1)
                    act.wait_ge(s.mix_b, 8 * i + k + 1)
                    split_high(k, tmp[:, 2 + k % 2, :], None, free)

            mixes(0, MIX_W, None)
            mixes(1, MIX_A, 0)
            act.wait_ge(s.norm_rt, 1)
            act.wait_ge(s.h_ready, 8)
            A(rstd[0:64, :], pb[0][0:64, :], ACT.Tanh).then_inc(s.dense_a, 1)
            high(2, 0)
            mixes(2, MIX_G, 8 * 1)
            act.wait_ge(s.pe_step, 16)
            A(rstd[64:128, :], pb[2][64:128, :], ACT.Copy).then_inc(s.dense_a, 1)
            high(3, 1, slice(0, 1024))
            act.wait_ge(s.dense_a, 2)
            A(lora_h[:, 0, :], rstd[:, :], ACT.Copy).then_inc(s.lora_hi, 1)
            mixes(3, MIX_K, 8 * 2)
            high(4, 0)
            for m in range(2):
                act.wait_ge(s.lora_rdy, 1 + m)
                A(rstd[:, :], pb[m][:, :], ACT.Sigmoid).then_inc(s.dense_a, 1)
                act.wait_ge(s.dense_a, 3 + m)
                A(lora_h[:, 1 + m, :], rstd[:, :], ACT.Copy).then_inc(s.lora_hi, 1)
            for g in range(8):
                act.wait_ge(s.pe_step, 24 + g + 1)
                for m in range(2):
                    c = (2 * g + m) % 8
                    kind, bias = (LW, V_W0) if g < 4 else (A_, V_A0)
                    A(St[:, kind, c, :], pb[2 * (1 - g % 2) + m][:, :], ACT.Sigmoid, bias=vec(c, bias))\
                        .then_inc(s.dense_a, 1)
            high(5, 1)

            def prep_act(c):
                if c >= 2:
                    act.wait_ge(s.prep, c - 1)
                act.wait_ge(s.dense_a, 20 + c + 1)
                A(tmp[:, c % 2, :], St[:, K_, c, :], ACT.Square, scale=vec(c, V_KK)).then_inc(s.kk_sq, 1)
                act.wait_ge(s.g_cum, 2 * c + 2)
                A(prep_b[:, :], rstd[:, :], ACT.Exp, scale=KAPPA).then_inc(s.exps, 1)
                A(St[:, LW, c, :], prep_a[:, :], ACT.Exp, scale=-KAPPA).then_inc(s.exps, 1)
                A(St[:, R_, c, :], rstd[:, :], ACT.Exp, scale=-KAPPA).then_inc(s.exps, 1)
                A(gC[:, c * 8:(c + 1) * 8], rstd[:, CH - 1:S:CH], ACT.Exp, scale=-KAPPA).then_inc(s.exps, 1)
                act.wait_ge(s.kk_ps, c + 1)
                A(tmp[:, c % 2, :], pb[4 + c % 2][:, :], ACT.Sqrt, bias=eps_0).then_inc(s.kk_rt, 1)

            for t in range(12):
                n = N_K + t
                if t == 3:
                    mixes(4, MIX_R, 8 * (N_K + 3))
                if t == 7:
                    mixes(5, MIX_V, 8 * (N_R + 3))
                if t < 4 or t >= 8:
                    kind, c = (K_, 2 * t) if t < 4 else (V_, 2 * (t - 8))
                    act.wait_ge(s.pe_step, 8 * (n + 1))
                    for m in range(2):
                        A(St[:, kind, c + m, :], pb[2 * (1 - t % 2) + m][:, :], ACT.Copy).then_inc(s.dense_a, 1)
                if n + 2 <= N_WO:
                    high(n + 2, t % 2)
                if t < 8:
                    prep_act(t)

            act.wait_ge(s.pe_step, 8 * N_G2)
            act.wait_ge(s.prep, CT)
            act.wait_ge(s.bd_zero, 8)
            act.wait_ge(s.dense_v, 8)

            def diag_copies(q):
                if q >= 1:
                    act.wait_ge(s.tr_mm, 4 * (q - 1) + 3)
                for dst, kind in ((Bbd, A_), (Kbd, K_)):
                    for h in range(2):
                        A(dst[64 * h:64 * h + 64, :, 64 * h:64 * h + 64],
                          St[64 * h:64 * h + 64, kind, q // 2, (q % 2) * QUAD * CH:(q % 2 + 1) * QUAD * CH]
                          .rearrange("p (u t) -> p u t", t=CH), ACT.Copy).then_inc(s.bd_a, 1)

            def flat(t):
                return t[:, :, :].rearrange("p u t -> p (u t)")

            diag_copies(0)
            for q in range(NQ + 1):
                inv, chain = q < NQ, q >= 1
                o = q - 1

                def turned(i):
                    act.wait_ge(s.tr_mm, 4 * q + (1, 3, 4)[i])
                    if q >= 2:
                        act.wait_ge(s.y_mm, 4 * (q - 1))
                    A(flat(sets[q % 2][i]), pb[2][:, :], ACT.Copy).then_inc(s.tr_ev, 1)

                def chunk(j):
                    J = 4 * o + j
                    if J % 8:
                        act.wait_ge(s.h_ev, J)
                        A(Hg[:, :], Hs[:, J % 2, :], ACT.Copy, scale=gC[:, (o // 2) * 8 + J % 8:(o // 2) * 8 + J % 8 + 1])\
                            .then_inc(s.hg, 1)
                    act.wait_ge(s.ch, 3 * J + 1)
                    A(Zs[:, :], pb[6][:, 0:P], ACT.Copy).then_inc(s.z_ev, 1)
                    act.wait_ge(s.ch, 3 * J + 2)
                    if J >= 1:
                        act.wait_ge(s.y_mm, J)
                    A(Us[:, :], pb[6][:, 0:P], ACT.Copy).then_inc(s.z_ev, 1)

                if inv:
                    turned(0)
                if chain:
                    chunk(0)
                if inv:
                    turned(1)
                if chain:
                    chunk(1)
                if inv:
                    turned(2)
                if chain:
                    chunk(2)
                if q + 1 < NQ:
                    diag_copies(q + 1)
                if chain:
                    chunk(3)
                    act.wait_ge(s.y_mm, 4 * (o + 1))
                    t0 = 4 + (o % 2) * QUAD * CH
                    A(X[:, o // 2, t0:t0 + QUAD * CH], pb[7][:, 0:QUAD * CH], ACT.Copy).then_inc(s.y_ev, 1)

            for t in range(TT):
                act.dma_start(xtok2[:, t, :], x[0, t * P:(t + 1) * P, :]).then_inc(s.x2_in, 16)
            for c in range(CT):
                act.wait_ge(s.yc_rdy, c + 1)
                A(tmp[:, 1, :], tmp[:, 0, :], ACT.Square).then_inc(s.gn_sq, 1)
                act.wait_ge(s.gn_ps, c + 1)
                A(tmp[:, 1, :], pb[1][:, :], ACT.Sqrt, bias=eps_g, scale=1.0 / HD).then_inc(s.gn_rt, 1)
                act.wait_ge(s.y_fin, c + 1)
                split_high(c, tmp[:, 3, :], None, None)
            for c in range(CT):
                act.wait_ge(s.x2_tr, c + 1)
                A(X[:, c, 0:S], pb[4 + c % 4][:, :], ACT.Copy).then_inc(s.x2_cp, 1)

            squares = [0]

            def square(c, slot, src_sem, src_count):
                i = squares[0]
                squares[0] += 1
                act.wait_ge(src_sem, src_count)
                act.wait_ge(s.acc, 8 + i - 1)
                A(tmp[:, slot, :], X[:, c, 0:S], ACT.Square).then_inc(s.sq_rdy, 1)

            def proj(n0, ev0):
                for b in range(4):
                    high(n0 + b + 1, (n0 + b + 1) % 2)
                    for m in range(2):
                        square(2 * b + m, m, s.dense_v, ev0 + 2 * b + m + 1)

            def splits(gain, free):
                for k in range(CT):
                    split_high(k, X[:, k, 0:S], vec(k, gain), free)

            def mlp(layer, n0, ev0):
                for half in range(2):
                    m0 = n0 + 16 * half
                    h0 = 32 * layer + 16 * half
                    with act.Fori(0, 4) as i:
                        for h in range(2):
                            high(m0 + 2 * i + h + 1, (m0 + h + 1) % 2)
                            for m in range(2):
                                act.wait_ge(s.hid_f, h0 + 4 * i + 2 * h + m + 1)
                                A(hid_h[:, bass.ds(4 * i + 2 * h + m, 1), :], tmp[:, 2 + m:3 + m, :], ACT.Copy)\
                                    .then_inc(s.hid_hi, 1)
                    m0 += 8
                    if half == 1:
                        for k in range(2):
                            act.wait_ge(s.p_tr, 2 * layer + k + 1)
                            A(lora_h[:, k, :], pb[5 + k][:, :], ACT.Copy).then_inc(s.p_hi, 1)
                    if half == 0:
                        with act.Fori(0, 4) as i:
                            for h in range(2):
                                high(m0 + 2 * i + h + 1, (m0 + h + 1) % 2)
                    else:
                        for b in range(8):
                            high(m0 + b + 1, (m0 + b + 1) % 2)
                            if b % 2:
                                for m in range(2):
                                    square(b - 1 + m, m, s.dense_v, ev0 + 40 + b + m)

            def ple(layer, n, gain, free, ni):
                splits(gain, free)
                high(n + 1, (n + 1) % 2)
                for m in range(CT):
                    act.wait_ge(s.pe_step, 8 * n + m + 1)
                    A(UP[:, m, :], pb[m % 4][:, :], ACT.Copy).then_inc(s.dense_a, 1)
                norm_root(ni)
                for b in range(4):
                    if n + 2 + b < N_ALL:
                        high(n + 2 + b, (n + b) % 2)
                    for m in range(2):
                        c = 2 * b + m
                        act.wait_ge(s.dense_v, 64 + 88 * layer + c + 1)
                        A(tmp[:, m, :], tmp[:, m, :], ACT.Sigmoid).then_inc(s.sig, 1)
                    if layer == 0:
                        for m in range(2):
                            square(2 * b + m, 2, s.upd, 2 * b + m + 1)

            proj(N_WO, 8)
            splits(V_N01, 8 * 20)
            norm_root(2)
            mlp(0, L_MLP[0], 16)
            ple(0, L_MLP[0] + 32, V_N02, 8 * (L_MLP[0] + 23), 3)

            act.wait_ge(s.upd, 8)
            act.dma_start(hot[:, :], consts[:, C_HOT:C_HOT + 640]).then_inc(s.hot_in, 16)
            act.dma_start(relb[0:BUCKETS, :], rel_bias).then_inc(s.rel_in, 16)

            splits(V_KV, 8 * 57)
            norm_root(4)

            def head_square(i):
                dst = KT if i < 8 else QT
                act.wait_ge(s.dense_v, 72 + i + 1 if i < 8 else 88 + i - 8 + 1)
                if i >= 2:
                    act.wait_ge(s.qk_n, i - 1)
                A(tmp[:, i % 2, :], dst[:, i % 8, :], ACT.Square).then_inc(s.qk_sq, 1)

            def head_root(i):
                act.wait_ge(s.qk_ps, i + 1)
                A(tmp[:, i % 2, :], pb[4 + i % 2][:, :], ACT.Sqrt, bias=eps_n, scale=1.0 / HD).then_inc(s.qk_rt, 1)

            def v_copy(i):
                act.wait_ge(s.v_tr, i + 1)
                A(VT[:, i, :, :].rearrange("p t v -> p (t v)"), pb[6 + i % 2][:, :], ACT.Copy).then_inc(s.v_ev, 1)

            for b in range(4):
                high(N_KS + b + 1, (b + 1) % 2)
                if b:
                    head_root(2 * b - 2)
                    head_root(2 * b - 1)
                head_square(2 * b)
                head_square(2 * b + 1)
            for b in range(4):
                high(N_VS + b + 1, (b + 1) % 2)
                if b:
                    v_copy(2 * b - 2)
                    v_copy(2 * b - 1)
                else:
                    head_root(6)
                    head_root(7)
            splits(V_N10, 8 * (N_VS + 3))
            for b in range(4):
                high(N_Q + b + 1, (b + 1) % 2)
                if b:
                    head_root(8 + 2 * b - 2)
                    head_root(8 + 2 * b - 1)
                else:
                    v_copy(6)
                    v_copy(7)
                head_square(8 + 2 * b)
                head_square(8 + 2 * b + 1)
            head_root(14)
            head_root(15)

            def exps(i):
                w = (i % 4 + 1) * P
                act.wait_ge(s.nm, i + 1)
                if i >= 2:
                    act.wait_ge(s.at_rdy, i - 1)
                for m in range(2):
                    k = 2 * (i % 2) + m
                    A(Pr[i % 2][:, m, 0:w], Lg[:, m, 0:w], ACT.Exp, bias=st_n[:, k:k + 1],
                      accum_out=st_l[:, k:k + 1]).then_inc(s.pexp, 1)

            def head_high(h):
                act.wait_ge(s.o_f, h + 1)
                if h == 0:
                    act.wait_ge(s.pe_step, 8 * N_DO)
                split_high(h, tmp[:, 2, :], None, None)

            def head_sq(h):
                act.wait_ge(s.o_mm, 4 * h + 4)
                if h >= 1:
                    act.wait_ge(s.o_f, h)
                else:
                    act.wait_ge(s.qk_n, 16)
                A(tmp[:, 0, :], pb[5 + h % 2][:, :], ACT.Square).then_inc(s.o_sq, 1)

            def head_rt(h):
                act.wait_ge(s.o_ps, h + 1)
                A(tmp[:, 1, :], pb[7][:, :], ACT.Sqrt, bias=eps_n, scale=1.0 / P).then_inc(s.o_rt, 1)

            exps(0)
            for i in range(32):
                h, b = i // 4, i % 4
                if i + 1 < 32:
                    exps(i + 1)
                act.wait_ge(s.at_tr, i + 1)
                if i >= 2:
                    act.wait_ge(s.o_mm, i - 1)
                A(ATt[:, i % 2, 0:(b + 1) * P], pb[4][:, 0:(b + 1) * P], ACT.Copy).then_inc(s.at_ev, 1)
                if h >= 1:
                    if b == 0:
                        head_sq(h - 1)
                    elif b == 1:
                        head_rt(h - 1)
                    elif b == 2:
                        head_high(h - 1)
            head_sq(7)
            head_rt(7)
            head_high(7)
            proj(N_DO, 96)
            splits(V_N11, 8 * 73)
            norm_root(5)
            mlp(1, L_MLP[1], 104)
            ple(1, L_MLP[1] + 32, V_N12, 8 * (L_MLP[1] + 23), 6)
            for c in range(CT):
                act.wait_ge(s.fin_tr, c + 1)
                A(OT[:, :, c * P:(c + 1) * P], pb[4 + c % 4][:, :].rearrange("p (t d) -> p t d", d=P), ACT.Copy)\
                    .then_inc(s.fin_ev, 1)

        @block.vector
        def _(dve):
            link = Link(dve, s.vec_link)
            tt, stt, ts = dve.tensor_tensor, dve.scalar_tensor_tensor, dve.tensor_scalar

            dve.memset(eps_n, NORM_EPS).then_inc(s.vec_link, 1)
            dve.memset(eps_g, GN_EPS).then_inc(s.vec_link, 1)
            link.n = 2
            dve.wait_ge(s.vec_link, 2)
            dve.memset(eps_0, 0.0).then_inc(s.small_set, 1)
            link(dve.memset(X[:, :, 0:4], 0.0))
            dve.wait_ge(s.par_tr, 1)
            dve.tensor_copy(PV[:, :, :], pb[7][:, 0:CT * NV].rearrange("p (c v) -> p c v", v=NV)).then_inc(s.par_ev, 1)
            dve.tensor_copy(hv[:, 0:3], pb[7][:, CT * NV:CT * NV + 3]).then_inc(s.par_ev, 1)
            dve.wait_ge(s.par_ev, 2)
            link(ts(nlnw, PV[:, :, V_LNW], -1.0, None, ALU.mult))
            link(ts(omka, PV[:, :, V_KA], -1.0, 1.0, ALU.mult, ALU.add))
            link(ts(omix3, PV[:, :, V_MIX:V_MIX + 6], -1.0, 1.0, ALU.mult, ALU.add))
            link(ts(qg8, hv[:, 1:2], HD ** -0.5, None, ALU.mult))
            link(ts(subg, hv[:, 2:3], 1.0 - LAMBDA_INIT, None, ALU.mult))

            link(dve.memset(tmp[:, 3, :], 0.0))
            for c in range(CT):
                dve.wait_ge(s.xt_sq, c + 1)
                if c:
                    dve.wait_ge(s.acc, c)
                tt(tmp[:, 3, :], tmp[:, 3, :], tmp[:, c % 2, :], ALU.add).then_inc(s.acc, 1)
            dve.wait_ge(s.lam_in, 16)
            link(tt(lrow[:, 0:2, :], lrow[:, 0:4:2, :], lrow[:, 1:4:2, :], ALU.mult))
            dve.tensor_reduce(lamw[:, 0:2], lrow[:, 0:2, :], AX.X, ALU.add).then_inc(s.lam_s, 1)

            def norm_finish(i):
                dve.wait_ge(s.norm_rt, i)
                link(dve.reciprocal(rstd[:, :], rstd[:, :]))

            norm_finish(1)
            for c in range(CT):
                dve.wait_ge(s.xt_cp, c + 1)
                stt(X[:, c, 4:4 + S], X[:, c, 4:4 + S], vec(c, V_N00), rstd[:, :], ALU.mult, ALU.mult)\
                    .then_inc(s.h_ready, 1)
            dve.wait_ge(s.h_ready, 8)
            dve.wait_ge(s.lam_e, 1)
            link(tt(lamf, lamw[:, 2:3], lamw[:, 3:4], ALU.subtract))
            link(ts(lamf, lamf, LAMBDA_INIT, None, ALU.add))

            def low(k, src, n):
                dve.wait_ge(s.x_hi, n + 1)
                tt(xl[:, k, :], src, xh[:, k, :].bitcast(F32), ALU.subtract).then_inc(s.x_ready, 1)

            def mixes(i, mix, free):
                def mixed(k):
                    dve.wait_ge(s.mix_a, 8 * i + k + 1)
                    if 8 * i + k >= 2:
                        dve.wait_ge(s.x_ready, 8 * i + k - 1)
                    stt(tmp[:, 2 + k % 2, :], X[:, k, 4:4 + S], omix3[:, k, mix:mix + 1], pb[6 + k % 2][:, :],
                        ALU.mult, ALU.add).then_inc(s.mix_b, 1)
                if i == 0:
                    dve.wait_ge(s.norm_ps, 1)
                mixed(0)
                for k in range(CT):
                    if k + 1 < CT:
                        mixed(k + 1)
                    dve.wait_ge(s.mix_b, 8 * i + k + 1)
                    low(k, tmp[:, 2 + k % 2, :], 8 * i + k)

            def lora_low(k):
                dve.wait_ge(s.lora_hi, k + 1)
                tt(lora_l[:, k, :], rstd[:, :], lora_h[:, k, :].bitcast(F32), ALU.subtract).then_inc(s.lora_rdy, 1)

            mixes(0, MIX_W, None)
            mixes(1, MIX_A, None)
            mixes(2, MIX_G, None)
            lora_low(0)
            mixes(3, MIX_K, None)
            lora_low(1)
            lora_low(2)

            def prep(c):
                lw, r, k, a = (St[:, kind, c, :] for kind in (LW, R_, K_, A_))
                dve.wait_ge(s.dense_a, 20)
                if c == 0:
                    dve.wait_ge(s.lora_rdy, 3)
                if c:
                    dve.wait_ge(s.prep, c)
                    dve.wait_ge(s.exps, 4 * c)
                dve.tensor_tensor_scan(rstd[:, :], cst[:, C_SEG:C_SEG + S], lw, 0.0, ALU.mult, ALU.add).then_inc(s.g_cum, 1)
                dve.wait_ge(s.g_cum, 2 * c + 1)
                tt(prep_a[:, :], rstd[:, :], lw, ALU.subtract).then_inc(s.g_cum, 1)
                kn = tmp[:, c % 2, :]
                dve.wait_ge(s.kk_rt, c + 1)
                link(ts(kn, kn, 1e-12, None, ALU.max))
                link(dve.reciprocal(kn, kn))
                link(stt(kn, k, vec(c, V_KK), kn, ALU.mult, ALU.mult))
                dve.wait_ge(s.exps, 4 * c + 4)
                link(stt(lw, kn, -1.0, lw, ALU.mult, ALU.mult))
                link(ts(prep_a[:, :], a, vec(c, V_KA), omka[:, c:c + 1], ALU.mult, ALU.add))
                link.mark(tt(k, k, prep_a[:, :], ALU.mult))
                link(tt(a, a, kn, ALU.mult))
                link.mark(tt(a, a, prep_b[:, :], ALU.mult))
                tt(k, k, prep_b[:, :], ALU.mult).then_inc(s.prep, 1)

            def r_tiles(b):
                dve.wait_ge(s.pe_step, 8 * (N_R + b + 1))
                for m in range(2):
                    c = 2 * b + m
                    dve.wait_ge(s.exps, 4 * c + 3)
                    tt(St[:, R_, c, :], St[:, R_, c, :], pb[2 * (1 - b % 2) + m][:, :], ALU.mult).then_inc(s.dense_v, 1)

            for t in range(12):
                if t == 3:
                    mixes(4, MIX_R, None)
                if t == 7:
                    mixes(5, MIX_V, None)
                if t < 8:
                    prep(t)
                if 4 <= t < 7:
                    r_tiles(t - 4)
                if t == 8:
                    r_tiles(3)
            dve.wait_ge(s.prep, 8)
            dve.wait_ge(s.vec_link, link.n)

            dve.wait_ge(s.pe_step, 8 * N_G2)
            dve.wait_ge(s.bd_zero, 8)
            for q in range(NQ + 1):
                inv, chain = q < NQ, q >= 1
                o = q - 1
                if inv:
                    Btok, Ktok, Vtok, LakT, LrbT, LrkT, TiT, Abd = sets[q % 2]

                def units(t):
                    return t[:, :, :]

                def bank(i):
                    return pb[i][:, :].rearrange("p (u t) -> p u t", t=P)

                def level_p(lv):
                    dve.wait_ge(s.lv_p, 5 * q + lv)
                    if q >= 1 and lv == 1:
                        dve.wait_ge(s.lv_t, 9 * q)
                    tt(units(Pm), bank(3), lvl(lv)[:, None, :].to_broadcast([P, QUAD, P]), ALU.mult).then_inc(s.lv_pe, 1)

                def level_t(lv):
                    e = 9 * q + 2 * (lv - 1)
                    if lv == 1:
                        dve.wait_ge(s.t0, q + 1)
                        dve.wait_ge(s.tt0, q + 1)
                    else:
                        dve.wait_ge(s.lv_te, e)
                    if lv < LEVELS - 1:
                        dve.wait_ge(s.lv_t, e + 1)
                        tt(units(Ti), units(Ti), bank(4), ALU.add).then_inc(s.lv_te, 1)
                        e += 1
                    dve.wait_ge(s.lv_t, e + 1)
                    tt(units(TiT), units(TiT), bank(5), ALU.add).then_inc(s.lv_te, 1)

                def state(j):
                    J = 4 * o + j
                    dve.wait_ge(s.ch, 3 * J + 3)
                    if J:
                        dve.wait_ge(s.y_mm, J)
                    g = gC[:, (o // 2) * 8 + J % 8:(o // 2) * 8 + J % 8 + 1]
                    if J % 8 == 0:
                        ts(Hs[:, (J + 1) % 2, :], pb[6][:, 0:P], g, None, ALU.mult).then_inc(s.h_ev, 1)
                    else:
                        dve.wait_ge(s.hg, J - J // 8)
                        stt(Hs[:, (J + 1) % 2, :], pb[6][:, 0:P], g, Hg[:, :], ALU.mult, ALU.add).then_inc(s.h_ev, 1)

                if inv:
                    tri = cst[:, C_TRS:C_TRS + CH]
                    tri_in = cst[:, C_TRS + CH:C_TRS + 2 * CH]
                    if q >= 1:
                        dve.wait_ge(s.lv_p, 5 * q)
                        dve.wait_ge(s.tt0, q)
                    if q >= 2:
                        dve.wait_ge(s.y_mm, 4 * (q - 1))
                    for b, bd, st in ((0, LabT, LrbT), (1, LakT, LrkT)):
                        dve.wait_ge(s.sc_mm, 2 * q + b + 1)
                        for h in range(2):
                            r = slice(64 * h, 64 * h + 64)
                            tt(bd[r, :, r], bank(b)[r, :, 0:CH], tri[r, None, :].to_broadcast([64, QUAD, CH]),
                               ALU.mult).then_inc(s.sc_ev, 1)
                        tt(st[:, :, :], bank(b)[:, :, CH:P], tri_in[:, None, :].to_broadcast([P, QUAD, CH]),
                           ALU.mult).then_inc(s.sc_ev, 1)
                    dve.wait_ge(s.tr_mm, 4 * q + 2)
                    tt(units(Ti), bank(2), lvl(0)[:, None, :].to_broadcast([P, QUAD, P]), ALU.mult).then_inc(s.lab_ev, 1)
                    dve.wait_ge(s.lab_ev, q + 1)
                    tt(units(Ti), units(Ti), ident[:, None, :].to_broadcast([P, QUAD, P]), ALU.add).then_inc(s.t0, 1)
                    level_p(1)
                if chain:
                    state(0)
                if inv:
                    level_t(1)
                for j in range(1, 4):
                    if inv:
                        level_p(j + 1)
                        level_t(j + 1)
                    if chain:
                        state(j)
                if inv:
                    level_p(5)
                    level_t(5)

            dve.wait_ge(s.y_ev, NQ)
            for c in range(CT):
                if c:
                    dve.wait_ge(s.bon_ps, c)
                else:
                    dve.wait_ge(s.tr_mm, 4 * NQ)
                    dve.wait_ge(s.lv_p, 5 * NQ)
                stt(tmp[:, 2, :], St[:, R_, c, :], vec(c, V_RK), St[:, K_, c, :], ALU.mult, ALU.mult).then_inc(s.pr_rdy, 1)
                dve.wait_ge(s.mu_mm, c + 1)
                stt(tmp[:, 0, :], pb[0][:, :], 1.0 / HD, X[:, c, 4:4 + S], ALU.mult, ALU.subtract).then_inc(s.yc_rdy, 1)
                dve.wait_ge(s.bon_ps, c + 1)
                if c:
                    dve.wait_ge(s.x_hi, X_Y + c)
                    dve.wait_ge(s.x_ready, X_Y + c)
                link(tt(tmp[:, 3, :], St[:, V_, c, :], pb[2][:, :], ALU.mult))
                dve.wait_ge(s.gn_rt, c + 1)
                link(dve.reciprocal(tmp[:, 1, :], tmp[:, 1, :]))
                link(stt(tmp[:, 0, :], tmp[:, 0, :], nlnw[:, c:c + 1], tmp[:, 1, :], ALU.mult, ALU.mult))
                link(stt(tmp[:, 0, :], tmp[:, 0, :], vec(c, V_LNB), tmp[:, 3, :], ALU.add, ALU.add))
                dve.wait_ge(s.pe_step, 8 * N_G2 + c + 1)
                tt(tmp[:, 3, :], tmp[:, 0, :], pb[3][:, :], ALU.mult).then_inc(s.y_fin, 1)
                dve.wait_ge(s.y_fin, c + 1)
                low(c, tmp[:, 3, :], X_Y + c)

            squares = [0]

            def clear_acc(i):
                dve.wait_ge(s.norm_ps, i - 1)
                link(dve.memset(tmp[:, 3, :], 0.0))

            def add_square(slot):
                i = squares[0]
                squares[0] += 1
                dve.wait_ge(s.sq_rdy, i + 1)
                dve.wait_ge(s.acc, 8 + i)
                tt(tmp[:, 3, :], tmp[:, 3, :], tmp[:, slot, :], ALU.add).then_inc(s.acc, 1)

            def residual(c, b, sem=s.dense_v):
                tt(X[:, c, 0:S], X[:, c, 0:S], b, ALU.add).then_inc(sem, 1)

            def proj(n0, i):
                dve.wait_ge(s.x_ready, (X_Y if i == 2 else X_O) + CT)
                clear_acc(i)
                for b in range(4):
                    dve.wait_ge(s.pe_step, 8 * (n0 + b + 1))
                    for m in range(2):
                        residual(2 * b + m, pb[2 * (b % 2) + m][:, :])
                    for m in range(2):
                        add_square(m)

            def splits(gain, base):
                for k in range(CT):
                    dve.wait_ge(s.x_hi, base + k + 1)
                    stt(xl[:, k, :], X[:, k, 0:S], vec(k, gain), xh[:, k, :].bitcast(F32), ALU.mult, ALU.subtract)\
                        .then_inc(s.x_ready, 1)

            def mlp(layer, n0, ev0):
                for half in range(2):
                    m0 = n0 + 16 * half
                    e = ev0 + 24 * half
                    h0 = 32 * layer + 16 * half
                    with dve.Fori(0, 4) as i:
                        for h in range(2):
                            done = 4 * i + 2 * h
                            dve.wait_ge(s.pe_step, 8 * (m0 + 2 * i + h + 1))
                            for m in range(2):
                                tt(tmp[:, m, :], pb[2 * h + m][:, :], rstd[:, :], ALU.mult).then_inc(s.dense_v, 1)
                            dve.wait_ge(s.hid_rdy, h0 + done)
                            for m in range(2):
                                dve.wait_ge(s.dense_v, e + done + m + 1)
                                stt(tmp[:, 2 + m, :], tmp[:, m, :], 0.0, tmp[:, m, :], ALU.max, ALU.mult)\
                                    .then_inc(s.hid_f, 1)
                            for m in range(2):
                                dve.wait_ge(s.hid_hi, h0 + done + m + 1)
                                tt(hid_l[:, bass.ds(done + m, 1), :], tmp[:, 2 + m:3 + m, :],
                                   hid_h[:, bass.ds(done + m, 1), :].bitcast(F32), ALU.subtract).then_inc(s.hid_rdy, 1)
                    m0 += 8
                    e += 16
                    if half == 1:
                        for k in range(2):
                            dve.wait_ge(s.p_hi, 2 * layer + k + 1)
                            tt(lora_l[:, k, :], pb[5 + k][:, :], lora_h[:, k, :].bitcast(F32), ALU.subtract).then_inc(s.p_rdy, 1)
                        dve.wait_ge(s.hid_rdy, h0 + 16)
                        clear_acc(3 + 3 * layer)
                    for g in range(4):
                        dve.wait_ge(s.pe_step, 8 * (m0 + 2 * g + 2))
                        for m in range(2):
                            residual(2 * g + m, pb[2 * (g % 2) + m][:, :])
                        if half == 1:
                            for m in range(2):
                                add_square(m)

            def ple(layer, n, gain, base, ni):
                splits(gain, base)
                norm_finish(ni)
                if layer == 0:
                    clear_acc(4)
                for b in range(4):
                    dve.wait_ge(s.pe_step, 8 * (n + 2 + b))
                    for m in range(2):
                        tt(tmp[:, m, :], pb[2 * (b % 2) + m][:, :], rstd[:, :], ALU.mult).then_inc(s.dense_v, 1)
                    for m in range(2):
                        c = 2 * b + m
                        dve.wait_ge(s.sig, 8 * layer + c + 1)
                        dve.wait_ge(s.dense_a, 36 + 8 * layer + c + 1)
                        link(tt(tmp[:, m, :], tmp[:, m, :], UP[:, c, :], ALU.mult))
                        residual(c, tmp[:, m, :], s.upd)
                        if layer == 0:
                            add_square(2)
                    dve.wait_ge(s.upd, 8 * layer + 2 * b + 2)

            dve.wait_ge(s.x2_cp, 8)
            proj(N_WO, 2)
            splits(V_N01, X_M0)
            norm_finish(2)
            mlp(0, L_MLP[0], 16)
            ple(0, L_MLP[0] + 32, V_N02, X_P0, 3)
            splits(V_KV, X_KV)
            norm_finish(4)
            dve.memset(relb[BUCKETS:BUCKETS + 1, :], NEG).then_inc(s.far_row, 1)
            dve.wait_ge(s.bv_mm, 1)
            dve.tensor_copy(bvec[:, 0:S], pb[5][0:8, 0:S]).then_inc(s.bv_ev, 1)
            dve.tensor_copy(bvec[:, S:640], pb[6][0:8, 0:128]).then_inc(s.bv_ev, 1)

            def head_norm(i):
                dst = (KT if i < 8 else QT)[:, i % 8, :]
                dve.wait_ge(s.qk_rt, i + 1)
                link(dve.reciprocal(tmp[:, i % 2, :], tmp[:, i % 2, :]))
                stt(dst, dst, hv[:, 0:1] if i < 8 else qg8, tmp[:, i % 2, :], ALU.mult, ALU.mult).then_inc(s.qk_n, 1)

            def times_rstd(n, b, dsts, sem=s.dense_v):
                dve.wait_ge(s.pe_step, 8 * (n + 1))
                for m in range(2):
                    tt(dsts[m], pb[2 * (b % 2) + m][:, :], rstd[:, :], ALU.mult).then_inc(sem, 1)

            for b in range(4):
                if b:
                    head_norm(2 * b - 2)
                    head_norm(2 * b - 1)
                times_rstd(N_KS + b, b, [KT[:, 2 * b + m, :] for m in range(2)])
            for b in range(4):
                if b == 0:
                    head_norm(6)
                    head_norm(7)
                else:
                    dve.wait_ge(s.v_tr, 2 * b)
                dve.wait_ge(s.pe_step, 8 * (N_VS + b + 1))
                for m in range(2):
                    tt(tmp[:, 2 + m, :], pb[2 * (b % 2) + m][:, :], rstd[:, :], ALU.mult).then_inc(s.dense_v, 1)
            splits(V_N10, X_Q)
            for b in range(4):
                if b:
                    head_norm(8 + 2 * b - 2)
                    head_norm(8 + 2 * b - 1)
                times_rstd(N_Q + b, b, [QT[:, 2 * b + m, :] for m in range(2)])
            head_norm(14)
            head_norm(15)
            dve.wait_ge(s.strip_in, 128)
            dve.wait_ge(s.qk_n, 16)

            def logits(i):
                h, w = i // 4, (i % 4 + 1) * P
                if i >= 1:
                    dve.wait_ge(s.pexp, 2 * i)
                bias = strip[:, h, 0:w]
                bias = bass.AP(bias.tensor, bias.offset + w - 1, [bias.ap[0], [-1, w]])
                for m in range(2):
                    k = 2 * (i % 2) + m
                    dve.wait_ge(s.s_mm, 2 * i + m + 1)
                    dve.tensor_tensor_reduce(out=Lg[:, m, 0:w], in0=pb[2 * (i % 2) + m][:, 0:w], in1=bias,
                                             scale=1.0, scalar=-3.0e38, op0=ALU.add, op1=ALU.max,
                                             accum_out=st_m[:, k:k + 1]).then_inc(s.lg, 1)
                dve.wait_ge(s.lg, 2 * i + 2)
                k = 2 * (i % 2)
                ts(st_n[:, k:k + 2], st_m[:, k:k + 2], -1.0, None, ALU.mult).then_inc(s.nm, 1)

            def combine(i):
                w, k, pr = (i % 4 + 1) * P, 2 * (i % 2), Pr[i % 2]
                dve.wait_ge(s.pexp, 2 * i + 2)
                link(dve.reciprocal(st_r[:, k:k + 2], st_l[:, k:k + 2]))
                link(tt(st_c[:, k:k + 1], st_r[:, k + 1:k + 2], lamf, ALU.mult))
                link(ts(pr[:, 1, 0:w], pr[:, 1, 0:w], st_c[:, k:k + 1], None, ALU.mult))
                if i >= 2:
                    dve.wait_ge(s.at_tr, i - 1)
                stt(At[:, i % 2, 0:w], pr[:, 0, 0:w], st_r[:, k:k + 1], pr[:, 1, 0:w], ALU.mult, ALU.subtract)\
                    .then_inc(s.at_rdy, 1)

            def head_out(h):
                dve.wait_ge(s.o_rt, h + 1)
                link(dve.reciprocal(tmp[:, 1, :], tmp[:, 1, :]))
                if h:
                    dve.wait_ge(s.x_ready, X_O + h)
                stt(tmp[:, 2, :], pb[5 + h % 2][:, :], subg, tmp[:, 1, :], ALU.mult, ALU.mult).then_inc(s.o_f, 1)

            def head_low(h):
                dve.wait_ge(s.o_f, h + 1)
                low(h, tmp[:, 2, :], X_O + h)

            logits(0)
            for i in range(32):
                h, b = i // 4, i % 4
                if i + 1 < 32:
                    logits(i + 1)
                combine(i)
                if h >= 1 and b == 1:
                    head_out(h - 1)
                if h >= 1 and b == 2:
                    head_low(h - 1)
            head_out(7)
            head_low(7)
            proj(N_DO, 5)
            splits(V_N11, X_M1)
            norm_finish(5)
            mlp(1, L_MLP[1], 104)
            ple(1, L_MLP[1] + 32, V_N12, X_P1, 6)


_INS = ["x", "p", "norm_g", "mlp_w1", "mlp_w2", "ple_w_up", "ple_w_gate", "rwkv_mix", "rwkv_w_rkvo", "rwkv_w0",
        "rwkv_w1", "rwkv_w2", "rwkv_a0", "rwkv_a1", "rwkv_a2", "rwkv_g1", "rwkv_g2", "rwkv_k_k", "rwkv_k_a",
        "rwkv_r_k", "rwkv_ln_w", "rwkv_ln_b", "kv_norm_g", "w_k_shared", "w_v_shared", "k_norm_g", "diff_w_q",
        "diff_q_norm_g", "diff_lam", "diff_subln_g", "diff_w_o", "rel_bias"]


def build(nc, shapes):
    args = [nc.dram_tensor(f"in_{n}_dram", shape, F32, kind="ExternalInput").ap() for n, shape in shapes]
    out = nc.dram_tensor("out_0_dram", (1, S, D), F32, kind="ExternalOutput").ap()
    trunk(nc, *args, out)


def kernel(**inputs):
    import numpy as _np
    import concourse.bacc as _bacc
    from concourse.bass_utils import run_bass_kernel_spmd as _run

    nc = _bacc.Bacc("TRN2", target_bir_lowering=False, num_devices=1)
    arrays = {f"in_{n}_dram": _np.ascontiguousarray(inputs[n]) for n in _INS}
    arrays["in_consts_dram"] = shape_constants()
    build(nc, [(n, arrays[f"in_{n}_dram"].shape) for n in _INS + ["consts"]])
    r = _run(nc, [arrays], core_ids=[0])
    return r.results[0]["out_0_dram"]
```

```python
import math
from contextlib import ExitStack

import numpy as np

import concourse.bass as bass
from concourse import mybir

F32 = mybir.dt.float32
F32R = mybir.dt.float32r
ALU = mybir.AluOpType
ACT = mybir.ActivationFunctionType
AX = mybir.AxisListType

P = 128
D = 1024
S = 512
CT = D // P
TT = S // P
FF = 4 * D
PLE = 256
HD = 64
CH = 64
QUAD = 4
NQ = CT * S // (CH * QUAD)
LEVELS = 6
BUCKETS, MAX_DIST = 32, 128
LAMBDA_INIT = 0.8 - 0.6 * math.exp(-0.3)
KAPPA = math.exp(-0.5)
NEG = -1.0e30
NORM_EPS, GN_EPS = 1e-6, 64e-5

(V_N00, V_N01, V_N02, V_N10, V_N11, V_N12, V_KV, V_MIX, _1, _2, _3, _4, _5,
 V_W0, V_A0, V_KK, V_KA, V_LNW, V_LNB, V_RK) = range(20)
NV = 20
MIX_R, MIX_W, MIX_K, MIX_V, MIX_A, MIX_G = range(6)

C_ID, C_BONES, C_ONES = 0, 128, 256
C_LVL = 384
C_TRS = C_LVL + LEVELS * P
C_SEG = C_TRS + 2 * CH
C_END = C_SEG + S
C_LVS = C_END
C_IDS = C_LVS + LEVELS * CH
C_CEN = C_IDS + CH
C_SEL = C_CEN + P
C_EXP = C_SEL + 32
C_HOT = C_EXP + D
C_ALL = C_HOT + 640


def shape_constants():
    c = np.zeros((P, C_ALL), np.float32)
    i = np.arange(P)
    c[:, C_ID:C_ID + P] = np.eye(P)
    c[:, C_BONES:C_BONES + P] = (i[:, None] // HD) == (i[None, :] // HD)
    c[:, C_ONES:C_ONES + P] = 1
    for lv in range(LEVELS):
        b = 1 << lv
        low = ((i[:, None] // (2 * b)) == (i[None, :] // (2 * b))) & ((i[:, None] // b) % 2 == 1) & ((i[None, :] // b) % 2 == 0)
        low = low - np.eye(P, dtype=np.float32)
        c[:, C_LVL + lv * P:C_LVL + (lv + 1) * P] = low
        c[:, C_LVS + lv * CH:C_LVS + (lv + 1) * CH] = low[:, :CH] + low[:, CH:]
    s, t = (i % CH)[:, None], np.arange(CH)[None, :]
    c[:, C_IDS:C_IDS + CH] = s == t
    c[:, C_TRS:C_TRS + CH] = s < t
    c[:, C_TRS + CH:C_TRS + 2 * CH] = s <= t
    c[:, C_SEG:C_SEG + S] = (np.arange(S) % CH != 0)[None, :]
    c[:, C_CEN:C_CEN + P] = np.eye(P) - ((i[:, None] // HD) == (i[None, :] // HD)) / HD
    c[i, C_SEL + 14 + i // HD] = 1
    for h in range(D // HD):
        c[h, C_EXP + h * HD:C_EXP + (h + 1) * HD] = 1
    for x in range(640):
        n = x - (P - 1)
        if n < 0:
            c[BUCKETS, C_HOT + x] = 1
            continue
        b = n
        if n >= BUCKETS // 2:
            b = BUCKETS // 2 + int(math.log(n / (BUCKETS // 2)) / math.log(MAX_DIST / (BUCKETS // 2)) * (BUCKETS // 2) + 1e-9)
        c[min(b, BUCKETS - 1), C_HOT + x] = 1
    return c


class Link:

    def __init__(self, eng, sem):
        self.eng, self.sem, self.n = eng, sem, 0

    def mark(self, ins):
        ins.then_inc(self.sem, 1)
        self.n = self.n + 1

    def wait(self):
        self.eng.wait_ge(self.sem, self.n)

    def __call__(self, ins):
        self.mark(ins)
        self.wait()


N_W1, N_A1, N_G1, N_WA2, N_K, N_R, N_V, N_G2, N_WO = 0, 1, 2, 3, 4, 8, 12, 16, 17
L_MLP = (21, 74)
N_KS, N_VS, N_Q, N_DO = 58, 62, 66, 70
N_ALL = 111
X_W, X_A, X_G, X_K, X_R, X_V, X_Y, X_M0, X_P0, X_KV, X_Q, X_O, X_M1, X_P1 = (8 * i for i in range(14))


def trunk(nc, x, p, norm_g, mlp_w1, mlp_w2, ple_w_up, ple_w_gate, rwkv_mix, rwkv_w_rkvo, rwkv_w0, rwkv_w1,
          rwkv_w2, rwkv_a0, rwkv_a1, rwkv_a2, rwkv_g1, rwkv_g2, rwkv_k_k, rwkv_k_a, rwkv_r_k, rwkv_ln_w,
          rwkv_ln_b, kv_norm_g, w_k_shared, w_v_shared, k_norm_g, diff_w_q, diff_q_norm_g, diff_lam,
          diff_subln_g, diff_w_o, rel_bias, consts, out):
    bias_rows = nc.dram_tensor("bias_rows", [8, 640], F32, kind="Internal").ap()
    ctx = ExitStack()
    with ctx:
        slab_bytes = 212800
        base = (nc.sbuf_base + 31) // 32 * 32
        ctx.enter_context(nc.sbuf_tensor("slab", [P, (slab_bytes + 32) // 4], F32))

        def at(name, offset, shape, dtype=F32):
            size = int(np.prod(shape[1:])) * 4
            assert offset + size <= slab_bytes, (name, offset, size)
            return nc.alloc_sbuf_tensor_at(name, shape, dtype, offset=base + offset)

        W_RAW, W_HI, W_LO, XH, XL, XX = 0, 16384, 32768, 49152, 65536, 81920
        ST, HIDH, HIDL, RSTD, TMP, CST = 98432, 180352, 186496, 192640, 194688, 202880
        wraw = at("wraw", W_RAW, [P, 2, 2048])
        whi = at("whi", W_HI, [P, 2, 2048], F32R)
        wlo = at("wlo", W_LO, [P, 2, 2048], F32R)
        xh = at("xh", XH, [P, CT, S], F32R)
        xl = at("xl", XL, [P, CT, S], F32R)
        X = at("X", XX, [P, CT, S + 4])
        lora_h = at("lora_h", HIDH, [P, 3, S], F32R)
        lora_l = at("lora_l", HIDL, [P, 3, S], F32R)
        rstd = at("rstd", RSTD, [P, S])
        tmp = at("tmp", TMP, [P, 4, S])
        cst = at("cst", CST, [P, C_END])
        PV = at("PV", CST + 4 * C_END, [P, CT, NV])
        small = at("small", CST + 4 * C_END + 4 * CT * NV, [P, 224])
        hv = small[:, 0:4]
        omka = small[:, 12:20]
        gC = small[:, 20:84]
        eps_n, eps_g, eps_0 = small[:, 84:85], small[:, 85:86], small[:, 86:87]
        lamf = small[:, 87:88]
        st_m, st_n, st_l, st_r, st_c = (small[:, 88 + 4 * k:92 + 4 * k] for k in range(5))
        lamw = small[:, 108:112]
        omix = small[:, 112:160]
        omix3 = omix.rearrange("p (c m) -> p c m", m=6)
        subg = small[:, 160:161]
        qg8 = small[:, 161:162]
        one_col = small[:, 162:178]

        St = at("St", ST, [P, 5, CT, S])
        LW, R_, K_, A_, V_ = range(5)
        xtok = at("xtok", ST + 4 * 16384, [P, TT, D])
        vrows = at("vrows", ST + 3 * 16384, [NV, D])
        hrows = at("hrows", ST + 3 * 16384 + 4096, [3, P])
        xtok2 = at("xtok2", ST, [P, TT, D])
        gn_c = at("gn_c", ST + 3 * 16384, [P, C_HOT - C_CEN])
        centre, head_sel, head_exp = gn_c[:, 0:P], gn_c[:, P:P + 32], gn_c[0:D // HD, P + 32:]
        prep_a = at("prep_a", HIDH, [P, S])
        prep_b = at("prep_b", HIDL, [P, S])
        sets = [[at(f"{n}{k}", W_HI + 14336 * k + o, [P, QUAD, w]) for n, o, w in (
            ("Btok", 0, P), ("Ktok", 2048, P), ("Vtok", 4096, P), ("LakT", 6144, P), ("LrbT", 8192, CH),
            ("LrkT", 9216, CH), ("TiT", 10240, P), ("Abd", 12288, P))] for k in range(3)]
        INV = W_HI + 3 * 14336
        MnT, Pbd, Pst, Tst, TTst = ([at(f"{n}{k}", INV + 7168 * k + o, [P, QUAD, w]) for k in range(2)] for n, o, w in (
            ("MnT", 0, P), ("Pbd", 2048, P), ("Pst", 4096, CH), ("Tst", 5120, CH), ("TTst", 6144, CH)))
        CHN = INV + 2 * 7168
        Hs = at("Hs", CHN, [P, 2, P])
        Zs = at("Zs", CHN + 1024, [P, P])
        Us = at("Us", CHN + 1536, [P, P])
        Hg = at("Hg", CHN + 2048, [P, P])
        inv_c = at("inv_c", HIDH, [P, (LEVELS + 1) * CH])
        Bbd = at("Bbd", TMP, [P, QUAD, P])
        Kbd = at("Kbd", TMP + 2048, [P, QUAD, P])
        Vbd = at("Vbd", TMP + 4096, [P, QUAD, P])
        hid_h = at("hid_h", ST, [P, 16, S], F32R)
        hid_l = at("hid_l", ST + 32768, [P, 16, S], F32R)
        UP = at("UP", ST + 65536, [P, CT, S])
        ptok = at("ptok", ST + 65536, [P, TT, PLE])
        KT = at("KT", ST, [P, CT, S])
        QT = at("QT", ST + 16384, [P, CT, S])
        VT = at("VT", ST + 32768, [P, CT, TT, P])
        strip = at("strip", ST + 49152, [P, 8, S])
        Lg = [at("Lg0", ST + 65536, [P, 2, S]), at("Lg1", HIDL, [P, 2, S])]
        Pr = [at("Pr0", ST + 69632, [P, 2, S]), at("Pr1", HIDH, [P, 2, S])]
        At = at("At", ST + 73728, [P, 2, S])
        ATt = at("ATt", ST + 77824, [P, 2, S])
        hot = at("hot", ST + 65536, [P, 640])
        relb = at("relb", ST + 69632, [P, 8])
        bvec = at("bvec", ST + 73728, [8, 640])
        lrow = at("lrow", HIDH + 4096, [P, 4, HD])
        OT = at("OT", ST, [P, TT, D])

        pb = [ctx.enter_context(nc.psum_tensor(f"pb{i}", [P, S], F32)) for i in range(8)]

        ident = cst[:, C_ID:C_ID + P]
        bones = cst[:, C_BONES:C_BONES + P]
        ones = cst[:, C_ONES:C_ONES + P]

        id_st = inv_c[:, LEVELS * CH:]

        names = """inv_in gnc_in raw0 raw1 w_hi w_lo pe_step cst_in x_in rows_in hrows_in x2_in p_in lam_in hot_in
            rel_in bvec_out strip_in out_st x_tr xt_cp xt_sq par_tr par_ev small_set gains lam_s lam_e lam_rdy
            h_ready mix_a mix_b x_hi x_ready acc norm_ps norm_rt dense_a dense_v act_link vec_link pool_link
            lora_hi lora_rdy g_cum exps kk_sq kk_ps kk_rt prep
            bd_a bd_p bd_zero set_zero sc_mm sc_ev mn_rdy tr_mm tr_ev p_mm0 p_mm1 p_ev0 p_ev1 t_mm0 t_mm1 t_ev0 t_ev1
            tt_mm0 tt_mm1 tt_ev0 tt_ev1 ch z_ev h_ev hg y_mm y_ev
            mu_mm yc_rdy gn_sq gn_ps gn_rt gn_rs rb_ps pr_rdy bon_ps bon_v y_fin x2_tr x2_cp
            hid_f hid_hi hid_rdy sq_rdy p_tr p_hi p_rdy sig upd far_row bv_mm bv_ev
            qk_sq qk_ps qk_rt qk_n v_tr v_ev s_mm lg pexp rec scaled at_rdy at_tr at_ev o_mm o_cp o_sq o_ps o_rt o_rs ob_ps o_f
            fin_tr fin_ev""".split()
        sem = {n: ctx.enter_context(nc.semaphore(n)) for n in names}
        s = type("Sems", (), sem)
        s.p_mm, s.p_ev, s.t_mm, s.t_ev, s.tt_mm, s.tt_ev = (
            (sem[n + "0"], sem[n + "1"]) for n in ("p_mm", "p_ev", "t_mm", "t_ev", "tt_mm", "tt_ev"))

        def vec(c, v):
            return PV[:, c, v:v + 1]

        def block_rows(w, m2):
            return w.rearrange("(k p) n -> p k n", p=P)[:, :, bass.ds(m2 * 256, 256)]

        block = ctx.enter_context(nc.Block())

        @block.sync
        def _(sp):
            for t in range(TT):
                sp.dma_start(xtok[:, t, :], x[0, t * P:(t + 1) * P, :]).then_inc(s.x_in, 16)
            raw = (s.raw0, s.raw1)

            def slot_free(n):
                sp.wait_ge(s.w_lo, n - 1)

            def load(n, par, parts):
                for dst, src in parts:
                    sp.dma_start(dst, src).then_inc(raw[par], 16)

            r0 = wraw[:, 0, :]
            r1 = wraw[:, 1, :]

            def cols(r, w, k=CT):
                return r[:, 0:k * w].rearrange("p (k n) -> p k n", n=w)
            w1v = rwkv_w1[0].rearrange("(k p) n -> p k n", p=P)
            a1v = rwkv_a1[0].rearrange("(k p) n -> p k n", p=P)
            g1v = rwkv_g1[0].rearrange("(k p) n -> p k n", p=P)
            load(0, 0, [(cols(r0, P)[:, :, 0:64], w1v), (cols(r0, P)[:, :, 64:128], w1v)])
            load(1, 1, [(cols(r1, P)[:, :, 0:64], a1v), (cols(r1, P)[:, :, 64:128], a1v)])
            slot_free(2)
            load(2, 0, [(cols(r0, 256)[:, :, 0:128], g1v[:, :, 0:128]),
                        (cols(r0, 256)[:, :, 128:256], g1v[:, :, 32:160])])
            slot_free(3)
            load(3, 1, [(r1[0:64, 0:1024], rwkv_w2[0]), (r1[64:128, 0:1024], rwkv_a2[0])])

            def square(w, n0):
                with sp.Fori(0, 2) as i:
                    for h in range(2):
                        sp.wait_ge(s.w_lo, n0 + 2 * i + h - 1)
                        v = block_rows(w, 2 * i + h)
                        for q in range(2):
                            sp.dma_start(cols(wraw[:, (n0 + h) % 2, :], 256)[:, 4 * q:4 * q + 4, :],
                                         v[:, 4 * q:4 * q + 4, :]).then_inc(raw[(n0 + h) % 2], 16)

            def mlp(layer, n0):
                for half in range(2):
                    m0 = n0 + 16 * half
                    with sp.Fori(0, 4) as i:
                        for h in range(2):
                            sp.wait_ge(s.w_lo, m0 + 2 * i + h - 1)
                            v = block_rows(mlp_w1[layer], 8 * half + 2 * i + h)
                            for q in range(2):
                                sp.dma_start(cols(wraw[:, (m0 + h) % 2, :], 256)[:, 4 * q:4 * q + 4, :],
                                             v[:, 4 * q:4 * q + 4, :]).then_inc(raw[(m0 + h) % 2], 16)
                    m0 += 8
                    with sp.Fori(0, 4) as i:
                        for h in range(2):
                            sp.wait_ge(s.w_lo, m0 + 2 * i + h - 1)
                            rows = mlp_w2[layer][half * 2048 + h * 1024:half * 2048 + (h + 1) * 1024, :]
                            v = block_rows(rows, i)
                            for q in range(2):
                                sp.dma_start(cols(wraw[:, (m0 + h) % 2, :], 256)[:, 4 * q:4 * q + 4, :],
                                             v[:, 4 * q:4 * q + 4, :]).then_inc(raw[(m0 + h) % 2], 16)
                    if half == 0:
                        sp.wait_ge(s.hid_rdy, 32 * layer + 16)
                        sp.dma_start(ptok[:, :, :], p[layer, 0].rearrange("(t p) d -> p t d", p=P)).then_inc(s.p_in, 16)

            def up(layer, n):
                slot_free(n)
                v = ple_w_up[layer].rearrange("(k p) n -> p k n", p=P)
                dst = cols(wraw[:, n % 2, :], 1024, 2)
                load(n, n % 2, [(dst[:, k:k + 1, :], v[:, k:k + 1, :]) for k in range(2)])

            square(rwkv_w_rkvo[0, 1], N_K)
            square(rwkv_w_rkvo[0, 0], N_R)
            square(rwkv_w_rkvo[0, 2], N_V)
            sp.wait_ge(s.prep, CT)
            sp.dma_start(inv_c[:, :], consts[:, C_LVS:C_CEN]).then_inc(s.inv_in, 16)
            sp.wait_ge(s.bd_a, 4 * NQ)
            sp.dma_start(gn_c[:, :], consts[:, C_CEN:C_HOT]).then_inc(s.gnc_in, 16)
            slot_free(N_G2)
            load(N_G2, 0, [(r0[:, 0:1024], rwkv_g2[0][0:128, :]), (r0[:, 1024:2048], rwkv_g2[0][32:160, :])])
            square(rwkv_w_rkvo[0, 3], N_WO)
            mlp(0, L_MLP[0])
            up(0, L_MLP[0] + 32)
            square(ple_w_gate[0], L_MLP[0] + 33)
            square(w_k_shared, N_KS)
            sp.wait_ge(s.bv_ev, 2)
            sp.dma_start(bias_rows, bvec[:, :]).then_inc(s.bvec_out, 16)
            sp.wait_ge(s.bvec_out, 16)
            for h in range(8):
                src = bass.AP(bias_rows.tensor, 640 * h, [[1, P], [1, S]])
                sp.dma_start(strip[:, h, :], src).then_inc(s.strip_in, 16)
            square(w_v_shared, N_VS)
            square(diff_w_q[0], N_Q)
            square(diff_w_o[0], N_DO)
            mlp(1, L_MLP[1])
            up(1, L_MLP[1] + 32)
            square(ple_w_gate[1], L_MLP[1] + 33)
            for c in range(CT // 2):
                sp.wait_ge(s.fin_ev, 2 * (c + 1))
                sp.dma_start(out[0].rearrange("(t p) d -> p t d", p=P)[:, :, 256 * c:256 * (c + 1)],
                             OT[:, :, 256 * c:256 * (c + 1)]).then_inc(s.out_st, 16)
            sp.wait_ge(s.out_st, 16 * (CT // 2))

        @block.gpsimd
        def _(pool):
            def low(n, par, rng, first):
                pool.wait_ge(s.w_hi, n + 1)
                if not first:
                    pool.wait_ge(s.pe_step, 8 * (n - 1))
                pool.tensor_tensor(wlo[:, par, rng], wraw[:, par, rng], whi[:, par, rng].bitcast(F32),
                                   ALU.subtract).then_inc(s.w_lo, 1)

            low(0, 0, slice(0, 1024), True)
            low(1, 1, slice(0, 1024), True)
            low(2, 0, slice(0, 2048), False)
            low(3, 1, slice(0, 1024), False)

            def lows(n0, n1):
                assert (n1 - n0) % 2 == 0
                with pool.Fori(0, (n1 - n0) // 2) as i:
                    for h in range(2):
                        low(n0 + 2 * i + h, (n0 + h) % 2, slice(0, 2048), False)

            lows(N_K, N_V + 4)

            link = Link(pool, s.pool_link)
            pool.wait_ge(s.prep, CT)
            pool.wait_ge(s.x_ready, X_V + CT)
            for t in (Bbd, Kbd, Vbd):
                pool.memset(t[:, :, :], 0.0).then_inc(s.bd_zero, 1)
            pool.wait_ge(s.pe_step, 8 * N_G2)
            for k in range(3):
                pool.memset(sets[k][7][:, :, :], 0.0).then_inc(s.bd_zero, 1)
            pool.wait_ge(s.bd_zero, 6)
            for q in range(NQ):
                c, t0 = q // 2, (q % 2) * QUAD * CH
                pool.wait_ge(s.sc_ev, 6 * q + 2)
                pool.tensor_tensor(MnT[q % 2][:, :, :], MnT[q % 2][:, :, :],
                                   ident[:, None, :].to_broadcast([P, QUAD, P]), ALU.subtract).then_inc(s.mn_rdy, 1)
                if q >= 1:
                    pool.wait_ge(s.tr_mm, 3 * q)
                if q >= 3:
                    pool.wait_ge(s.y_mm, 4 * (q - 2))
                if q == 0:
                    pool.wait_ge(s.dense_a, 36)
                pool.wait_ge(s.mn_rdy, q + 1)
                for i, (dst, kind) in enumerate(((Vbd, V_), (sets[q % 3][7], LW))):
                    for h in range(2):
                        if q or i or h:
                            pool.wait_ge(s.bd_p, 4 * q + 2 * i + h)
                        pool.tensor_copy(dst[64 * h:64 * h + 64, :, 64 * h:64 * h + 64],
                                         St[64 * h:64 * h + 64, kind, c, t0:t0 + QUAD * CH]
                                         .rearrange("p (u t) -> p u t", t=CH)).then_inc(s.bd_p, 1)
                pool.wait_ge(s.bd_p, 4 * q + 4)

            pool.wait_ge(s.y_mm, 4 * NQ)
            low(N_G2, 0, slice(0, 2048), False)
            low(N_WO, 1, slice(0, 2048), False)
            lows(N_WO + 1, L_MLP[0] + 31)
            low(L_MLP[0] + 31, 0, slice(0, 2048), False)
            low(L_MLP[0] + 32, 1, slice(0, 2048), False)
            lows(L_MLP[0] + 33, N_DO)
            low(N_DO, 0, slice(0, 2048), False)
            low(N_DO + 1, 1, slice(0, 2048), False)
            for i in range(32):
                w, k = (i % 4 + 1) * P, 2 * (i % 2)
                pool.wait_ge(s.rec, i + 1)
                pool.tensor_scalar(Pr[i % 2][:, 1, 0:w], Pr[i % 2][:, 1, 0:w], st_r[:, k + 1:k + 2], lamf, ALU.mult, ALU.mult)\
                    .then_inc(s.scaled, 1)
            lows(N_DO + 2, N_DO + 4)
            lows(L_MLP[1], L_MLP[1] + 32)
            low(L_MLP[1] + 32, 0, slice(0, 2048), False)
            lows(L_MLP[1] + 33, N_ALL)

        @block.tensor
        def _(pe):
            mm = pe.matmul

            def three(o, n, w, xs, first, last):
                (wh, wl), (ah, al) = w, xs
                mm(o, wh, ah, start=first, stop=False)
                mm(o, wh, al, start=False, stop=False)
                return mm(o, wl, ah, start=False, stop=last)

            def wslice(par, c0):
                return whi[:, par, c0:c0 + P], wlo[:, par, c0:c0 + P]

            def xs(k):
                return xh[:, k, :], xl[:, k, :]

            pe.wait_ge(s.cst_in, 16)
            pe.wait_ge(s.rows_in, 160)
            for c in range(CT):
                pe.transpose(pb[7][:, c * NV:(c + 1) * NV], vrows[:, c * P:(c + 1) * P], ident[0:NV, 0:NV])
            pe.wait_ge(s.hrows_in, 80)
            pe.transpose(pb[7][:, CT * NV:CT * NV + 3], hrows[:, :], ident[0:3, 0:3]).then_inc(s.par_tr, 1)
            pe.wait_ge(s.x_in, 64)
            for c in range(CT):
                if c == 7:
                    pe.wait_ge(s.xt_sq, 1)
                for t in range(TT):
                    ins = pe.transpose(pb[c % 7][:, t * P:(t + 1) * P], xtok[:, t, c * P:(c + 1) * P], ident)
                ins.then_inc(s.x_tr, 1)
            norms = [0]

            def norm_total(bank):
                norms[0] += 1
                pe.wait_ge(s.acc, 8 * norms[0])
                mm(pb[bank][:, :], ones, tmp[:, 3, :], start=True, stop=True).then_inc(s.norm_ps, 1)

            pe.wait_ge(s.xt_sq, 5)
            norm_total(4)

            def dense_block(n, par, pair, width=2, x_base=None, hook=None, rows=None):
                pe.wait_ge(s.w_lo, n + 1)
                for k in range(CT):
                    if x_base is not None:
                        pe.wait_ge(s.x_ready, x_base + k + 1)
                    if hook and k in hook:
                        hook[k]()
                    for m in range(width):
                        ins = three(pb[2 * pair + m][:, :], n, wslice(par, k * P * width + m * P), xs(k),
                                    k == 0, k == CT - 1)
                    ins.then_inc(s.pe_step, 1)

            pe.wait_ge(s.xt_cp, 8)
            pe.wait_ge(s.xt_sq, 8)
            pe.wait_ge(s.par_ev, 2)
            dense_block(0, 0, 0, 1, X_W)
            dense_block(1, 1, 1, 1, X_A)
            pe.wait_ge(s.dense_a, 1)
            dense_block(2, 0, 0, 2, X_G)
            pe.wait_ge(s.w_lo, 4)
            pe.wait_ge(s.lora_rdy, 1)
            for g in range(8):
                if g == 0:
                    pe.wait_ge(s.dense_a, 2)
                elif g == 1:
                    pe.wait_ge(s.dense_a, 4)
                else:
                    pe.wait_ge(s.dense_a, 4 + 2 * (g - 1))
                pair = 1 - g % 2
                r = slice(0, 64) if g < 4 else slice(64, 128)
                for m in range(2):
                    c = (2 * g + m) % 8
                    w = (whi[r, 1, c * P:(c + 1) * P], wlo[r, 1, c * P:(c + 1) * P])
                    ins = three(pb[2 * pair + m][:, :], 3, w, (lora_h[r, 0, :], lora_l[r, 0, :]), True, True)
                ins.then_inc(s.pe_step, 1)

            def kk_total(c):
                def f():
                    pe.wait_ge(s.kk_sq, c + 1)
                    if c >= 2:
                        pe.wait_ge(s.kk_rt, c - 1)
                    mm(pb[4 + c % 2][:, :], bones, tmp[:, c % 2, :], start=True, stop=True).then_inc(s.kk_ps, 1)
                return f

            for t in range(12):
                if t < 2:
                    pe.wait_ge(s.dense_a, 18 + 2 * t)
                elif t < 6:
                    pe.wait_ge(s.dense_a, 20 + 2 * (t - 1))
                elif t < 10:
                    pe.wait_ge(s.dense_v, 2 * (t - 5))
                else:
                    pe.wait_ge(s.dense_a, 28 + 2 * (t - 9))
                dense_block(N_K + t, t % 2, 1 - t % 2, 2, {0: X_K, 4: X_R, 8: X_V}.get(t),
                            {3: kk_total(t - 1)} if 1 <= t <= 8 else None)

            pe.wait_ge(s.dense_a, 36)
            pe.wait_ge(s.prep, CT)
            pe.wait_ge(s.dense_v, 8)
            pe.wait_ge(s.bd_zero, 6)
            pe.wait_ge(s.set_zero, 8)
            pe.wait_ge(s.inv_in, 16)

            def score(q, i):
                if i == 0:
                    pe.wait_ge(s.bd_a, 4 * (q + 1))
                    if q >= 2:
                        pe.wait_ge(s.p_ev[q % 2], 12 * (q // 2))
                        pe.wait_ge(s.tt_ev[q % 2], 17 * (q // 2))
                tokens = slice((q % 2) * QUAD * CH, (q % 2 + 1) * QUAD * CH)
                src = (Bbd, Kbd)[i]
                for u in range(QUAD):
                    t = slice(tokens.start + u * CH, tokens.start + (u + 1) * CH)
                    ins = mm(pb[3 + 2 * (q % 2) + i][:, u * P:(u + 1) * P], src[:, u, :], St[:, LW:R_ + 1, q // 2, t],
                             start=True, stop=True)
                ins.then_inc(s.sc_mm, 1)

            def turn(q, i):
                if q or i:
                    pe.wait_ge(s.tr_ev, 3 * q + i)
                if i == 2:
                    pe.wait_ge(s.bd_p, 4 * q + 2)
                for u in range(QUAD):
                    ins = pe.transpose(pb[2][:, u * P:(u + 1) * P], (Bbd, Kbd, Vbd)[i][:, u, :], ident)
                ins.then_inc(s.tr_mm, 1)

            def level_p(q, lv):
                par, n = q % 2, q // 2
                if lv == 0:
                    pe.wait_ge(s.mn_rdy, q + 1)
                    pe.wait_ge(s.sc_ev, 6 * q + 3)
                elif lv == 1:
                    pe.wait_ge(s.p_ev[par], 12 * n + 2)
                else:
                    pe.wait_ge(s.t_ev[par], 4 * n + lv - 1)
                for u in range(QUAD):
                    T = (id_st, Pst[par][:, u, :])[lv] if lv < 2 else Tst[par][:, u, :]
                    ins = mm(pb[3 + 2 * par][:, u * CH:(u + 1) * CH], MnT[par][:, u, :], T, start=True, stop=True)
                ins.then_inc(s.p_mm[par], 1)

            def level_t(q, lv):
                par, n = q % 2, q // 2
                pe.wait_ge(s.p_ev[par], 12 * n + 2 * lv + 1)
                if lv:
                    pe.wait_ge(s.tt_ev[par], 17 * n + 3 * lv)
                else:
                    pe.wait_ge(s.sc_ev, 6 * q + 6)
                for u in range(QUAD):
                    TT = TTst[par][:, u, :] if lv else id_st
                    ins = mm(pb[4 + 2 * par][:, u * CH:(u + 1) * CH], Pbd[par][:, u, :], TT, start=True, stop=True)
                ins.then_inc(s.tt_mm[par], 1)
                if 1 <= lv < LEVELS - 1:
                    pe.wait_ge(s.p_ev[par], 12 * n + 2 * lv + 2)
                    for u in range(QUAD):
                        ins = mm(pb[3 + 2 * par][:, (QUAD + u) * CH:(QUAD + u + 1) * CH], sets[q % 3][6][:, u, :],
                                 Pst[par][:, u, :], start=True, stop=True)
                    ins.then_inc(s.t_mm[par], 1)

            def chain_z(o, j):
                oB, oK, oV, oLak, oLrb, oLrk, oTiT, oA = sets[o % 3]
                J = 4 * o + j
                if J >= 1:
                    pe.wait_ge(s.h_ev, J)
                new = J % 8 == 0
                if j == 0:
                    pe.wait_ge(s.tr_ev, 3 * o + 3)
                    pe.wait_ge(s.sc_ev, 6 * o + 6)
                    pe.wait_ge(s.bd_p, 4 * o + 4)
                ins = mm(pb[0][:, 0:P], oLak[:, j, :], oV[:, j, :], start=True, stop=new)
                if not new:
                    ins = mm(pb[0][:, 0:P], oA[:, j, :], Hs[:, J % 2, :], start=False, stop=True)
                ins.then_inc(s.ch, 1)

            def chain_u(o, j):
                pe.wait_ge(s.z_ev, 2 * (4 * o + j) + 1)
                if j == 0:
                    pe.wait_ge(s.tt_ev[o % 2], 17 * (o // 2) + 17)
                mm(pb[0][:, 0:P], sets[o % 3][6][:, j, :], Zs[:, :], start=True, stop=True).then_inc(s.ch, 1)

            def chain_h(o, j):
                oB, oK, oV, oLak, oLrb, oLrk, oTiT, oA = sets[o % 3]
                J = 4 * o + j
                new = J % 8 == 0
                pe.wait_ge(s.z_ev, 2 * J + 2)
                mm(pb[0][:, 0:P], oK[:, j, :], oV[:, j, :], start=True, stop=False)
                mm(pb[0][:, 0:P], oB[:, j, :], Us[:, :], start=False, stop=True).then_inc(s.ch, 1)
                if j == 0 and o >= 1:
                    pe.wait_ge(s.y_ev, o)
                y = pb[1][:, j * CH:(j + 1) * CH]
                t = slice((J % 8) * CH, (J % 8 + 1) * CH)
                if not new:
                    mm(y, Hs[:, J % 2, :], St[:, R_, o // 2, t], start=True, stop=False)
                mm(y, Us[:, :], oLrb[:, j, :], start=new, stop=False)
                mm(y, oV[:, j, :], oLrk[:, j, :], start=False, stop=True).then_inc(s.y_mm, 1)

            for i in range(NQ + 2):
                a, b, o = i, i - 1, i - 2
                first, second, chain = a < NQ, 0 <= b < NQ, o >= 0
                if first:
                    score(a, 0)
                if chain:
                    chain_z(o, 0)
                if second:
                    level_p(b, 3)
                if chain:
                    chain_u(o, 0)
                if first:
                    score(a, 1)
                if second:
                    level_t(b, 3)
                if chain:
                    chain_h(o, 0)
                if first:
                    turn(a, 0)
                if second:
                    level_p(b, 4)
                if chain:
                    chain_z(o, 1)
                if first:
                    level_p(a, 0)
                if chain:
                    chain_u(o, 1)
                if second:
                    level_t(b, 4)
                if first:
                    turn(a, 1)
                if chain:
                    chain_h(o, 1)
                if first:
                    level_t(a, 0)
                if second:
                    level_p(b, 5)
                if chain:
                    chain_z(o, 2)
                if first:
                    level_p(a, 1)
                if chain:
                    chain_u(o, 2)
                if second:
                    level_t(b, 5)
                if chain:
                    chain_h(o, 2)
                if first:
                    level_t(a, 1)
                if chain:
                    chain_z(o, 3)
                if first:
                    turn(a, 2)
                    level_p(a, 2)
                if chain:
                    chain_u(o, 3)
                if first:
                    level_t(a, 2)
                if chain:
                    chain_h(o, 3)

            def variance(c):
                pe.wait_ge(s.gn_sq, c + 1)
                mm(pb[7][0:16, :], head_sel[:, 14 - 2 * c:30 - 2 * c], tmp[:, c % 2, :], start=(c == 0), stop=(c == CT - 1))\
                    .then_inc(s.gn_ps, 1)

            pe.wait_ge(s.h_ev, 4 * NQ)
            pe.wait_ge(s.y_ev, NQ)
            pe.wait_ge(s.tr_ev, 3 * NQ)
            for par in range(2):
                pe.wait_ge(s.p_ev[par], 12 * NQ // 2)
                pe.wait_ge(s.t_ev[par], 4 * NQ // 2)
                pe.wait_ge(s.tt_ev[par], 17 * NQ // 2)
            pe.wait_ge(s.gnc_in, 16)
            for c in range(CT):
                if c >= 2:
                    pe.wait_ge(s.gn_sq, c - 1)
                mm(pb[c % 2][:, :], centre, X[:, c, 4:4 + S], start=True, stop=True).then_inc(s.mu_mm, 1)
                pe.wait_ge(s.pr_rdy, c + 1)
                if c >= 2:
                    pe.wait_ge(s.bon_v, c - 1)
                mm(pb[2 + c % 2][:, :], bones, tmp[:, 2 + c % 2, :], start=True, stop=True).then_inc(s.bon_ps, 1)
                if c:
                    variance(c - 1)
            variance(CT - 1)
            pe.wait_ge(s.w_lo, N_G2 + 1)
            pe.wait_ge(s.lora_rdy, 3)
            for c in range(CT):
                if c >= 2:
                    pe.wait_ge(s.y_fin, c - 1)
                if c == 1:
                    pe.wait_ge(s.gn_rt, 1)
                w = (whi[:, 0, c * P:(c + 1) * P], wlo[:, 0, c * P:(c + 1) * P])
                three(pb[6 + c % 2][:, :], N_G2, w, (lora_h[:, 1, :], lora_l[:, 1, :]), True, False)
                w = (whi[96:128, 0, 1024 + c * P:1024 + (c + 1) * P], wlo[96:128, 0, 1024 + c * P:1024 + (c + 1) * P])
                three(pb[6 + c % 2][:, :], N_G2, w, (lora_h[96:128, 2, :], lora_l[96:128, 2, :]), False, True)\
                    .then_inc(s.pe_step, 1)
                pe.wait_ge(s.x2_in, 64)
                if c >= 2:
                    pe.wait_ge(s.x2_cp, c - 1)
                else:
                    pe.wait_ge(s.bon_v, CT)
                for t in range(TT):
                    ins = pe.transpose(pb[2 + c % 2][:, t * P:(t + 1) * P], xtok2[:, t, c * P:(c + 1) * P], ident)
                ins.then_inc(s.x2_tr, 1)
                pe.wait_ge(s.gn_rs, 1)
                mm(pb[4 + c % 2][:, :], head_exp[:, c * P:(c + 1) * P], rstd[0:16, :], start=True, stop=True)\
                    .then_inc(s.rb_ps, 1)

            def proj(n0, x_base, ev0, hook=None):
                for b in range(4):
                    if b >= 2:
                        pe.wait_ge(s.dense_v, ev0 + 2 * (b - 1))
                    dense_block(n0 + b, (n0 + b) % 2, b % 2, 2, x_base if b == 0 else None, hook if b == 0 else None)

            pe.wait_ge(s.gn_sq, CT)
            pe.wait_ge(s.x2_cp, CT)
            proj(N_WO, X_Y, 8)

            def mlp(layer, n0, x_base, ev0):
                for half in range(2):
                    e = ev0 + 24 * half
                    m0 = n0 + 16 * half
                    pe.wait_ge(s.dense_v, e)
                    if half == 0:
                        norm_total(4)
                    with pe.Fori(0, 4) as i:
                        for h in range(2):
                            pe.wait_ge(s.dense_v, e + 2 * (2 * i + h) - 2)
                            dense_block(m0 + 2 * i + h, (m0 + h) % 2, h, 2, x_base if h == 0 else None)
                    m0 += 8
                    e += 16
                    if half == 1:
                        pe.wait_ge(s.p_in, 16 * (layer + 1))
                        for k in range(2):
                            for t in range(TT):
                                ins = pe.transpose(pb[5 + k][:, t * P:(t + 1) * P], ptok[:, t, k * P:(k + 1) * P], ident)
                            ins.then_inc(s.p_tr, 1)
                    pe.wait_ge(s.dense_v, e)
                    with pe.Fori(0, 2) as i:
                        for g in range(2):
                            pe.wait_ge(s.dense_v, e + 2 * (2 * i + g) - 2)
                            for kb in range(2):
                                n = m0 + 4 * i + 2 * g + kb
                                par = (m0 + kb) % 2
                                pe.wait_ge(s.w_lo, n + 1)
                                for k in range(CT):
                                    if g == 0:
                                        pe.wait_ge(s.hid_rdy, 32 * layer + 16 * half + 8 * kb + k + 1)
                                    a = (hid_h[:, 8 * kb + k, :], hid_l[:, 8 * kb + k, :])
                                    for m in range(2):
                                        ins = three(pb[2 * g + m][:, :], n, wslice(par, k * 256 + m * P), a,
                                                    kb == 0 and k == 0, kb == 1 and k == CT - 1)
                                    ins.then_inc(s.pe_step, 1)

            def ple(layer, n, x_base, ev_a, ev0):
                pe.wait_ge(s.w_lo, n + 1)
                pe.wait_ge(s.p_rdy, 2 * (layer + 1))
                pe.wait_ge(s.dense_v, ev0)
                for m in range(CT):
                    if m >= 4:
                        pe.wait_ge(s.dense_a, ev_a + m - 3)
                    for k in range(2):
                        ins = three(pb[m % 4][:, :], n, wslice(n % 2, k * 1024 + m * P), (lora_h[:, k, :], lora_l[:, k, :]),
                                    k == 0, k == 1)
                    ins.then_inc(s.pe_step, 1)
                norm_total(4)
                for b in range(4):
                    if b < 2:
                        pe.wait_ge(s.dense_a, ev_a + 6 + 2 * b)
                    else:
                        pe.wait_ge(s.dense_v, ev0 + 2 * (b - 1))
                    dense_block(n + 1 + b, (n + 1 + b) % 2, b % 2, 2, x_base if b == 0 else None)

            mlp(0, L_MLP[0], X_M0, 16)
            ple(0, L_MLP[0] + 32, X_P0, 36, 64)

            norm_total(4)
            pe.wait_ge(s.far_row, 1)
            pe.wait_ge(s.hot_in, 16)
            pe.wait_ge(s.rel_in, 16)
            mm(pb[5][0:8, 0:S], relb[0:BUCKETS + 1, :], hot[0:BUCKETS + 1, 0:S], start=True, stop=True)
            mm(pb[6][0:8, 0:128], relb[0:BUCKETS + 1, :], hot[0:BUCKETS + 1, S:640], start=True, stop=True).then_inc(s.bv_mm, 1)

            def qk_total(i0):
                def f():
                    for i in (i0, i0 + 1):
                        pe.wait_ge(s.qk_sq, i + 1)
                        if i == 0:
                            pe.wait_ge(s.bv_ev, 2)
                        if i >= 2:
                            pe.wait_ge(s.qk_rt, i - 1)
                        mm(pb[4 + i % 2][:, :], bones, tmp[:, i % 2, :], start=True, stop=True).then_inc(s.qk_ps, 1)
                return f

            def v_turn(i0):
                def f():
                    for i in (i0, i0 + 1):
                        pe.wait_ge(s.dense_v, 80 + i + 1)
                        if i >= 2:
                            pe.wait_ge(s.v_ev, i - 1)
                        for t in range(TT):
                            ins = pe.transpose(pb[6 + i % 2][:, t * P:(t + 1) * P], tmp[:, 2 + i % 2, t * P:(t + 1) * P], ident)
                        ins.then_inc(s.v_tr, 1)
                return f

            for b in range(4):
                pe.wait_ge(s.dense_v, 72 + max(2 * (b - 1), 0))
                dense_block(N_KS + b, b % 2, b % 2, 2, X_KV if b == 0 else None, {5: qk_total(2 * b - 2)} if b else None)
            for b in range(4):
                pe.wait_ge(s.dense_v, 80 + 2 * (b - 1))
                dense_block(N_VS + b, b % 2, b % 2, 2, None, {5: v_turn(2 * b - 2)} if b else {5: qk_total(6)})
            for b in range(4):
                pe.wait_ge(s.dense_v, 88 + 2 * (b - 1))
                dense_block(N_Q + b, b % 2, b % 2, 2, X_Q if b == 0 else None, {5: qk_total(8 + 2 * b - 2)} if b else {5: v_turn(6)})
            pe.wait_ge(s.dense_v, 96)
            qk_total(14)()

            def scores(i):
                h, b = i // 4, i % 4
                w = (b + 1) * P
                if b == 0:
                    pe.wait_ge(s.qk_n, 8 + h + 1)
                if i >= 2:
                    pe.wait_ge(s.lg, 2 * (i - 1))
                for cmp in range(2):
                    r = slice(64 * cmp, 64 * cmp + 64)
                    mm(pb[2 * (i % 2) + cmp][:, 0:w], QT[r, h, b * P:(b + 1) * P], KT[r, h, 0:w],
                       start=True, stop=True).then_inc(s.s_mm, 1)

            def attn_turn(i):
                pe.wait_ge(s.at_rdy, i + 1)
                if i >= 1:
                    pe.wait_ge(s.at_ev, i)
                for j in range(i % 4 + 1):
                    ins = pe.transpose(pb[4][:, j * P:(j + 1) * P], At[:, i % 2, j * P:(j + 1) * P], ident)
                ins.then_inc(s.at_tr, 1)

            def head_total(h):
                pe.wait_ge(s.o_sq, h + 1)
                mm(pb[7][0:8, :], one_col[:, 8 - h:16 - h], tmp[:, h % 2, :], start=(h == 0), stop=(h == 7)).then_inc(s.o_ps, 1)

            def values(i):
                h, b = i // 4, i % 4
                if b == 0 and h >= 2:
                    pe.wait_ge(s.o_sq, h - 1)
                pe.wait_ge(s.at_ev, i + 1)
                for j in range(b + 1):
                    ins = mm(pb[5 + h % 2][:, b * P:(b + 1) * P], VT[:, h, j, :], ATt[:, i % 2, j * P:(j + 1) * P],
                             start=(j == 0), stop=(j == b))
                ins.then_inc(s.o_mm, 1)

            def head_rstd(h):
                if h >= 4:
                    pe.wait_ge(s.o_f, h - 3)
                mm(pb[4 + h % 4][:, :], ident[0:8, h:h + 1].to_broadcast([8, P]), rstd[0:8, :], start=True, stop=True)\
                    .then_inc(s.ob_ps, 1)

            pe.wait_ge(s.v_ev, 8)
            pe.wait_ge(s.dense_v, 96)
            pe.wait_ge(s.qk_rt, 16)
            for i in range(32 + 4):
                if i < 32:
                    scores(i)
                if 0 <= i - 3 < 32:
                    attn_turn(i - 3)
                if i >= 4:
                    values(i - 4)
                if i >= 9 and i % 4 == 1:
                    head_total((i - 9) // 4)
            head_total(7)
            pe.wait_ge(s.o_rs, 1)
            for h in range(4):
                head_rstd(h)
            proj(N_DO, X_O, 96, {k: (lambda h=k + 4: head_rstd(h)) for k in range(4)})
            mlp(1, L_MLP[1], X_M1, 104)
            ple(1, L_MLP[1] + 32, X_P1, 44, 152)
            for c in range(CT):
                pe.wait_ge(s.upd, 8 + c + 1)
                if c >= 4:
                    pe.wait_ge(s.fin_ev, c - 3)
                for t in range(TT):
                    ins = pe.transpose(pb[4 + c % 4][:, t * P:(t + 1) * P], X[:, c, t * P:(t + 1) * P], ident)
                ins.then_inc(s.fin_tr, 1)

        @block.scalar
        def _(act):
            A = act.activation
            raw = (s.raw0, s.raw1)
            act.dma_start(cst[:, :], consts[:, 0:C_END]).then_inc(s.cst_in, 16)

            def row(a):
                return a.rearrange("(o n) -> o n", o=1)

            for dst, src in ((vrows[0:6, :], norm_g.rearrange("a b n -> (a b) n")), (vrows[6:7, :], row(kv_norm_g)),
                             (vrows[7:13, :], rwkv_mix[0]), (vrows[13:14, :], rwkv_w0), (vrows[14:15, :], rwkv_a0),
                             (vrows[15:16, :], rwkv_k_k), (vrows[16:17, :], rwkv_k_a), (vrows[17:18, :], rwkv_ln_w),
                             (vrows[18:19, :], rwkv_ln_b), (vrows[19:20, :], rwkv_r_k.rearrange("o h n -> o (h n)"))):
                act.dma_start(dst, src).then_inc(s.rows_in, 16)
            for i, src in ((0, row(k_norm_g)), (1, diff_q_norm_g)):
                for h in range(2):
                    act.dma_start(hrows[i:i + 1, h * HD:(h + 1) * HD], src).then_inc(s.hrows_in, 16)
            act.dma_start(hrows[2:3, :], diff_subln_g).then_inc(s.hrows_in, 16)
            act.dma_start(lrow[:, :, :], bass.AP(diff_lam.tensor, diff_lam.offset, [[0, P], [HD, 4], [1, HD]]))\
               .then_inc(s.lam_in, 16)

            def high(n, par, rng=slice(0, 2048), first=False):
                act.wait_ge(raw[par], 16 * (n - par) + 32)
                if not first:
                    act.wait_ge(s.pe_step, 8 * (n - 1))
                A(whi[:, par, rng], wraw[:, par, rng], ACT.Copy).then_inc(s.w_hi, 1)

            def split_high(k, src, gain, free):
                if free is not None:
                    act.wait_ge(s.pe_step, free + k + 1)
                if gain is None:
                    A(xh[:, k, :], src, ACT.Copy).then_inc(s.x_hi, 1)
                else:
                    A(xh[:, k, :], src, ACT.Copy, scale=gain).then_inc(s.x_hi, 1)

            def norm_root(i):
                act.wait_ge(s.norm_ps, i)
                A(rstd[:, :], pb[4][:, :], ACT.Sqrt, bias=eps_n, scale=1.0 / D).then_inc(s.norm_rt, 1)

            for c in range(CT):
                act.wait_ge(s.x_tr, c + 1)
                A(X[:, c, 4:4 + S], pb[c % 7][:, :], ACT.Copy).then_inc(s.xt_cp, 1)
                if c >= 2:
                    act.wait_ge(s.acc, c - 1)
                A(tmp[:, c % 2, :], pb[c % 7][:, :], ACT.Square).then_inc(s.xt_sq, 1)
            high(0, 0, slice(0, 1024), True)
            high(1, 1, slice(0, 1024), True)
            act.wait_ge(s.small_set, 1)
            norm_root(1)
            act.wait_ge(s.lam_s, 1)
            A(lamw[:, 2:4], lamw[:, 0:2], ACT.Exp).then_inc(s.lam_e, 1)

            def mixes(i, mix, free):
                def product(k):
                    if i == 0:
                        act.wait_ge(s.h_ready, k + 1)
                    if 8 * i + k >= 2:
                        act.wait_ge(s.mix_b, 8 * i + k - 1)
                    A(pb[6 + k % 2][:, :], X[:, k, 3:3 + S], ACT.Copy, scale=vec(k, V_MIX + mix)).then_inc(s.mix_a, 1)
                product(0)
                for k in range(CT):
                    if k + 1 < CT:
                        product(k + 1)
                    act.wait_ge(s.mix_b, 8 * i + k + 1)
                    split_high(k, tmp[:, 2 + k % 2, :], None, free)

            mixes(0, MIX_W, None)
            mixes(1, MIX_A, 0)
            act.wait_ge(s.norm_rt, 1)
            act.wait_ge(s.h_ready, 8)
            A(rstd[0:64, :], pb[0][0:64, :], ACT.Tanh).then_inc(s.dense_a, 1)
            high(2, 0)
            mixes(2, MIX_G, 8 * 1)
            act.wait_ge(s.pe_step, 16)
            A(rstd[64:128, :], pb[2][64:128, :], ACT.Copy).then_inc(s.dense_a, 1)
            high(3, 1, slice(0, 1024))
            act.wait_ge(s.dense_a, 2)
            A(lora_h[:, 0, :], rstd[:, :], ACT.Copy).then_inc(s.lora_hi, 1)
            mixes(3, MIX_K, 8 * 2)
            high(4, 0)
            for m in range(2):
                act.wait_ge(s.lora_rdy, 1 + m)
                A(rstd[:, :], pb[m][:, :], ACT.Sigmoid).then_inc(s.dense_a, 1)
                act.wait_ge(s.dense_a, 3 + m)
                A(lora_h[:, 1 + m, :], rstd[:, :], ACT.Copy).then_inc(s.lora_hi, 1)
            for g in range(8):
                act.wait_ge(s.pe_step, 24 + g + 1)
                for m in range(2):
                    c = (2 * g + m) % 8
                    kind, bias = (LW, V_W0) if g < 4 else (A_, V_A0)
                    A(St[:, kind, c, :], pb[2 * (1 - g % 2) + m][:, :], ACT.Sigmoid, bias=vec(c, bias))\
                        .then_inc(s.dense_a, 1)
            high(5, 1)

            def prep_act(c):
                if c >= 2:
                    act.wait_ge(s.prep, c - 1)
                act.wait_ge(s.dense_a, 20 + c + 1)
                A(tmp[:, c % 2, :], St[:, K_, c, :], ACT.Square, scale=vec(c, V_KK)).then_inc(s.kk_sq, 1)
                act.wait_ge(s.g_cum, 2 * c + 2)
                A(prep_b[:, :], rstd[:, :], ACT.Exp, scale=KAPPA).then_inc(s.exps, 1)
                A(St[:, LW, c, :], prep_a[:, :], ACT.Exp, scale=-KAPPA).then_inc(s.exps, 1)
                A(St[:, R_, c, :], rstd[:, :], ACT.Exp, scale=-KAPPA).then_inc(s.exps, 1)
                A(gC[:, c * 8:(c + 1) * 8], rstd[:, CH - 1:S:CH], ACT.Exp, scale=-KAPPA).then_inc(s.exps, 1)
                act.wait_ge(s.kk_ps, c + 1)
                A(tmp[:, c % 2, :], pb[4 + c % 2][:, :], ACT.Sqrt, bias=eps_0).then_inc(s.kk_rt, 1)

            for t in range(12):
                n = N_K + t
                if t == 3:
                    mixes(4, MIX_R, 8 * (N_K + 3))
                if t == 7:
                    mixes(5, MIX_V, 8 * (N_R + 3))
                if t < 4 or t >= 8:
                    kind, c = (K_, 2 * t) if t < 4 else (V_, 2 * (t - 8))
                    act.wait_ge(s.pe_step, 8 * (n + 1))
                    for m in range(2):
                        A(St[:, kind, c + m, :], pb[2 * (1 - t % 2) + m][:, :], ACT.Copy).then_inc(s.dense_a, 1)
                if n + 2 < N_G2:
                    high(n + 2, t % 2)
                if t < 8:
                    prep_act(t)

            act.wait_ge(s.pe_step, 8 * N_G2)
            act.wait_ge(s.prep, CT)
            act.wait_ge(s.bd_zero, 6)
            act.wait_ge(s.set_zero, 8)
            act.wait_ge(s.dense_v, 8)

            def diag_copies(q):
                if q >= 1:
                    act.wait_ge(s.tr_mm, 3 * (q - 1) + 2)
                for dst, kind in ((Bbd, A_), (Kbd, K_)):
                    for h in range(2):
                        A(dst[64 * h:64 * h + 64, :, 64 * h:64 * h + 64],
                          St[64 * h:64 * h + 64, kind, q // 2, (q % 2) * QUAD * CH:(q % 2 + 1) * QUAD * CH]
                          .rearrange("p (u t) -> p u t", t=CH), ACT.Copy).then_inc(s.bd_a, 1)

            def flat(t):
                return t[:, :, :].rearrange("p u t -> p (u t)")

            def turned(q, i):
                act.wait_ge(s.tr_mm, 3 * q + i + 1)
                if q >= 3:
                    act.wait_ge(s.y_mm, 4 * (q - 2))
                A(flat(sets[q % 3][i]), pb[2][:, :], ACT.Copy).then_inc(s.tr_ev, 1)

            def inverse_t(q, lv):
                par, n = q % 2, q // 2
                act.wait_ge(s.tt_mm[par], 6 * n + lv + 1)
                bank = pb[4 + 2 * par]
                if lv < LEVELS - 1:
                    A(flat(TTst[par]), bank[:, 0:QUAD * CH], ACT.Copy).then_inc(s.tt_ev[par], 1)
                if 1 <= lv < LEVELS - 1:
                    act.wait_ge(s.t_mm[par], 4 * n + lv)
                for h in range(2):
                    r = slice(64 * h, 64 * h + 64)
                    A(sets[q % 3][6][r, :, r], bank[r, 0:QUAD * CH].rearrange("p (u t) -> p u t", t=CH), ACT.Copy)\
                        .then_inc(s.tt_ev[par], 1)

            def decayed(o, j):
                J = 4 * o + j
                if J % 8:
                    act.wait_ge(s.h_ev, J)
                    A(Hg[:, :], Hs[:, J % 2, :], ACT.Copy, scale=gC[:, (o // 2) * 8 + J % 8:(o // 2) * 8 + J % 8 + 1])\
                        .then_inc(s.hg, 1)

            def take_z(o, j):
                act.wait_ge(s.ch, 3 * (4 * o + j) + 1)
                A(Zs[:, :], pb[0][:, 0:P], ACT.Copy).then_inc(s.z_ev, 1)

            def take_u(o, j):
                J = 4 * o + j
                act.wait_ge(s.ch, 3 * J + 2)
                if J >= 1:
                    act.wait_ge(s.y_mm, J)
                A(Us[:, :], pb[0][:, 0:P], ACT.Copy).then_inc(s.z_ev, 1)

            diag_copies(0)
            for i in range(NQ + 2):
                a, b, o = i, i - 1, i - 2
                first, second, chain = a < NQ, 0 <= b < NQ, o >= 0
                if chain:
                    take_z(o, 0)
                    decayed(o, 0)
                    take_u(o, 0)
                if second:
                    inverse_t(b, 3)
                if first:
                    turned(a, 0)
                if chain:
                    take_z(o, 1)
                    decayed(o, 1)
                    take_u(o, 1)
                if second:
                    inverse_t(b, 4)
                if first:
                    turned(a, 1)
                    inverse_t(a, 0)
                if chain:
                    take_z(o, 2)
                    decayed(o, 2)
                    take_u(o, 2)
                if second:
                    inverse_t(b, 5)
                if first:
                    inverse_t(a, 1)
                if chain:
                    take_z(o, 3)
                    decayed(o, 3)
                if first:
                    turned(a, 2)
                if chain:
                    take_u(o, 3)
                if a + 1 < NQ:
                    diag_copies(a + 1)
                if first:
                    inverse_t(a, 2)
                if chain:
                    act.wait_ge(s.y_mm, 4 * (o + 1))
                    t0 = 4 + (o % 2) * QUAD * CH
                    A(X[:, o // 2, t0:t0 + QUAD * CH], pb[1][:, 0:QUAD * CH], ACT.Copy).then_inc(s.y_ev, 1)

            for t in range(TT):
                act.dma_start(xtok2[:, t, :], x[0, t * P:(t + 1) * P, :]).then_inc(s.x2_in, 16)
            for c in range(CT):
                act.wait_ge(s.mu_mm, c + 1)
                A(X[:, c, 4:4 + S], pb[c % 2][:, :], ACT.Copy).then_inc(s.yc_rdy, 1)
                if c >= 2:
                    act.wait_ge(s.gn_ps, c - 1)
                A(tmp[:, c % 2, :], pb[c % 2][:, :], ACT.Square).then_inc(s.gn_sq, 1)
                if c == 0:
                    high(N_G2, 0)
                if c == 4:
                    high(N_WO, 1)
            act.wait_ge(s.gn_ps, CT)
            A(rstd[0:16, :], pb[7][0:16, :], ACT.Sqrt, bias=eps_g[0:16, :], scale=1.0 / HD).then_inc(s.gn_rt, 1)
            act.wait_ge(s.pr_rdy, CT)
            for c in range(CT):
                act.wait_ge(s.x2_tr, c + 1)
                A(St[:, K_, c, :], pb[2 + c % 2][:, :], ACT.Copy).then_inc(s.x2_cp, 1)
                act.wait_ge(s.y_fin, c + 1)
                split_high(c, tmp[:, 2 + c % 2, :], None, None)

            squares = [0]

            def square(c, slot, src_sem, src_count):
                i = squares[0]
                squares[0] += 1
                act.wait_ge(src_sem, src_count)
                act.wait_ge(s.acc, 8 + i - 1)
                A(tmp[:, slot, :], X[:, c, 0:S], ACT.Square).then_inc(s.sq_rdy, 1)

            def proj(n0, ev0):
                for b in range(4):
                    if n0 == N_WO or b:
                        high(n0 + b + 1, (n0 + b + 1) % 2)
                    for m in range(2):
                        square(2 * b + m, m, s.dense_v, ev0 + 2 * b + m + 1)

            def splits(gain, free):
                for k in range(CT):
                    split_high(k, X[:, k, 0:S], vec(k, gain), free)

            def mlp(layer, n0, ev0):
                for half in range(2):
                    m0 = n0 + 16 * half
                    h0 = 32 * layer + 16 * half
                    with act.Fori(0, 4) as i:
                        for h in range(2):
                            high(m0 + 2 * i + h + 1, (m0 + h + 1) % 2)
                            for m in range(2):
                                act.wait_ge(s.hid_f, h0 + 4 * i + 2 * h + m + 1)
                                A(hid_h[:, bass.ds(4 * i + 2 * h + m, 1), :], tmp[:, 2 + m:3 + m, :], ACT.Copy)\
                                    .then_inc(s.hid_hi, 1)
                    m0 += 8
                    if half == 1:
                        for k in range(2):
                            act.wait_ge(s.p_tr, 2 * layer + k + 1)
                            A(lora_h[:, k, :], pb[5 + k][:, :], ACT.Copy).then_inc(s.p_hi, 1)
                    if half == 0:
                        with act.Fori(0, 4) as i:
                            for h in range(2):
                                high(m0 + 2 * i + h + 1, (m0 + h + 1) % 2)
                    else:
                        for b in range(8):
                            high(m0 + b + 1, (m0 + b + 1) % 2)
                            if b % 2:
                                for m in range(2):
                                    square(b - 1 + m, m, s.dense_v, ev0 + 40 + b + m)

            def ple(layer, n, gain, free, ni):
                splits(gain, free)
                high(n + 1, (n + 1) % 2)
                for m in range(CT):
                    act.wait_ge(s.pe_step, 8 * n + m + 1)
                    A(UP[:, m, :], pb[m % 4][:, :], ACT.Copy).then_inc(s.dense_a, 1)
                norm_root(ni)
                for b in range(4):
                    if n + 2 + b < N_ALL:
                        high(n + 2 + b, (n + b) % 2)
                    for m in range(2):
                        c = 2 * b + m
                        act.wait_ge(s.dense_v, 64 + 88 * layer + c + 1)
                        A(tmp[:, m, :], tmp[:, m, :], ACT.Sigmoid).then_inc(s.sig, 1)
                    if layer == 0:
                        for m in range(2):
                            square(2 * b + m, 2, s.upd, 2 * b + m + 1)

            proj(N_WO, 8)
            splits(V_N01, 8 * 20)
            norm_root(2)
            mlp(0, L_MLP[0], 16)
            ple(0, L_MLP[0] + 32, V_N02, 8 * (L_MLP[0] + 23), 3)

            act.wait_ge(s.upd, 8)
            act.dma_start(hot[:, :], consts[:, C_HOT:C_HOT + 640]).then_inc(s.hot_in, 16)
            act.dma_start(relb[0:BUCKETS, :], rel_bias).then_inc(s.rel_in, 16)

            splits(V_KV, 8 * 57)
            norm_root(4)

            def head_square(i):
                dst = KT if i < 8 else QT
                act.wait_ge(s.dense_v, 72 + i + 1 if i < 8 else 88 + i - 8 + 1)
                if i >= 2:
                    act.wait_ge(s.qk_n, i - 1)
                A(tmp[:, i % 2, :], dst[:, i % 8, :], ACT.Square).then_inc(s.qk_sq, 1)

            def head_root(i):
                act.wait_ge(s.qk_ps, i + 1)
                A(tmp[:, i % 2, :], pb[4 + i % 2][:, :], ACT.Sqrt, bias=eps_n, scale=1.0 / HD).then_inc(s.qk_rt, 1)

            def v_copy(i):
                act.wait_ge(s.v_tr, i + 1)
                A(VT[:, i, :, :].rearrange("p t v -> p (t v)"), pb[6 + i % 2][:, :], ACT.Copy).then_inc(s.v_ev, 1)

            for b in range(4):
                high(N_KS + b + 1, (b + 1) % 2)
                if b:
                    head_root(2 * b - 2)
                    head_root(2 * b - 1)
                head_square(2 * b)
                head_square(2 * b + 1)
            for b in range(4):
                high(N_VS + b + 1, (b + 1) % 2)
                if b:
                    v_copy(2 * b - 2)
                    v_copy(2 * b - 1)
                else:
                    head_root(6)
                    head_root(7)
            splits(V_N10, 8 * (N_VS + 3))
            for b in range(4):
                high(N_Q + b + 1, (b + 1) % 2)
                if b:
                    head_root(8 + 2 * b - 2)
                    head_root(8 + 2 * b - 1)
                else:
                    v_copy(6)
                    v_copy(7)
                head_square(8 + 2 * b)
                head_square(8 + 2 * b + 1)
            head_root(14)
            head_root(15)

            def exps(i):
                w = (i % 4 + 1) * P
                act.wait_ge(s.lg, 2 * i + 2)
                if i >= 2:
                    act.wait_ge(s.at_rdy, i - 1)
                for m in range(2):
                    k = 2 * (i % 2) + m
                    A(Pr[i % 2][:, m, 0:w], Lg[i % 2][:, m, 0:w], ACT.Exp, bias=st_n[:, k:k + 1], scale=-1.0,
                      accum_out=st_l[:, k:k + 1]).then_inc(s.pexp, 1)

            def attn_copy(i):
                w = (i % 4 + 1) * P
                act.wait_ge(s.at_tr, i + 1)
                if i >= 2:
                    act.wait_ge(s.o_mm, i - 1)
                A(ATt[:, i % 2, 0:w], pb[4][:, 0:w], ACT.Copy).then_inc(s.at_ev, 1)

            def head_take(h):
                act.wait_ge(s.o_mm, 4 * h + 4)
                A(QT[:, h, :], pb[5 + h % 2][:, :], ACT.Copy).then_inc(s.o_cp, 1)
                if h >= 2:
                    act.wait_ge(s.o_ps, h - 1)
                A(tmp[:, h % 2, :], pb[5 + h % 2][:, :], ACT.Square).then_inc(s.o_sq, 1)

            high(N_DO + 1, 1)
            act.wait_ge(s.qk_n, 16)
            for i in range(1, 32 + 4):
                if i - 1 < 32:
                    exps(i - 1)
                if 0 <= i - 3 < 32:
                    attn_copy(i - 3)
                if i >= 8 and i % 4 == 0:
                    head_take((i - 8) // 4)
            head_take(7)
            act.wait_ge(s.o_ps, 8)
            A(rstd[0:8, :], pb[7][0:8, :], ACT.Sqrt, bias=eps_n[0:8, :], scale=1.0 / P).then_inc(s.o_rt, 1)
            act.wait_ge(s.pe_step, 8 * N_DO)
            for h in range(8):
                act.wait_ge(s.o_f, h + 1)
                split_high(h, tmp[:, 2 + h % 2, :], None, None)
            proj(N_DO, 96)
            splits(V_N11, 8 * 73)
            norm_root(5)
            mlp(1, L_MLP[1], 104)
            ple(1, L_MLP[1] + 32, V_N12, 8 * (L_MLP[1] + 23), 6)
            for c in range(CT):
                act.wait_ge(s.fin_tr, c + 1)
                A(OT[:, :, c * P:(c + 1) * P], pb[4 + c % 4][:, :].rearrange("p (t d) -> p t d", d=P), ACT.Copy)\
                    .then_inc(s.fin_ev, 1)

        @block.vector
        def _(dve):
            link = Link(dve, s.vec_link)
            tt, stt, ts = dve.tensor_tensor, dve.scalar_tensor_tensor, dve.tensor_scalar

            dve.memset(eps_n, NORM_EPS).then_inc(s.vec_link, 1)
            dve.memset(eps_g, GN_EPS).then_inc(s.vec_link, 1)
            link.n = 2
            dve.wait_ge(s.vec_link, 2)
            dve.memset(eps_0, 0.0).then_inc(s.small_set, 1)
            link(dve.memset(X[:, :, 0:4], 0.0))
            dve.wait_ge(s.par_tr, 1)
            dve.tensor_copy(PV[:, :, :], pb[7][:, 0:CT * NV].rearrange("p (c v) -> p c v", v=NV)).then_inc(s.par_ev, 1)
            dve.tensor_copy(hv[:, 0:3], pb[7][:, CT * NV:CT * NV + 3]).then_inc(s.par_ev, 1)
            dve.wait_ge(s.par_ev, 2)
            link(ts(omka, PV[:, :, V_KA], -1.0, 1.0, ALU.mult, ALU.add))
            link(ts(omix3, PV[:, :, V_MIX:V_MIX + 6], -1.0, 1.0, ALU.mult, ALU.add))
            link(ts(qg8, hv[:, 1:2], HD ** -0.5, None, ALU.mult))
            link(ts(subg, hv[:, 2:3], 1.0 - LAMBDA_INIT, None, ALU.mult))

            link(dve.memset(one_col, 0.0))
            link(dve.memset(one_col[:, 8:9], 1.0))

            link(dve.memset(tmp[:, 3, :], 0.0))
            for c in range(CT):
                dve.wait_ge(s.xt_sq, c + 1)
                if c:
                    dve.wait_ge(s.acc, c)
                tt(tmp[:, 3, :], tmp[:, 3, :], tmp[:, c % 2, :], ALU.add).then_inc(s.acc, 1)
            dve.wait_ge(s.lam_in, 16)
            link(tt(lrow[:, 0:2, :], lrow[:, 0:4:2, :], lrow[:, 1:4:2, :], ALU.mult))
            dve.tensor_reduce(lamw[:, 0:2], lrow[:, 0:2, :], AX.X, ALU.add).then_inc(s.lam_s, 1)

            def norm_finish(i):
                dve.wait_ge(s.norm_rt, i)
                link(dve.reciprocal(rstd[:, :], rstd[:, :]))

            norm_finish(1)
            for c in range(CT):
                dve.wait_ge(s.xt_cp, c + 1)
                stt(X[:, c, 4:4 + S], X[:, c, 4:4 + S], vec(c, V_N00), rstd[:, :], ALU.mult, ALU.mult)\
                    .then_inc(s.h_ready, 1)
            dve.wait_ge(s.h_ready, 8)
            dve.wait_ge(s.lam_e, 1)
            link(tt(lamf, lamw[:, 2:3], lamw[:, 3:4], ALU.subtract))
            link(ts(lamf, lamf, LAMBDA_INIT, None, ALU.add))

            def low(k, src, n):
                dve.wait_ge(s.x_hi, n + 1)
                tt(xl[:, k, :], src, xh[:, k, :].bitcast(F32), ALU.subtract).then_inc(s.x_ready, 1)

            def mixes(i, mix, free):
                def mixed(k):
                    dve.wait_ge(s.mix_a, 8 * i + k + 1)
                    if 8 * i + k >= 2:
                        dve.wait_ge(s.x_ready, 8 * i + k - 1)
                    stt(tmp[:, 2 + k % 2, :], X[:, k, 4:4 + S], omix3[:, k, mix:mix + 1], pb[6 + k % 2][:, :],
                        ALU.mult, ALU.add).then_inc(s.mix_b, 1)
                if i == 0:
                    dve.wait_ge(s.norm_ps, 1)
                mixed(0)
                for k in range(CT):
                    if k + 1 < CT:
                        mixed(k + 1)
                    dve.wait_ge(s.mix_b, 8 * i + k + 1)
                    low(k, tmp[:, 2 + k % 2, :], 8 * i + k)

            def lora_low(k):
                dve.wait_ge(s.lora_hi, k + 1)
                tt(lora_l[:, k, :], rstd[:, :], lora_h[:, k, :].bitcast(F32), ALU.subtract).then_inc(s.lora_rdy, 1)

            mixes(0, MIX_W, None)
            mixes(1, MIX_A, None)
            mixes(2, MIX_G, None)
            lora_low(0)
            mixes(3, MIX_K, None)
            lora_low(1)
            lora_low(2)

            def prep(c):
                lw, r, k, a = (St[:, kind, c, :] for kind in (LW, R_, K_, A_))
                dve.wait_ge(s.dense_a, 20)
                if c == 0:
                    dve.wait_ge(s.lora_rdy, 3)
                if c:
                    dve.wait_ge(s.prep, c)
                    dve.wait_ge(s.exps, 4 * c)
                dve.tensor_tensor_scan(rstd[:, :], cst[:, C_SEG:C_SEG + S], lw, 0.0, ALU.mult, ALU.add).then_inc(s.g_cum, 1)
                dve.wait_ge(s.g_cum, 2 * c + 1)
                tt(prep_a[:, :], rstd[:, :], lw, ALU.subtract).then_inc(s.g_cum, 1)
                kn = tmp[:, c % 2, :]
                dve.wait_ge(s.kk_rt, c + 1)
                link(ts(kn, kn, 1e-12, None, ALU.max))
                link(dve.reciprocal(kn, kn))
                link(stt(kn, k, vec(c, V_KK), kn, ALU.mult, ALU.mult))
                dve.wait_ge(s.exps, 4 * c + 4)
                link(stt(lw, kn, -1.0, lw, ALU.mult, ALU.mult))
                link(ts(prep_a[:, :], a, vec(c, V_KA), omka[:, c:c + 1], ALU.mult, ALU.add))
                link.mark(tt(k, k, prep_a[:, :], ALU.mult))
                link(tt(a, a, kn, ALU.mult))
                link.mark(tt(a, a, prep_b[:, :], ALU.mult))
                tt(k, k, prep_b[:, :], ALU.mult).then_inc(s.prep, 1)

            def r_tiles(b):
                dve.wait_ge(s.pe_step, 8 * (N_R + b + 1))
                for m in range(2):
                    c = 2 * b + m
                    dve.wait_ge(s.exps, 4 * c + 3)
                    tt(St[:, R_, c, :], St[:, R_, c, :], pb[2 * (1 - b % 2) + m][:, :], ALU.mult).then_inc(s.dense_v, 1)

            for t in range(12):
                if t == 3:
                    mixes(4, MIX_R, None)
                if t == 7:
                    mixes(5, MIX_V, None)
                if t < 8:
                    prep(t)
                if 4 <= t < 7:
                    r_tiles(t - 4)
                if t == 8:
                    r_tiles(3)
            dve.wait_ge(s.prep, 8)
            dve.wait_ge(s.vec_link, link.n)

            dve.wait_ge(s.pe_step, 8 * N_G2)
            for t in (MnT[0], MnT[1], *(sets[k][i] for k in range(3) for i in (3, 6))):
                dve.memset(t[:, :, :], 0.0).then_inc(s.set_zero, 1)
            dve.wait_ge(s.set_zero, 8)
            dve.wait_ge(s.inv_in, 16)
            tri = cst[:, C_TRS:C_TRS + CH]
            tri_in = cst[:, C_TRS + CH:C_TRS + 2 * CH]

            def scored(q, i):
                dve.wait_ge(s.sc_mm, 2 * q + i + 1)
                if q >= 3:
                    dve.wait_ge(s.y_mm, 4 * (q - 2))
                sets_q = sets[q % 3]
                bd, st = (MnT[q % 2], sets_q[4]) if i == 0 else (sets_q[3], sets_q[5])
                bank = pb[3 + 2 * (q % 2) + i][:, :].rearrange("p (u t) -> p u t", t=P)
                for h in range(2):
                    r = slice(64 * h, 64 * h + 64)
                    tt(bd[r, :, r], bank[r, :, 0:CH], tri[r, None, :].to_broadcast([64, QUAD, CH]), ALU.mult)\
                        .then_inc(s.sc_ev, 1)
                tt(st[:, :, :], bank[:, :, CH:P], tri_in[:, None, :].to_broadcast([P, QUAD, CH]), ALU.mult)\
                    .then_inc(s.sc_ev, 1)

            def masked_p(q, lv):
                par, n = q % 2, q // 2
                dve.wait_ge(s.p_mm[par], 6 * n + lv + 1)
                p_ = pb[3 + 2 * par][:, 0:QUAD * CH].rearrange("p (u t) -> p u t", t=CH)
                tt(Pbd[par][:, :, :].rearrange("p u (h t) -> p u h t", h=2),
                   p_[:, :, None, :].to_broadcast([P, QUAD, 2, CH]),
                   cst[:, None, C_LVL + lv * P:C_LVL + (lv + 1) * P].rearrange("p o (h t) -> p o h t", h=2)
                   .to_broadcast([P, QUAD, 2, CH]), ALU.mult).then_inc(s.p_ev[par], 1)
                tt(Pst[par][:, :, :], p_,
                   inv_c[:, None, lv * CH:(lv + 1) * CH].to_broadcast([P, QUAD, CH]), ALU.mult)\
                    .then_inc(s.p_ev[par], 1)

            def inverse(q, lv):
                par, n = q % 2, q // 2
                dve.wait_ge(s.t_mm[par], 4 * n + lv)
                dve.tensor_copy(Tst[par][:, :, :].rearrange("p u t -> p (u t)"), pb[3 + 2 * par][:, QUAD * CH:2 * QUAD * CH])\
                    .then_inc(s.t_ev[par], 1)

            def state(o, j):
                J = 4 * o + j
                dve.wait_ge(s.ch, 3 * J + 3)
                if J:
                    dve.wait_ge(s.y_mm, J)
                g = gC[:, (o // 2) * 8 + J % 8:(o // 2) * 8 + J % 8 + 1]
                if J % 8 == 0:
                    ts(Hs[:, (J + 1) % 2, :], pb[0][:, 0:P], g, None, ALU.mult).then_inc(s.h_ev, 1)
                else:
                    dve.wait_ge(s.hg, J - J // 8)
                    stt(Hs[:, (J + 1) % 2, :], pb[0][:, 0:P], g, Hg[:, :], ALU.mult, ALU.add).then_inc(s.h_ev, 1)

            for i in range(NQ + 2):
                a, b, o = i, i - 1, i - 2
                first, second, chain = a < NQ, 0 <= b < NQ, o >= 0
                if first:
                    scored(a, 0)
                if second:
                    masked_p(b, 3)
                if first:
                    scored(a, 1)
                if second:
                    inverse(b, 3)
                if chain:
                    state(o, 0)
                if second:
                    masked_p(b, 4)
                if first:
                    masked_p(a, 0)
                if second:
                    inverse(b, 4)
                if chain:
                    state(o, 1)
                if second:
                    masked_p(b, 5)
                if first:
                    masked_p(a, 1)
                if chain:
                    state(o, 2)
                if first:
                    inverse(a, 1)
                    masked_p(a, 2)
                    inverse(a, 2)
                if chain:
                    state(o, 3)

            def bonus_product(c):
                if c >= 2:
                    dve.wait_ge(s.bon_ps, c - 1)
                stt(tmp[:, 2 + c % 2, :], St[:, R_, c, :], vec(c, V_RK), St[:, K_, c, :], ALU.mult, ALU.mult)\
                    .then_inc(s.pr_rdy, 1)

            dve.wait_ge(s.tr_mm, 3 * NQ)
            dve.wait_ge(s.y_mm, 4 * NQ)
            bonus_product(0)
            for c in range(CT):
                if c + 1 < CT:
                    bonus_product(c + 1)
                dve.wait_ge(s.bon_ps, c + 1)
                tt(St[:, V_, c, :], St[:, V_, c, :], pb[2 + c % 2][:, :], ALU.mult).then_inc(s.bon_v, 1)
            dve.wait_ge(s.gn_rt, 1)
            dve.reciprocal(rstd[0:16, :], rstd[0:16, :]).then_inc(s.gn_rs, 1)
            dve.wait_ge(s.yc_rdy, CT)
            dve.wait_ge(s.bon_v, CT)
            for c in range(CT):
                t = tmp[:, c % 2, :]
                dve.wait_ge(s.rb_ps, c + 1)
                if c >= 2:
                    dve.wait_ge(s.y_fin, c - 1)
                link(stt(t, X[:, c, 4:4 + S], vec(c, V_LNW), pb[4 + c % 2][:, :], ALU.mult, ALU.mult))
                link(stt(t, t, vec(c, V_LNB), St[:, V_, c, :], ALU.add, ALU.add))
                dve.wait_ge(s.pe_step, 8 * N_G2 + c + 1)
                if c >= 2:
                    dve.wait_ge(s.x_hi, X_Y + c - 1)
                    dve.wait_ge(s.x_ready, X_Y + c - 1)
                tt(tmp[:, 2 + c % 2, :], t, pb[6 + c % 2][:, :], ALU.mult).then_inc(s.y_fin, 1)
                if c:
                    low(c - 1, tmp[:, 2 + (c - 1) % 2, :], X_Y + c - 1)
            dve.wait_ge(s.y_fin, CT)
            low(CT - 1, tmp[:, 3, :], X_Y + CT - 1)

            squares = [0]

            def clear_acc(i):
                dve.wait_ge(s.norm_ps, i - 1)
                link(dve.memset(tmp[:, 3, :], 0.0))

            def add_square(slot):
                i = squares[0]
                squares[0] += 1
                dve.wait_ge(s.sq_rdy, i + 1)
                dve.wait_ge(s.acc, 8 + i)
                tt(tmp[:, 3, :], tmp[:, 3, :], tmp[:, slot, :], ALU.add).then_inc(s.acc, 1)

            def residual(c, b, sem=s.dense_v, old=None):
                tt(X[:, c, 0:S], X[:, c, 0:S] if old is None else old, b, ALU.add).then_inc(sem, 1)

            def proj(n0, i):
                dve.wait_ge(s.x_ready, (X_Y if i == 2 else X_O) + CT)
                clear_acc(i)
                for b in range(4):
                    dve.wait_ge(s.pe_step, 8 * (n0 + b + 1))
                    for m in range(2):
                        residual(2 * b + m, pb[2 * (b % 2) + m][:, :], old=St[:, K_, 2 * b + m, :] if i == 2 else None)
                    for m in range(2):
                        add_square(m)

            def splits(gain, base):
                for k in range(CT):
                    dve.wait_ge(s.x_hi, base + k + 1)
                    stt(xl[:, k, :], X[:, k, 0:S], vec(k, gain), xh[:, k, :].bitcast(F32), ALU.mult, ALU.subtract)\
                        .then_inc(s.x_ready, 1)

            def mlp(layer, n0, ev0):
                for half in range(2):
                    m0 = n0 + 16 * half
                    e = ev0 + 24 * half
                    h0 = 32 * layer + 16 * half
                    with dve.Fori(0, 4) as i:
                        for h in range(2):
                            done = 4 * i + 2 * h
                            dve.wait_ge(s.pe_step, 8 * (m0 + 2 * i + h + 1))
                            for m in range(2):
                                tt(tmp[:, m, :], pb[2 * h + m][:, :], rstd[:, :], ALU.mult).then_inc(s.dense_v, 1)
                            dve.wait_ge(s.hid_rdy, h0 + done)
                            for m in range(2):
                                dve.wait_ge(s.dense_v, e + done + m + 1)
                                stt(tmp[:, 2 + m, :], tmp[:, m, :], 0.0, tmp[:, m, :], ALU.max, ALU.mult)\
                                    .then_inc(s.hid_f, 1)
                            for m in range(2):
                                dve.wait_ge(s.hid_hi, h0 + done + m + 1)
                                tt(hid_l[:, bass.ds(done + m, 1), :], tmp[:, 2 + m:3 + m, :],
                                   hid_h[:, bass.ds(done + m, 1), :].bitcast(F32), ALU.subtract).then_inc(s.hid_rdy, 1)
                    m0 += 8
                    e += 16
                    if half == 1:
                        for k in range(2):
                            dve.wait_ge(s.p_hi, 2 * layer + k + 1)
                            tt(lora_l[:, k, :], pb[5 + k][:, :], lora_h[:, k, :].bitcast(F32), ALU.subtract).then_inc(s.p_rdy, 1)
                        dve.wait_ge(s.hid_rdy, h0 + 16)
                        clear_acc(3 + 3 * layer)
                    for g in range(4):
                        dve.wait_ge(s.pe_step, 8 * (m0 + 2 * g + 2))
                        for m in range(2):
                            residual(2 * g + m, pb[2 * (g % 2) + m][:, :])
                        if half == 1:
                            for m in range(2):
                                add_square(m)

            def ple(layer, n, gain, base, ni):
                splits(gain, base)
                norm_finish(ni)
                if layer == 0:
                    clear_acc(4)
                for b in range(4):
                    dve.wait_ge(s.pe_step, 8 * (n + 2 + b))
                    for m in range(2):
                        tt(tmp[:, m, :], pb[2 * (b % 2) + m][:, :], rstd[:, :], ALU.mult).then_inc(s.dense_v, 1)
                    for m in range(2):
                        c = 2 * b + m
                        dve.wait_ge(s.sig, 8 * layer + c + 1)
                        dve.wait_ge(s.dense_a, 36 + 8 * layer + c + 1)
                        link(tt(tmp[:, m, :], tmp[:, m, :], UP[:, c, :], ALU.mult))
                        residual(c, tmp[:, m, :], s.upd)
                        if layer == 0:
                            add_square(2)
                    dve.wait_ge(s.upd, 8 * layer + 2 * b + 2)

            dve.wait_ge(s.x2_cp, 8)
            proj(N_WO, 2)
            splits(V_N01, X_M0)
            norm_finish(2)
            mlp(0, L_MLP[0], 16)
            ple(0, L_MLP[0] + 32, V_N02, X_P0, 3)
            splits(V_KV, X_KV)
            norm_finish(4)
            dve.memset(relb[BUCKETS:BUCKETS + 1, :], NEG).then_inc(s.far_row, 1)
            dve.wait_ge(s.bv_mm, 1)
            dve.tensor_copy(bvec[:, 0:S], pb[5][0:8, 0:S]).then_inc(s.bv_ev, 1)
            dve.tensor_copy(bvec[:, S:640], pb[6][0:8, 0:128]).then_inc(s.bv_ev, 1)

            def head_norm(i):
                dst = (KT if i < 8 else QT)[:, i % 8, :]
                dve.wait_ge(s.qk_rt, i + 1)
                link(dve.reciprocal(tmp[:, i % 2, :], tmp[:, i % 2, :]))
                stt(dst, dst, hv[:, 0:1] if i < 8 else qg8, tmp[:, i % 2, :], ALU.mult, ALU.mult).then_inc(s.qk_n, 1)

            def times_rstd(n, b, dsts, sem=s.dense_v):
                dve.wait_ge(s.pe_step, 8 * (n + 1))
                for m in range(2):
                    tt(dsts[m], pb[2 * (b % 2) + m][:, :], rstd[:, :], ALU.mult).then_inc(sem, 1)

            for b in range(4):
                if b:
                    head_norm(2 * b - 2)
                    head_norm(2 * b - 1)
                times_rstd(N_KS + b, b, [KT[:, 2 * b + m, :] for m in range(2)])
            for b in range(4):
                if b == 0:
                    head_norm(6)
                    head_norm(7)
                else:
                    dve.wait_ge(s.v_tr, 2 * b)
                dve.wait_ge(s.pe_step, 8 * (N_VS + b + 1))
                for m in range(2):
                    tt(tmp[:, 2 + m, :], pb[2 * (b % 2) + m][:, :], rstd[:, :], ALU.mult).then_inc(s.dense_v, 1)
            splits(V_N10, X_Q)
            for b in range(4):
                if b:
                    head_norm(8 + 2 * b - 2)
                    head_norm(8 + 2 * b - 1)
                times_rstd(N_Q + b, b, [QT[:, 2 * b + m, :] for m in range(2)])
            head_norm(14)
            head_norm(15)
            dve.wait_ge(s.strip_in, 128)
            dve.wait_ge(s.qk_n, 16)

            def logits(i):
                h, w = i // 4, (i % 4 + 1) * P
                if i >= 2:
                    dve.wait_ge(s.pexp, 2 * (i - 1))
                bias = strip[:, h, 0:w]
                bias = bass.AP(bias.tensor, bias.offset + w - 1, [bias.ap[0], [-1, w]])
                for m in range(2):
                    k = 2 * (i % 2) + m
                    dve.wait_ge(s.s_mm, 2 * i + m + 1)
                    dve.tensor_tensor_reduce(out=Lg[i % 2][:, m, 0:w], in0=pb[2 * (i % 2) + m][:, 0:w], in1=bias,
                                             scale=-1.0, scalar=3.0e38, op0=ALU.add, op1=ALU.min,
                                             accum_out=st_n[:, k:k + 1]).then_inc(s.lg, 1)

            def combine(i):
                w, k, pr = (i % 4 + 1) * P, 2 * (i % 2), Pr[i % 2]
                dve.wait_ge(s.scaled, i + 1)
                dve.wait_ge(s.rec, i + 1)
                if i >= 2:
                    dve.wait_ge(s.at_tr, i - 1)
                stt(At[:, i % 2, 0:w], pr[:, 0, 0:w], st_r[:, k:k + 1], pr[:, 1, 0:w], ALU.mult, ALU.subtract)\
                    .then_inc(s.at_rdy, 1)

            def invert_sums(i):
                k = 2 * (i % 2)
                dve.wait_ge(s.pexp, 2 * i + 2)
                dve.reciprocal(st_r[:, k:k + 2], st_l[:, k:k + 2]).then_inc(s.rec, 1)

            for i in range(32 + 2):
                if i < 32:
                    logits(i)
                if i >= 2:
                    combine(i - 2)
                if 1 <= i <= 32:
                    invert_sums(i - 1)
            dve.wait_ge(s.o_rt, 1)
            dve.reciprocal(rstd[0:8, :], rstd[0:8, :]).then_inc(s.o_rs, 1)
            for h in range(8):
                dve.wait_ge(s.ob_ps, h + 1)
                if h == 0:
                    dve.wait_ge(s.o_cp, 8)
                if h >= 2:
                    dve.wait_ge(s.x_ready, X_O + h - 1)
                stt(tmp[:, 2 + h % 2, :], QT[:, h, :], subg, pb[4 + h % 4][:, :], ALU.mult, ALU.mult).then_inc(s.o_f, 1)
                if h:
                    low(h - 1, tmp[:, 2 + (h - 1) % 2, :], X_O + h - 1)
            dve.wait_ge(s.o_f, 8)
            low(7, tmp[:, 3, :], X_O + 7)
            proj(N_DO, 5)
            splits(V_N11, X_M1)
            norm_finish(5)
            mlp(1, L_MLP[1], 104)
            ple(1, L_MLP[1] + 32, V_N12, X_P1, 6)


_INS = ["x", "p", "norm_g", "mlp_w1", "mlp_w2", "ple_w_up", "ple_w_gate", "rwkv_mix", "rwkv_w_rkvo", "rwkv_w0",
        "rwkv_w1", "rwkv_w2", "rwkv_a0", "rwkv_a1", "rwkv_a2", "rwkv_g1", "rwkv_g2", "rwkv_k_k", "rwkv_k_a",
        "rwkv_r_k", "rwkv_ln_w", "rwkv_ln_b", "kv_norm_g", "w_k_shared", "w_v_shared", "k_norm_g", "diff_w_q",
        "diff_q_norm_g", "diff_lam", "diff_subln_g", "diff_w_o", "rel_bias"]


def build(nc, shapes):
    args = [nc.dram_tensor(f"in_{n}_dram", shape, F32, kind="ExternalInput").ap() for n, shape in shapes]
    out = nc.dram_tensor("out_0_dram", (1, S, D), F32, kind="ExternalOutput").ap()
    trunk(nc, *args, out)


def kernel(**inputs):
    import numpy as _np
    import concourse.bacc as _bacc
    from concourse.bass_utils import run_bass_kernel_spmd as _run

    nc = _bacc.Bacc("TRN2", target_bir_lowering=False, num_devices=1)
    arrays = {f"in_{n}_dram": _np.ascontiguousarray(inputs[n]) for n in _INS}
    arrays["in_consts_dram"] = shape_constants()
    build(nc, [(n, arrays[f"in_{n}_dram"].shape) for n in _INS + ["consts"]])
    r = _run(nc, [arrays], core_ids=[0])
    return r.results[0]["out_0_dram"]
```

```python
import math
from contextlib import ExitStack

import numpy as np

import concourse.bass as bass
from concourse import mybir

F32 = mybir.dt.float32
F32R = mybir.dt.float32r
ALU = mybir.AluOpType
ACT = mybir.ActivationFunctionType
AX = mybir.AxisListType

P = 128
D = 1024
S = 512
CT = D // P
TT = S // P
FF = 4 * D
PLE = 256
HD = 64
CH = 64
QUAD = 4
NQ = CT * S // (CH * QUAD)
LEVELS = 6
BUCKETS, MAX_DIST = 32, 128
LAMBDA_INIT = 0.8 - 0.6 * math.exp(-0.3)
KAPPA = math.exp(-0.5)
NEG = -1.0e30
NORM_EPS, GN_EPS = 1e-6, 64e-5

(V_N00, V_N01, V_N02, V_N10, V_N11, V_N12, V_KV, V_MIX, _1, _2, _3, _4, _5,
 V_W0, V_A0, V_KK, V_KA, V_LNW, V_LNB, V_RK) = range(20)
NV = 20
MIX_R, MIX_W, MIX_K, MIX_V, MIX_A, MIX_G = range(6)

C_ID, C_BONES, C_ONES = 0, 128, 256
C_LVL = 384
C_TRS = C_LVL + LEVELS * P
C_EX2 = C_TRS + 2 * CH
C_IDS = C_EX2 + P
C_SEG = C_IDS + CH
C_END = C_SEG + S
C_CEN = C_END
C_SEL = C_CEN + P
C_EXP = C_SEL + 32
C_HOT = C_EXP + D
C_ALL = C_HOT + 640


def shape_constants():
    c = np.zeros((P, C_ALL), np.float32)
    i = np.arange(P)
    c[:, C_ID:C_ID + P] = np.eye(P)
    c[:, C_BONES:C_BONES + P] = (i[:, None] // HD) == (i[None, :] // HD)
    c[:, C_ONES:C_ONES + P] = 1
    for lv in range(LEVELS):
        b = 1 << lv
        low = ((i[:, None] // (2 * b)) == (i[None, :] // (2 * b))) & ((i[:, None] // b) % 2 == 1) & ((i[None, :] // b) % 2 == 0)
        c[:, C_LVL + lv * P:C_LVL + (lv + 1) * P] = low.T - np.eye(P)
    s, t = (i % CH)[:, None], np.arange(CH)[None, :]
    c[:, C_IDS:C_IDS + CH] = s == t
    c[:, C_TRS:C_TRS + CH] = s < t
    c[:, C_TRS + CH:C_TRS + 2 * CH] = s <= t
    c[:, C_SEG:C_SEG + S] = (np.arange(S) % CH != 0)[None, :]
    c[::32, C_EX2:C_EX2 + HD] = 1
    c[16::32, C_EX2 + HD:C_EX2 + P] = 1
    c[:, C_CEN:C_CEN + P] = np.eye(P) - ((i[:, None] // HD) == (i[None, :] // HD)) / HD
    c[i, C_SEL + 14 + i // HD] = 1
    for h in range(D // HD):
        c[h, C_EXP + h * HD:C_EXP + (h + 1) * HD] = 1
    for x in range(640):
        n = x - (P - 1)
        if n < 0:
            c[BUCKETS, C_HOT + x] = 1
            continue
        b = n
        if n >= BUCKETS // 2:
            b = BUCKETS // 2 + int(math.log(n / (BUCKETS // 2)) / math.log(MAX_DIST / (BUCKETS // 2)) * (BUCKETS // 2) + 1e-9)
        c[min(b, BUCKETS - 1), C_HOT + x] = 1
    return c


class Link:

    def __init__(self, eng, sem):
        self.eng, self.sem, self.n = eng, sem, 0

    def mark(self, ins):
        ins.then_inc(self.sem, 1)
        self.n = self.n + 1

    def wait(self):
        self.eng.wait_ge(self.sem, self.n)

    def __call__(self, ins):
        self.mark(ins)
        self.wait()


N_W1, N_A1, N_G1, N_WA2, N_K, N_R, N_V, N_G2, N_WO = 0, 1, 2, 3, 4, 8, 12, 16, 17
L_MLP = (21, 74)
N_KS, N_VS, N_Q, N_DO = 58, 62, 66, 70
N_ALL = 111
X_W, X_A, X_G, X_K, X_R, X_V, X_Y, X_M0, X_P0, X_KV, X_Q, X_O, X_M1, X_P1 = (8 * i for i in range(14))


def trunk(nc, x, p, norm_g, mlp_w1, mlp_w2, ple_w_up, ple_w_gate, rwkv_mix, rwkv_w_rkvo, rwkv_w0, rwkv_w1,
          rwkv_w2, rwkv_a0, rwkv_a1, rwkv_a2, rwkv_g1, rwkv_g2, rwkv_k_k, rwkv_k_a, rwkv_r_k, rwkv_ln_w,
          rwkv_ln_b, kv_norm_g, w_k_shared, w_v_shared, k_norm_g, diff_w_q, diff_q_norm_g, diff_lam,
          diff_subln_g, diff_w_o, rel_bias, consts, out):
    bias_rows = nc.dram_tensor("bias_rows", [8, 640], F32, kind="Internal").ap()
    ctx = ExitStack()
    with ctx:
        slab_bytes = 212800
        base = (nc.sbuf_base + 31) // 32 * 32
        ctx.enter_context(nc.sbuf_tensor("slab", [P, (slab_bytes + 32) // 4], F32))

        def at(name, offset, shape, dtype=F32):
            size = int(np.prod(shape[1:])) * 4
            assert offset + size <= slab_bytes, (name, offset, size)
            return nc.alloc_sbuf_tensor_at(name, shape, dtype, offset=base + offset)

        W_RAW, W_HI, W_LO, XH, XL, XX = 0, 16384, 32768, 49152, 65536, 81920
        ST, HIDH, HIDL, RSTD, TMP, CST = 98432, 180352, 186496, 192640, 194688, 202880
        wraw = at("wraw", W_RAW, [P, 2, 2048])
        whi = at("whi", W_HI, [P, 2, 2048], F32R)
        wlo = at("wlo", W_LO, [P, 2, 2048], F32R)
        xh = at("xh", XH, [P, CT, S], F32R)
        xl = at("xl", XL, [P, CT, S], F32R)
        X = at("X", XX, [P, CT, S + 4])
        lora_h = at("lora_h", HIDH, [P, 3, S], F32R)
        lora_l = at("lora_l", HIDL, [P, 3, S], F32R)
        rate_h = at("rate_h", ST + 2 * 16384 + 4 * 2048, [P, S], F32R)
        rate_l = at("rate_l", ST + 2 * 16384 + 5 * 2048, [P, S], F32R)
        rstd = at("rstd", RSTD, [P, S])
        tmp = at("tmp", TMP, [P, 4, S])
        cst = at("cst", CST, [P, C_END])
        PV = at("PV", CST + 4 * C_END, [P, CT, NV])
        small = at("small", CST + 4 * C_END + 4 * CT * NV, [P, 224])
        x_ss, x_rms = small[:, 4:8], small[:, 112:116]
        hv = small[:, 0:4]
        omka = small[:, 12:20]
        gC = small[:, 20:84]
        eps_n, eps_g, eps_0 = small[:, 84:85], small[:, 85:86], small[:, 86:87]
        lamf = small[:, 87:88]
        st_n, st_l, st_r = (small[:, 88 + 4 * k:92 + 4 * k] for k in (1, 2, 3))
        lamw = small[:, 108:112]
        subg = small[:, 160:161]
        qk_gain = small[:, 161:162]
        one_col = small[:, 162:178]

        St = at("St", ST, [P, 5, CT, S])
        LW, R_, K_, A_, V_ = range(5)
        xtok = at("xtok", ST + 2 * 16384, [P, TT, D])
        vrows = at("vrows", ST + 3 * 16384, [NV, D])
        hrows = at("hrows", ST + 3 * 16384 + 4096, [3, P])
        xtok2 = at("xtok2", ST, [P, TT, D])
        gn_c = at("gn_c", ST + 3 * 16384, [P, C_HOT - C_CEN])
        centre, head_sel, head_exp = gn_c[:, 0:P], gn_c[:, P:P + 32], gn_c[:, P + 32:]
        prep_a = at("prep_a", HIDH, [P, S])
        prep_b = at("prep_b", HIDL, [P, S])
        sets = [[at(f"{n}{k}", W_HI + 14336 * k + o, [P, QUAD, w]) for n, o, w in (
            ("Btok", 0, P), ("Ktok", 2048, P), ("Vtok", 4096, P), ("LakT", 6144, P), ("LrbT", 8192, CH),
            ("LrkT", 9216, CH), ("TiT", 10240, P), ("Abd", 12288, P))] for k in range(3)]
        INV = W_HI + 3 * 14336
        Wq, PT, Pb = ([at(f"{n}{k}", INV + 6144 * k + o, [P, QUAD, P]) for k in range(2)]
                      for n, o in (("Wq", 0), ("PT", 2048), ("Pb", 4096)))
        CHN = INV + 2 * 6144
        Hs = at("Hs", CHN, [P, 2, P])
        Zs = at("Zs", CHN + 1024, [P, P])
        Us = at("Us", CHN + 1536, [P, P])
        Hg = at("Hg", CHN + 2048, [P, P])
        Bbd = at("Bbd", TMP, [P, QUAD, P])
        Kbd = at("Kbd", TMP + 2048, [P, QUAD, P])
        Vbd = at("Vbd", TMP + 4096, [P, QUAD, P])
        hid_h = at("hid_h", ST, [P, 16, S], F32R)
        hid_l = at("hid_l", ST + 32768, [P, 16, S], F32R)
        UP = at("UP", ST + 65536, [P, CT, S])
        ptok = at("ptok", ST + 65536, [P, TT, PLE])
        KT = at("KT", ST, [P, CT, S])
        QZ = [at("QZ0", ST + 16384, [P, CT, S]), at("QZ1", ST + 65536, [P, CT, S])]
        VT = at("VT", ST + 32768, [P, CT, TT, P])
        strip = at("strip", ST + 49152, [P, 8, S])
        Lg = [at("Lg0", XH, [P, 2, S]), at("Lg1", HIDL, [P, 2, S])]
        Pr = [at("Pr0", XH + 4096, [P, 2, S]), at("Pr1", HIDH, [P, 2, S])]
        At = at("At", XH + 8192, [P, 2, S])
        ATt = at("ATt", XH + 12288, [P, 2, S])
        hot = at("hot", ST + 32768, [P, 640])
        relb = at("relb", ST + 32768 + 2560, [P, 8])
        bvec = at("bvec", ST + 32768 + 2624, [8, 640])
        lrow = at("lrow", HIDH + 4096, [P, 4, HD])
        q_last = [at("q14", HIDH + 4096, [P, S]), at("q15", HIDL + 4096, [P, S])]
        OT = at("OT", ST, [P, TT, D])

        pb = [ctx.enter_context(nc.psum_tensor(f"pb{i}", [P, S], F32)) for i in range(8)]

        ident = cst[:, C_ID:C_ID + P]
        ex2 = cst[:, C_EX2:C_EX2 + P]
        bones = cst[:, C_BONES:C_BONES + P]
        ones = cst[:, C_ONES:C_ONES + P]

        id_st = cst[:, None, C_IDS:C_IDS + CH].to_broadcast([P, QUAD, CH])

        names = """gnc_in raw0 raw1 w_hi w_lo pe_step cst_in cst2_in x_in0 x_in1 x_in2 x_in3 rows_in hrows_in x2_in p_in lam_in hot_in
            rel_in bvec_out strip_in out_st x_tr x_sq x_rt x_rs x_dg dx par_tr par_ev small_set gains lam_s lam_e
            h_ready x_edge mix_b x_hi x_ready acc norm_ps norm_rt dense_a dense_v act_link vec_link pool_link
            lora_hi lora_rdy g_cum dec exps kk_sq kk_ps kk_rt kk_rs kb_ps kn prep
            bd_a bd_p bd_zero set_zero sc_mm sc_ev mn_rdy tr_mm tr_ev pt_ev0 pt_ev1 pt_tr0 pt_tr1 pb_ev0 pb_ev1
            w_mm0 w_mm1 w_ev0 w_ev1 tt_ev0 tt_ev1 ch z_ev h_ev hg y_mm y_ev
            mu_mm yc_rdy gn_sq gn_ps gn_rt gn_rs rows_0 rb_ps pr_rdy bon_ps bon_v y_fin x2_tr x2_cp
            hid_f hid_hi hid_rdy sq_rdy p_tr p_hi p_rdy sig upd far_row bv_mm bv_ev
            qk_sq qk_ps qk_rt qk_rs qk_n q_ps q1_n q1_zero q0_zero v_tr v_ev s_mm lg pexp rec scaled at_rdy at_tr at_ev o_mm o_cp o_sq o_ps o_rt o_rs ob_ps o_f
            fin_tr fin_ev""".split()
        sem = {n: ctx.enter_context(nc.semaphore(n)) for n in names}
        s = type("Sems", (), sem)
        s.x_in = [sem[f"x_in{t}"] for t in range(TT)]
        s.pt_ev, s.pt_tr, s.pb_ev, s.w_mm, s.w_ev, s.tt_ev = (
            (sem[n + "0"], sem[n + "1"]) for n in ("pt_ev", "pt_tr", "pb_ev", "w_mm", "w_ev", "tt_ev"))

        def vec(c, v):
            return PV[:, c, v:v + 1]

        def block_rows(w, m2):
            return w.rearrange("(k p) n -> p k n", p=P)[:, :, bass.ds(m2 * 256, 256)]

        block = ctx.enter_context(nc.Block())

        def set_of(q):
            return sets[(q + 2) % 3]

        def q_raw(i):
            return tmp[:, 2 + i % 2, :] if i < 14 else q_last[i - 14][:, :]

        def mix_place(i, k):
            return k % 4 if i != 4 else 2 + k % 2

        @block.sync
        def _(sp):
            for t in range(TT):
                sp.dma_start(xtok[:, t, :], x[0, t * P:(t + 1) * P, :]).then_inc(s.x_in[t], 16)
            raw = (s.raw0, s.raw1)

            def slot_free(n):
                sp.wait_ge(s.w_lo, n - 1)

            def load(n, par, parts):
                for dst, src in parts:
                    sp.dma_start(dst, src).then_inc(raw[par], 16)

            r0 = wraw[:, 0, :]
            r1 = wraw[:, 1, :]

            def cols(r, w, k=CT):
                return r[:, 0:k * w].rearrange("p (k n) -> p k n", n=w)
            w1v = rwkv_w1[0].rearrange("(k p) n -> p k n", p=P)
            a1v = rwkv_a1[0].rearrange("(k p) n -> p k n", p=P)
            g1v = rwkv_g1[0].rearrange("(k p) n -> p k n", p=P)
            load(0, 0, [(cols(r0, P)[:, :, 0:64], w1v), (cols(r0, P)[:, :, 64:128], w1v)])
            load(1, 1, [(cols(r1, P)[:, :, 0:64], a1v), (cols(r1, P)[:, :, 64:128], a1v)])
            slot_free(2)
            load(2, 0, [(cols(r0, 256)[:, :, 0:128], g1v[:, :, 0:128]),
                        (cols(r0, 256)[:, :, 128:256], g1v[:, :, 32:160])])
            slot_free(3)
            load(3, 1, [(r1[0:64, 0:1024], rwkv_w2[0]), (r1[64:128, 0:1024], rwkv_a2[0])])

            def square(w, n0):
                with sp.Fori(0, 2) as i:
                    for h in range(2):
                        sp.wait_ge(s.w_lo, n0 + 2 * i + h - 1)
                        v = block_rows(w, 2 * i + h)
                        for q in range(2):
                            sp.dma_start(cols(wraw[:, (n0 + h) % 2, :], 256)[:, 4 * q:4 * q + 4, :],
                                         v[:, 4 * q:4 * q + 4, :]).then_inc(raw[(n0 + h) % 2], 16)

            def mlp(layer, n0):
                for half in range(2):
                    m0 = n0 + 16 * half
                    with sp.Fori(0, 4) as i:
                        for h in range(2):
                            sp.wait_ge(s.w_lo, m0 + 2 * i + h - 1)
                            v = block_rows(mlp_w1[layer], 8 * half + 2 * i + h)
                            for q in range(2):
                                sp.dma_start(cols(wraw[:, (m0 + h) % 2, :], 256)[:, 4 * q:4 * q + 4, :],
                                             v[:, 4 * q:4 * q + 4, :]).then_inc(raw[(m0 + h) % 2], 16)
                    m0 += 8
                    with sp.Fori(0, 4) as i:
                        for h in range(2):
                            sp.wait_ge(s.w_lo, m0 + 2 * i + h - 1)
                            rows = mlp_w2[layer][half * 2048 + h * 1024:half * 2048 + (h + 1) * 1024, :]
                            v = block_rows(rows, i)
                            for q in range(2):
                                sp.dma_start(cols(wraw[:, (m0 + h) % 2, :], 256)[:, 4 * q:4 * q + 4, :],
                                             v[:, 4 * q:4 * q + 4, :]).then_inc(raw[(m0 + h) % 2], 16)
                    if half == 0:
                        sp.wait_ge(s.hid_rdy, 32 * layer + 16)
                        sp.dma_start(ptok[:, :, :], p[layer, 0].rearrange("(t p) d -> p t d", p=P)).then_inc(s.p_in, 16)

            def up(layer, n):
                slot_free(n)
                v = ple_w_up[layer].rearrange("(k p) n -> p k n", p=P)
                dst = cols(wraw[:, n % 2, :], 1024, 2)
                load(n, n % 2, [(dst[:, k:k + 1, :], v[:, k:k + 1, :]) for k in range(2)])

            square(rwkv_w_rkvo[0, 1], N_K)
            square(rwkv_w_rkvo[0, 0], N_R)
            square(rwkv_w_rkvo[0, 2], N_V)
            sp.wait_ge(s.bd_a, 4 * NQ)
            sp.dma_start(gn_c[:, :], consts[:, C_CEN:C_HOT]).then_inc(s.gnc_in, 16)
            slot_free(N_G2)
            load(N_G2, 0, [(r0[:, 0:1024], rwkv_g2[0][0:128, :]), (r0[:, 1024:2048], rwkv_g2[0][32:160, :])])
            square(rwkv_w_rkvo[0, 3], N_WO)
            mlp(0, L_MLP[0])
            up(0, L_MLP[0] + 32)
            square(ple_w_gate[0], L_MLP[0] + 33)
            square(w_k_shared, N_KS)
            sp.wait_ge(s.bv_ev, 2)
            sp.dma_start(bias_rows, bvec[:, :]).then_inc(s.bvec_out, 16)
            sp.wait_ge(s.bvec_out, 16)
            for h in range(8):
                src = bass.AP(bias_rows.tensor, 640 * h, [[1, P], [1, S]])
                sp.dma_start(strip[:, h, :], src).then_inc(s.strip_in, 16)
            square(w_v_shared, N_VS)
            square(diff_w_q[0], N_Q)
            square(diff_w_o[0], N_DO)
            mlp(1, L_MLP[1])
            up(1, L_MLP[1] + 32)
            square(ple_w_gate[1], L_MLP[1] + 33)
            for c in range(CT // 2):
                sp.wait_ge(s.fin_ev, 2 * (c + 1))
                sp.dma_start(out[0].rearrange("(t p) d -> p t d", p=P)[:, :, 256 * c:256 * (c + 1)],
                             OT[:, :, 256 * c:256 * (c + 1)]).then_inc(s.out_st, 16)
            sp.wait_ge(s.out_st, 16 * (CT // 2))

        @block.gpsimd
        def _(pool):
            for i, src in ((0, k_norm_g.rearrange("(o n) -> o n", o=1)), (1, diff_q_norm_g)):
                for h in range(2):
                    pool.dma_start(hrows[i:i + 1, h * HD:(h + 1) * HD], src).then_inc(s.hrows_in, 16)
            pool.dma_start(hrows[2:3, :], diff_subln_g).then_inc(s.hrows_in, 16)
            pool.dma_start(lrow[:, :, :], bass.AP(diff_lam.tensor, diff_lam.offset, [[0, P], [HD, 4], [1, HD]]))\
                .then_inc(s.lam_in, 16)
            pool.dma_start(cst[:, C_LVL:C_END], consts[:, C_LVL:C_END]).then_inc(s.cst2_in, 16)

            def low(n, par, rng, first):
                pool.wait_ge(s.w_hi, n + 1)
                if not first:
                    pool.wait_ge(s.pe_step, 8 * (n - 1))
                pool.tensor_tensor(wlo[:, par, rng], wraw[:, par, rng], whi[:, par, rng].bitcast(F32),
                                   ALU.subtract).then_inc(s.w_lo, 1)

            low(0, 0, slice(0, 1024), True)
            for k in range(CT):
                pool.wait_ge(s.h_ready, k + 1)
                if k == 0:
                    pool.wait_ge(s.x_edge, 1)
                pool.tensor_tensor(St[:, V_, k, :], X[:, k, 3:3 + S], X[:, k, 4:4 + S], ALU.subtract).then_inc(s.dx, 1)
            low(1, 1, slice(0, 1024), True)
            low(2, 0, slice(0, 2048), False)
            low(3, 1, slice(0, 1024), False)

            def lows(n0, n1):
                assert (n1 - n0) % 2 == 0
                with pool.Fori(0, (n1 - n0) // 2) as i:
                    for h in range(2):
                        low(n0 + 2 * i + h, (n0 + h) % 2, slice(0, 2048), False)

            lows(N_K, N_V + 4)

            link = Link(pool, s.pool_link)
            pool.wait_ge(s.prep, CT)
            pool.wait_ge(s.x_ready, X_V + CT)
            for t in (Bbd, Kbd, Vbd):
                pool.memset(t[:, :, :], 0.0).then_inc(s.bd_zero, 1)
            pool.wait_ge(s.pe_step, 8 * N_G2)
            pool.wait_ge(s.bd_zero, 3)
            for q in range(NQ):
                c, t0 = q // 2, (q % 2) * QUAD * CH
                pool.wait_ge(s.sc_ev, 5 * q + 1)
                pool.tensor_tensor(Wq[q % 2][:, :, 0:CH], Wq[q % 2][:, :, 0:CH], id_st, ALU.subtract).then_inc(s.mn_rdy, 1)
                pool.tensor_copy(Wq[q % 2][:, :, CH:P], id_st).then_inc(s.mn_rdy, 1)
                if q >= 1:
                    pool.wait_ge(s.tr_mm, 3 * q)
                if q >= 3:
                    pool.wait_ge(s.y_mm, 4 * (q - 2))
                if q == 0:
                    pool.wait_ge(s.dense_a, 36)
                if q < 3:
                    pool.memset(set_of(q)[7][:, :, :], 0.0).then_inc(s.bd_zero, 1)
                    pool.wait_ge(s.bd_zero, 4 + q)
                pool.wait_ge(s.mn_rdy, 2 * q + 2)
                for i, (dst, kind) in enumerate(((Vbd, V_), (set_of(q)[7], LW))):
                    for h in range(2):
                        if q or i or h:
                            pool.wait_ge(s.bd_p, 4 * q + 2 * i + h)
                        pool.tensor_copy(dst[64 * h:64 * h + 64, :, 64 * h:64 * h + 64],
                                         St[64 * h:64 * h + 64, kind, c, t0:t0 + QUAD * CH]
                                         .rearrange("p (u t) -> p u t", t=CH)).then_inc(s.bd_p, 1)
                pool.wait_ge(s.bd_p, 4 * q + 4)

            pool.wait_ge(s.y_mm, 4 * (NQ - 1))
            low(N_G2, 0, slice(0, 2048), False)
            pool.wait_ge(s.y_mm, 4 * NQ)
            low(N_WO, 1, slice(0, 2048), False)
            lows(N_WO + 1, L_MLP[0] + 31)
            low(L_MLP[0] + 31, 0, slice(0, 2048), False)
            low(L_MLP[0] + 32, 1, slice(0, 2048), False)
            lows(L_MLP[0] + 33, N_KS + 2)
            pool.wait_ge(s.upd, 8)
            pool.wait_ge(s.w_lo, N_KS + 2)
            pool.memset(QZ[0][64:128, :, :], 0.0).then_inc(s.q0_zero, 1)
            pool.wait_ge(s.q0_zero, 1)
            lows(N_KS + 2, N_VS)
            pool.wait_ge(s.w_lo, N_VS)
            pool.memset(QZ[1][0:64, :, :], 0.0).then_inc(s.q1_zero, 1)
            pool.wait_ge(s.q1_zero, 1)
            lows(N_VS, N_Q)

            def second_component(i, done):
                if i:
                    pool.wait_ge(s.q1_n, i)
                if done:
                    pool.wait_ge(s.w_lo, done)
                pool.wait_ge(s.qk_rs, 8 + i + 1)
                r = slice(64, 128)
                pool.tensor_tensor(QZ[1][r, i, :], q_raw(8 + i)[r, :], tmp[r, i % 2, :], ALU.mult).then_inc(s.q1_n, 1)
                pool.wait_ge(s.q1_n, i + 1)

            low(N_Q, 0, slice(0, 2048), False)
            for b in range(1, 6):
                low(N_Q + b, b % 2, slice(0, 2048), False)
                if 2 <= b < 4:
                    second_component(2 * b - 4, N_Q + b + 1)
                    second_component(2 * b - 3, 0)
            for i in range(32):
                w, k = (i % 4 + 1) * P, 2 * (i % 2)
                pool.wait_ge(s.rec, i + 1)
                pool.tensor_scalar(Pr[i % 2][:, 1, 0:w], Pr[i % 2][:, 1, 0:w], st_r[:, k + 1:k + 2], lamf, ALU.mult, ALU.mult)\
                    .then_inc(s.scaled, 1)
            lows(N_DO + 2, N_DO + 4)
            lows(L_MLP[1], L_MLP[1] + 32)
            low(L_MLP[1] + 32, 0, slice(0, 2048), False)
            lows(L_MLP[1] + 33, N_ALL)

        @block.tensor
        def _(pe):
            mm = pe.matmul

            def three(o, n, w, xs, first, last):
                (wh, wl), (ah, al) = w, xs
                mm(o, wh, ah, start=first, stop=False)
                mm(o, wh, al, start=False, stop=False)
                return mm(o, wl, ah, start=False, stop=last)

            def wslice(par, c0):
                return whi[:, par, c0:c0 + P], wlo[:, par, c0:c0 + P]

            def xs(k):
                return xh[:, k, :], xl[:, k, :]

            pe.wait_ge(s.cst_in, 16)
            pe.wait_ge(s.x_dg, TT)
            for c in range(CT):
                if c == 1:
                    pe.wait_ge(s.rows_in, 160)
                    for k in range(CT):
                        pe.transpose(pb[7][:, k * NV:(k + 1) * NV], vrows[:, k * P:(k + 1) * P], ident[0:NV, 0:NV])
                    pe.wait_ge(s.hrows_in, 80)
                    pe.transpose(pb[7][:, CT * NV:CT * NV + 3], hrows[:, :], ident[0:3, 0:3]).then_inc(s.par_tr, 1)
                if c == 7:
                    pe.wait_ge(s.par_ev, 2)
                for t in range(TT):
                    ins = mm(pb[c][:, t * P:(t + 1) * P], xtok[:, t, c * P:(c + 1) * P], rstd[:, t * P:(t + 1) * P],
                             start=True, stop=True)
                ins.then_inc(s.x_tr, 1)
            norms = [0]

            def norm_total(bank):
                norms[0] += 1
                pe.wait_ge(s.acc, 8 * norms[0])
                mm(pb[bank][:, :], ones, tmp[:, 3, :], start=True, stop=True).then_inc(s.norm_ps, 1)

            def dense_block(n, par, pair, width=2, x_base=None, hook=None, rows=None):
                pe.wait_ge(s.w_lo, n + 1)
                for k in range(CT):
                    if x_base is not None:
                        pe.wait_ge(s.x_ready, x_base + k + 1)
                    if hook and k in hook:
                        hook[k]()
                    for m in range(width):
                        ins = three(pb[2 * pair + m][:, :], n, wslice(par, k * P * width + m * P), xs(k),
                                    k == 0, k == CT - 1)
                    ins.then_inc(s.pe_step, 1)

            pe.wait_ge(s.h_ready, 3)
            dense_block(0, 0, 0, 1, X_W)
            dense_block(1, 1, 1, 1, X_A)
            pe.wait_ge(s.dense_a, 1)
            dense_block(2, 0, 0, 2, X_G)
            pe.wait_ge(s.w_lo, 4)
            pe.wait_ge(s.lora_rdy, 4)
            for g in range(8):
                if g == 0:
                    pe.wait_ge(s.dense_a, 2)
                elif g == 1:
                    pe.wait_ge(s.dense_a, 4)
                else:
                    pe.wait_ge(s.dense_a, 4 + 2 * (g - 1))
                pair = 1 - g % 2
                low_rank = (lora_h[:, 0, :], lora_l[:, 0, :]) if g < 4 else (rate_h[:, :], rate_l[:, :])
                for m in range(2):
                    c = (2 * g + m) % 8
                    w = (whi[:, 1, c * P:(c + 1) * P], wlo[:, 1, c * P:(c + 1) * P])
                    ins = three(pb[2 * pair + m][:, :], 3, w, low_rank, True, True)
                ins.then_inc(s.pe_step, 1)

            def kk_total(c):
                def f():
                    pe.wait_ge(s.kk_sq, c + 1)
                    j = c % 4
                    mm(pb[4 + c // 4][32 * j:32 * j + 32, :], bones[:, 0:P:4], tmp[:, c % 2, :], start=True, stop=True)\
                        .then_inc(s.kk_ps, 1)
                return f

            def kk_spread(c):
                def f():
                    pe.wait_ge(s.kk_rs, 1 + c // 4)
                    if c >= 3:
                        pe.wait_ge(s.kn, c - 2)
                    r = slice(32 * (c % 4), 32 * (c % 4) + 32)
                    mm(pb[(6, 7, 4)[c % 3]][:, :], ex2[r, :], rstd[r, :], start=True, stop=True).then_inc(s.kb_ps, 1)
                return f

            hooks = {1: {3: kk_total(0), 4: kk_total(1)}, 2: {3: kk_total(2), 4: kk_total(3)},
                     3: {3: kk_total(4), 4: kk_total(5)}, 4: {3: kk_total(6), 4: kk_total(7), 5: kk_spread(0), 6: kk_spread(1), 7: kk_spread(2)},
                     5: {5: kk_spread(3)}, 6: {6: kk_spread(4), 7: kk_spread(5)}, 7: {1: kk_spread(6)}, 8: {4: kk_spread(7)}}
            for t in range(12):
                if t < 2:
                    pe.wait_ge(s.dense_a, 18 + 2 * t)
                elif t < 6:
                    pe.wait_ge(s.dense_a, 20 + 2 * (t - 1))
                elif t < 10:
                    pe.wait_ge(s.dense_v, 2 * (t - 5))
                else:
                    pe.wait_ge(s.dense_a, 28 + 2 * (t - 9))
                dense_block(N_K + t, t % 2, 1 - t % 2, 2, {0: X_K, 4: X_R, 8: X_V}.get(t),
                            hooks.get(t))

            pe.wait_ge(s.prep, CT)
            pe.wait_ge(s.dense_v, 8)

            def score(q, i):
                if i == 0:
                    pe.wait_ge(s.bd_a, 4 * (q + 1))
                    if q >= 2:
                        pe.wait_ge(s.pb_ev[q % 2], 6 * (q // 2))
                        pe.wait_ge(s.tt_ev[q % 2], 2 * (q // 2))
                tokens = slice((q % 2) * QUAD * CH, (q % 2 + 1) * QUAD * CH)
                src = (Bbd, Kbd)[i]
                for u in range(QUAD):
                    t = slice(tokens.start + u * CH, tokens.start + (u + 1) * CH)
                    ins = mm(pb[3 + 2 * (q % 2) + i][:, u * P:(u + 1) * P], src[:, u, :], St[:, LW:R_ + 1, q // 2, t],
                             start=True, stop=True)
                ins.then_inc(s.sc_mm, 1)

            def turn(q, i):
                if q or i:
                    pe.wait_ge(s.tr_ev, 3 * q + i)
                if i == 2:
                    if q == 0:
                        pe.wait_ge(s.dense_a, 36)
                    pe.wait_ge(s.bd_p, 4 * q + 2)
                for u in range(QUAD):
                    ins = pe.transpose(pb[2][:, u * P:(u + 1) * P], (Bbd, Kbd, Vbd)[i][:, u, :], ident)
                ins.then_inc(s.tr_mm, 1)

            def level_p(q, lv):
                par, n = q % 2, q // 2
                pe.wait_ge(s.pt_ev[par], 6 * n + lv + 1)
                if lv:
                    pe.wait_ge(s.pb_ev[par], 6 * n + lv)
                else:
                    pe.wait_ge(s.sc_ev, 5 * q + 2)
                for u in range(QUAD):
                    ins = pe.transpose(pb[3 + 2 * par][:, u * P:(u + 1) * P], PT[par][:, u, :], ident)
                ins.then_inc(s.pt_tr[par], 1)

            def level_t(q, lv):
                par, n = q % 2, q // 2
                pe.wait_ge(s.pb_ev[par], 6 * n + lv + 1)
                if lv:
                    pe.wait_ge(s.w_ev[par], 5 * n + lv)
                else:
                    pe.wait_ge(s.mn_rdy, 2 * q + 2)
                    pe.wait_ge(s.sc_ev, 5 * q + 5)
                c0 = CH if lv == LEVELS - 1 else 0
                for u in range(QUAD):
                    ins = mm(pb[4 + 2 * par][:, u * P + c0:(u + 1) * P], Pb[par][:, u, :], Wq[par][:, u, c0:P],
                             start=True, stop=True)
                ins.then_inc(s.w_mm[par], 1)

            def chain_z(o, j):
                oB, oK, oV, oLak, oLrb, oLrk, oTiT, oA = set_of(o)
                J = 4 * o + j
                if J >= 1:
                    pe.wait_ge(s.h_ev, J)
                new = J % 8 == 0
                if j == 0:
                    pe.wait_ge(s.tr_ev, 3 * o + 3)
                    pe.wait_ge(s.sc_ev, 5 * o + 5)
                    pe.wait_ge(s.bd_p, 4 * o + 4)
                ins = mm(pb[0][:, 0:P], oLak[:, j, :], oV[:, j, :], start=True, stop=new)
                if not new:
                    ins = mm(pb[0][:, 0:P], oA[:, j, :], Hs[:, J % 2, :], start=False, stop=True)
                ins.then_inc(s.ch, 1)

            def chain_u(o, j):
                pe.wait_ge(s.z_ev, 2 * (4 * o + j) + 1)
                if j == 0:
                    pe.wait_ge(s.tt_ev[o % 2], 2 * (o // 2) + 2)
                mm(pb[0][:, 0:P], set_of(o)[6][:, j, :], Zs[:, :], start=True, stop=True).then_inc(s.ch, 1)

            def chain_h(o, j):
                oB, oK, oV, oLak, oLrb, oLrk, oTiT, oA = set_of(o)
                J = 4 * o + j
                new = J % 8 == 0
                pe.wait_ge(s.z_ev, 2 * J + 2)
                mm(pb[0][:, 0:P], oK[:, j, :], oV[:, j, :], start=True, stop=False)
                mm(pb[0][:, 0:P], oB[:, j, :], Us[:, :], start=False, stop=True).then_inc(s.ch, 1)
                if j == 0 and o >= 1:
                    pe.wait_ge(s.y_ev, o)
                y = pb[1][:, j * CH:(j + 1) * CH]
                t = slice((J % 8) * CH, (J % 8 + 1) * CH)
                if not new:
                    mm(y, Hs[:, J % 2, :], St[:, R_, o // 2, t], start=True, stop=False)
                mm(y, Us[:, :], oLrb[:, j, :], start=new, stop=False)
                mm(y, oV[:, j, :], oLrk[:, j, :], start=False, stop=True).then_inc(s.y_mm, 1)

            def centred(c):
                if c == 0:
                    pe.wait_ge(s.gnc_in, 16)
                    pe.wait_ge(s.pb_ev[0], 6 * NQ // 2)
                else:
                    pe.wait_ge(s.gn_sq, c)
                pe.wait_ge(s.y_ev, 2 * c + 2)
                mm(pb[3][:, :], centre, X[:, c, 4:4 + S], start=True, stop=True).then_inc(s.mu_mm, 1)

            def bonus(c):
                pe.wait_ge(s.pr_rdy, c + 1)
                if c == 0:
                    pe.wait_ge(s.tt_ev[0], 2 * NQ // 2)
                else:
                    pe.wait_ge(s.bon_v, c)
                mm(pb[4][:, :], bones, tmp[:, 2 + c % 2, :], start=True, stop=True).then_inc(s.bon_ps, 1)

            def variance(c):
                pe.wait_ge(s.gn_sq, c + 1)
                mm(pb[7][0:16, :], head_sel[:, 14 - 2 * c:30 - 2 * c], tmp[:, c % 2, :], start=(c == 0), stop=(c == CT - 1))\
                    .then_inc(s.gn_ps, 1)

            for i in range(NQ + 2):
                a, b, o = i, i - 1, i - 2
                first, second, chain = a < NQ, 0 <= b < NQ, o >= 0
                tile = 4 * (i - NQ) if i >= NQ else None
                if first:
                    score(a, 0)
                if chain:
                    chain_z(o, 0)
                if tile is not None:
                    centred(tile)
                if second:
                    level_p(b, 3)
                if chain:
                    chain_u(o, 0)
                if tile is not None:
                    bonus(tile)
                if first:
                    score(a, 1)
                if second:
                    level_t(b, 3)
                if chain:
                    chain_h(o, 0)
                if tile is not None:
                    variance(tile)
                if first:
                    turn(a, 0)
                if second:
                    level_p(b, 4)
                if chain:
                    chain_z(o, 1)
                if tile is not None:
                    centred(tile + 1)
                if first:
                    level_p(a, 0)
                if chain:
                    chain_u(o, 1)
                if tile is not None:
                    bonus(tile + 1)
                if second:
                    level_t(b, 4)
                if first:
                    turn(a, 1)
                if chain:
                    chain_h(o, 1)
                if tile is not None:
                    variance(tile + 1)
                if first:
                    level_t(a, 0)
                if second:
                    level_p(b, 5)
                if chain:
                    chain_z(o, 2)
                if tile is not None:
                    centred(tile + 2)
                if first:
                    level_p(a, 1)
                if chain:
                    chain_u(o, 2)
                if tile is not None:
                    bonus(tile + 2)
                if second:
                    level_t(b, 5)
                if chain:
                    chain_h(o, 2)
                if tile is not None:
                    variance(tile + 2)
                if first:
                    level_t(a, 1)
                if chain:
                    chain_z(o, 3)
                if tile == 0:
                    centred(tile + 3)
                if first:
                    turn(a, 2)
                    level_p(a, 2)
                if chain:
                    chain_u(o, 3)
                if tile == 0:
                    bonus(tile + 3)
                if first:
                    level_t(a, 2)
                if chain:
                    chain_h(o, 3)
                if tile == 0:
                    variance(tile + 3)

            centred(CT - 1)
            bonus(CT - 1)
            variance(CT - 1)
            pe.wait_ge(s.h_ev, 4 * NQ)
            pe.wait_ge(s.y_ev, NQ)
            pe.wait_ge(s.tr_ev, 3 * NQ)
            for par in range(2):
                pe.wait_ge(s.pb_ev[par], 6 * NQ // 2)
                pe.wait_ge(s.tt_ev[par], 2 * NQ // 2)
            pe.wait_ge(s.gn_sq, CT)
            pe.wait_ge(s.bon_v, CT)
            pe.wait_ge(s.w_lo, N_G2 + 1)
            pe.wait_ge(s.lora_rdy, 7)
            for c in range(CT):
                if c >= 2:
                    pe.wait_ge(s.y_fin, c - 1)
                if c == 1:
                    pe.wait_ge(s.gn_rt, 1)
                w = (whi[:, 0, c * P:(c + 1) * P], wlo[:, 0, c * P:(c + 1) * P])
                three(pb[6 + c % 2][:, :], N_G2, w, (lora_h[:, 1, :], lora_l[:, 1, :]), True, False)
                w = (whi[:, 0, 1024 + c * P:1024 + (c + 1) * P], wlo[:, 0, 1024 + c * P:1024 + (c + 1) * P])
                three(pb[6 + c % 2][:, :], N_G2, w, (lora_h[:, 2, :], lora_l[:, 2, :]), False, True)\
                    .then_inc(s.pe_step, 1)
                pe.wait_ge(s.x2_in, 64)
                if c >= 2:
                    pe.wait_ge(s.x2_cp, c - 1)
                else:
                    pe.wait_ge(s.bon_v, CT)
                for t in range(TT):
                    ins = pe.transpose(pb[2 + c % 2][:, t * P:(t + 1) * P], xtok2[:, t, c * P:(c + 1) * P], ident)
                ins.then_inc(s.x2_tr, 1)
                pe.wait_ge(s.gn_rs, 1)
                mm(pb[4 + c % 2][:, :], head_exp[:, c * P:(c + 1) * P], rstd[:, :], start=True, stop=True)\
                    .then_inc(s.rb_ps, 1)

            def proj(n0, x_base, ev0, hook=None):
                for b in range(4):
                    if b >= 2:
                        pe.wait_ge(s.dense_v, ev0 + 2 * (b - 1))
                    dense_block(n0 + b, (n0 + b) % 2, b % 2, 2, x_base if b == 0 else None, hook if b == 0 else None)

            pe.wait_ge(s.gn_sq, CT)
            pe.wait_ge(s.x2_cp, CT)
            proj(N_WO, X_Y, 8)

            def mlp(layer, n0, x_base, ev0):
                for half in range(2):
                    e = ev0 + 24 * half
                    m0 = n0 + 16 * half

                    def two_blocks(i, first):
                        for h in range(2):
                            pe.wait_ge(s.dense_v, e + 2 * (2 * i + h) - 2)
                            dense_block(m0 + 2 * i + h, (m0 + h) % 2, h, 2, x_base if h == 0 else None,
                                        {7: lambda: norm_total(4)} if first and h == 0 and half == 0 else None)
                    two_blocks(0, True)
                    with pe.Fori(1, 4) as i:
                        two_blocks(i, False)
                    m0 += 8
                    e += 16
                    if half == 1:
                        pe.wait_ge(s.p_in, 16 * (layer + 1))
                        for k in range(2):
                            for t in range(TT):
                                ins = pe.transpose(pb[5 + k][:, t * P:(t + 1) * P], ptok[:, t, k * P:(k + 1) * P], ident)
                            ins.then_inc(s.p_tr, 1)
                    with pe.Fori(0, 2) as i:
                        for g in range(2):
                            pe.wait_ge(s.dense_v, e + 2 * (2 * i + g) - 2)
                            for kb in range(2):
                                n = m0 + 4 * i + 2 * g + kb
                                par = (m0 + kb) % 2
                                pe.wait_ge(s.w_lo, n + 1)
                                for k in range(CT):
                                    if g == 0:
                                        pe.wait_ge(s.hid_rdy, 32 * layer + 16 * half + 8 * kb + k + 1)
                                    a = (hid_h[:, 8 * kb + k, :], hid_l[:, 8 * kb + k, :])
                                    for m in range(2):
                                        ins = three(pb[2 * g + m][:, :], n, wslice(par, k * 256 + m * P), a,
                                                    kb == 0 and k == 0, kb == 1 and k == CT - 1)
                                    ins.then_inc(s.pe_step, 1)

            def bias_by_distance():
                pe.wait_ge(s.far_row, 1)
                pe.wait_ge(s.hot_in, 16)
                pe.wait_ge(s.rel_in, 16)
                mm(pb[5][0:8, 0:S], relb[0:BUCKETS + 1, :], hot[0:BUCKETS + 1, 0:S], start=True, stop=True)
                mm(pb[6][0:8, 0:128], relb[0:BUCKETS + 1, :], hot[0:BUCKETS + 1, S:640], start=True, stop=True).then_inc(s.bv_mm, 1)

            def ple(layer, n, x_base, ev_a, ev0):
                pe.wait_ge(s.w_lo, n + 1)
                pe.wait_ge(s.p_rdy, 2 * (layer + 1))
                for m in range(CT):
                    if m == 0 or m == 2:
                        pe.wait_ge(s.dense_v, ev0 - 2 + m)
                    if m == 6:
                        norm_total(4)
                    if m >= 4:
                        pe.wait_ge(s.dense_a, ev_a + m - 3)
                    for k in range(2):
                        ins = three(pb[m % 4][:, :], n, wslice(n % 2, k * 1024 + m * P), (lora_h[:, k, :], lora_l[:, k, :]),
                                    k == 0, k == 1)
                    ins.then_inc(s.pe_step, 1)
                for b in range(4):
                    if b < 2:
                        pe.wait_ge(s.dense_a, ev_a + 6 + 2 * b)
                    else:
                        pe.wait_ge(s.dense_v, ev0 + 2 * (b - 1))
                    dense_block(n + 1 + b, (n + 1 + b) % 2, b % 2, 2, x_base if b == 0 else None,
                                {0: bias_by_distance} if layer == 0 and b == 3 else None)

            mlp(0, L_MLP[0], X_M0, 16)
            ple(0, L_MLP[0] + 32, X_P0, 36, 64)

            def square_total(i):
                pe.wait_ge(s.qk_sq, i + 1)
                if i == 0:
                    pe.wait_ge(s.bv_ev, 2)
                if i < 12:
                    if i >= 2:
                        pe.wait_ge(s.qk_rt, i - 1)
                    mm(pb[4 + i % 2][:, :], bones, tmp[:, i % 2, :], start=True, stop=True).then_inc(s.qk_ps, 1)
                else:
                    pe.wait_ge(s.v_ev, 8)
                    j = i - 12
                    mm(pb[6][32 * j:32 * j + 32, :], bones[:, 0:P:4], tmp[:, i % 2, :], start=True, stop=True)\
                        .then_inc(s.qk_ps, 1)

            def q_spread(i):
                pe.wait_ge(s.qk_rs, 13)
                if i >= 14:
                    pe.wait_ge(s.qk_n, 2 * i - 14)
                r = slice(32 * (i - 12), 32 * (i - 12) + 32)
                mm(pb[7 - i % 2][:, :], ex2[r, :], rstd[r, :], start=True, stop=True).then_inc(s.q_ps, 1)

            def qk_total(i0):
                def f():
                    square_total(i0)
                    square_total(i0 + 1)
                return f

            def v_turn(i0):
                def f():
                    for i in (i0, i0 + 1):
                        pe.wait_ge(s.dense_v, 80 + i + 1)
                        if i >= 2:
                            pe.wait_ge(s.v_ev, i - 1)
                        for t in range(TT):
                            ins = pe.transpose(pb[6 + i % 2][:, t * P:(t + 1) * P], tmp[:, 2 + i % 2, t * P:(t + 1) * P], ident)
                        ins.then_inc(s.v_tr, 1)
                return f

            for b in range(4):
                pe.wait_ge(s.dense_v, 72 + 2 * (b - 1))
                dense_block(N_KS + b, b % 2, b % 2, 2, X_KV if b == 0 else None,
                            {5: qk_total(2 * b - 2)} if b else {7: lambda: norm_total(4)})
            for b in range(4):
                pe.wait_ge(s.dense_v, 80 + 2 * (b - 1))
                dense_block(N_VS + b, b % 2, b % 2, 2, None, {5: v_turn(2 * b - 2)} if b else {5: qk_total(6)})
            for b in range(4):
                pe.wait_ge(s.dense_v, 88 + 2 * (b - 1))
                dense_block(N_Q + b, b % 2, b % 2, 2, X_Q if b == 0 else None, {5: qk_total(8 + 2 * b - 2)} if b else {5: v_turn(6)})
            def scores(i):
                h, b = i // 4, i % 4
                w = (b + 1) * P
                if b == 0:
                    if h < 4:
                        pe.wait_ge(s.qk_n, 8 + h + 1)
                        pe.wait_ge(s.q1_n, h + 1)
                    else:
                        pe.wait_ge(s.qk_n, 12 + 2 * (h - 3))
                if i >= 2:
                    pe.wait_ge(s.lg, 2 * (i - 1))
                for cmp in range(2):
                    mm(pb[2 * (i % 2) + cmp][:, 0:w], QZ[cmp][:, h, b * P:(b + 1) * P], KT[:, h, 0:w],
                       start=True, stop=True).then_inc(s.s_mm, 1)

            def attn_turn(i):
                pe.wait_ge(s.at_rdy, i + 1)
                if i >= 1:
                    pe.wait_ge(s.at_ev, i)
                for j in range(i % 4 + 1):
                    ins = pe.transpose(pb[4][:, j * P:(j + 1) * P], At[:, i % 2, j * P:(j + 1) * P], ident)
                ins.then_inc(s.at_tr, 1)

            def head_total(h):
                pe.wait_ge(s.o_sq, h + 1)
                mm(pb[7][0:8, :], one_col[:, 8 - h:16 - h], tmp[:, h % 2, :], start=(h == 0), stop=(h == 7)).then_inc(s.o_ps, 1)

            def values(i):
                h, b = i // 4, i % 4
                if b == 0 and h >= 2:
                    pe.wait_ge(s.o_sq, h - 1)
                pe.wait_ge(s.at_ev, i + 1)
                for j in range(b + 1):
                    ins = mm(pb[5 + h % 2][:, b * P:(b + 1) * P], VT[:, h, j, :], ATt[:, i % 2, j * P:(j + 1) * P],
                             start=(j == 0), stop=(j == b))
                ins.then_inc(s.o_mm, 1)

            def head_rstd(h):
                if h >= 4:
                    pe.wait_ge(s.o_f, h - 3)
                mm(pb[4 + h % 4][:, :], ident[:, h:h + 1].to_broadcast([P, P]), rstd[:, :], start=True, stop=True)\
                    .then_inc(s.ob_ps, 1)

            pe.wait_ge(s.v_ev, 8)
            for i in range(32 + 4):
                if i < 2:
                    pe.wait_ge(s.dense_v, 94 + 2 * i)
                if i < 32:
                    scores(i)
                if i == 1:
                    qk_total(14)()
                if i in (5, 7):
                    q_spread(7 + i)
                    q_spread(8 + i)
                if i == 3:
                    pe.wait_ge(s.qk_rt, 12)
                if i == 8:
                    pe.wait_ge(s.qk_n, 20)
                if 0 <= i - 3 < 32:
                    attn_turn(i - 3)
                if i >= 4:
                    values(i - 4)
                if i >= 9 and i % 4 == 1:
                    head_total((i - 9) // 4)
            head_total(7)
            pe.wait_ge(s.o_rs, 1)
            for h in range(4):
                head_rstd(h)
            proj(N_DO, X_O, 96, {k: (lambda h=k + 4: head_rstd(h)) for k in range(4)})
            mlp(1, L_MLP[1], X_M1, 104)
            ple(1, L_MLP[1] + 32, X_P1, 44, 152)
            for c in range(CT):
                pe.wait_ge(s.upd, 8 + c + 1)
                if c >= 4:
                    pe.wait_ge(s.fin_ev, c - 3)
                for t in range(TT):
                    ins = pe.transpose(pb[4 + c % 4][:, t * P:(t + 1) * P], X[:, c, t * P:(t + 1) * P], ident)
                ins.then_inc(s.fin_tr, 1)

        @block.scalar
        def _(act):
            A = act.activation
            raw = (s.raw0, s.raw1)
            act.dma_start(cst[:, 0:C_LVL], consts[:, 0:C_LVL]).then_inc(s.cst_in, 16)

            def row(a):
                return a.rearrange("(o n) -> o n", o=1)

            for dst, src in ((vrows[0:6, :], norm_g.rearrange("a b n -> (a b) n")), (vrows[6:7, :], row(kv_norm_g)),
                             (vrows[7:13, :], rwkv_mix[0]), (vrows[13:14, :], rwkv_w0), (vrows[14:15, :], rwkv_a0),
                             (vrows[15:16, :], rwkv_k_k), (vrows[16:17, :], rwkv_k_a), (vrows[17:18, :], rwkv_ln_w),
                             (vrows[18:19, :], rwkv_ln_b), (vrows[19:20, :], rwkv_r_k.rearrange("o h n -> o (h n)"))):
                act.dma_start(dst, src).then_inc(s.rows_in, 16)
            def high(n, par, rng=slice(0, 2048), first=False):
                act.wait_ge(raw[par], 16 * (n - par) + 32)
                if not first:
                    act.wait_ge(s.pe_step, 8 * (n - 1))
                A(whi[:, par, rng], wraw[:, par, rng], ACT.Copy).then_inc(s.w_hi, 1)

            def split_high(k, src, gain, free):
                if free is not None:
                    act.wait_ge(s.pe_step, free + k + 1)
                if gain is None:
                    A(xh[:, k, :], src, ACT.Copy).then_inc(s.x_hi, 1)
                else:
                    A(xh[:, k, :], src, ACT.Copy, scale=gain).then_inc(s.x_hi, 1)

            def norm_root(i):
                act.wait_ge(s.norm_ps, i)
                A(rstd[:, :], pb[4][:, :], ACT.Sqrt, bias=eps_n, scale=1.0 / D).then_inc(s.norm_rt, 1)

            for t in range(TT):
                act.wait_ge(s.x_in[t], 16)
                if t >= 2:
                    act.wait_ge(s.x_sq, t - 1)
                A(tmp[:, 2 * (t % 2):2 * (t % 2) + 2, :].rearrange("p a b -> p (a b)"), xtok[:, t, :], ACT.Square,
                  accum_out=x_ss[:, t:t + 1]).then_inc(s.x_sq, 1)
            act.wait_ge(s.x_sq, TT)
            act.wait_ge(s.small_set, 1)
            A(x_rms, x_ss, ACT.Sqrt, bias=eps_n, scale=1.0 / D).then_inc(s.x_rt, 1)
            high(0, 0, slice(0, 1024), True)
            act.wait_ge(s.par_ev, 1)
            for c in range(CT):
                act.wait_ge(s.x_tr, c + 1)
                A(X[:, c, 4:4 + S], pb[c][:, :], ACT.Copy, scale=vec(c, V_N00)).then_inc(s.h_ready, 1)
                if c == 3:
                    high(1, 1, slice(0, 1024), True)

            def mix_high(i, k, free):
                act.wait_ge(s.mix_b, 8 * i + k + 1)
                split_high(k, tmp[:, mix_place(i, k), :], None, free)

            def mixes(i, free):
                for k in range(CT):
                    mix_high(i, k, free)

            mixes(0, None)
            act.wait_ge(s.lam_s, 1)
            A(lamw[:, 2:4], lamw[:, 0:2], ACT.Exp).then_inc(s.lam_e, 1)
            mixes(1, 0)
            act.wait_ge(s.pe_step, 8)
            A(rstd[0:64, :], pb[0][0:64, :], ACT.Tanh).then_inc(s.dense_a, 1)
            high(2, 0)
            mixes(2, 8 * 1)
            act.wait_ge(s.pe_step, 16)
            A(rstd[64:128, :], pb[2][64:128, :], ACT.Copy).then_inc(s.dense_a, 1)
            high(3, 1, slice(0, 1024))
            act.wait_ge(s.dense_a, 2)
            for dst, r, z in ((lora_h[:, 0, :], slice(0, 64), slice(64, 128)), (rate_h[:, :], slice(64, 128), slice(0, 64))):
                A(dst[r], rstd[r, :], ACT.Copy).then_inc(s.lora_hi, 1)
                A(dst[z], rstd[z, :], ACT.Copy, scale=0.0).then_inc(s.lora_hi, 1)
            act.wait_ge(s.pe_step, 24)
            for m in range(2):
                A(St[:, K_, m, :], pb[m][:, :], ACT.Sigmoid).then_inc(s.dense_a, 1)
            act.wait_ge(s.dense_a, 3)
            A(lora_h[:, 1, :], St[:, K_, 0, :], ACT.Copy).then_inc(s.lora_hi, 1)
            act.wait_ge(s.dense_a, 4)
            A(lora_h[0:96, 2, :], St[0:96, K_, 1, :], ACT.Copy, scale=0.0).then_inc(s.lora_hi, 1)
            A(lora_h[96:128, 2, :], St[96:128, K_, 1, :], ACT.Copy).then_inc(s.lora_hi, 1)
            high(4, 0)
            for g in range(8):
                act.wait_ge(s.pe_step, 24 + g + 1)
                for m in range(2):
                    c = (2 * g + m) % 8
                    kind, bias = (LW, V_W0) if g < 4 else (A_, V_A0)
                    A(St[:, kind, c, :], pb[2 * (1 - g % 2) + m][:, :], ACT.Sigmoid, bias=vec(c, bias))\
                        .then_inc(s.dense_a, 1)
                mix_high(3, g, 8 * 2)
            high(5, 1)

            def decay_before(c):
                act.wait_ge(s.g_cum, 2 * c + 2)
                A(St[:, LW, c, :], (prep_a, prep_b)[c % 2][:, :], ACT.Exp, scale=-KAPPA).then_inc(s.dec, 1)

            def kk_square(c):
                if c >= 2:
                    act.wait_ge(s.kk_ps, c - 1)
                act.wait_ge(s.dense_a, 20 + c + 1)
                A(tmp[:, c % 2, :], St[:, K_, c, :], ACT.Square, scale=vec(c, V_KK)).then_inc(s.kk_sq, 1)

            def kk_root(i):
                act.wait_ge(s.kk_ps, 4 * i + 4)
                if i:
                    act.wait_ge(s.kb_ps, 4)
                A(rstd[:, :], pb[4 + i][:, :], ACT.Sqrt, bias=eps_0).then_inc(s.kk_rt, 1)

            def decays(c):
                act.wait_ge(s.g_cum, 16)
                act.wait_ge(s.dec, 8)
                if c >= 2:
                    act.wait_ge(s.prep, c - 1)
                A((prep_a, prep_b)[c % 2][:, :], St[:, R_, c, :], ACT.Exp, scale=KAPPA).then_inc(s.exps, 1)
                A(gC[:, c * 8:(c + 1) * 8], St[:, R_, c, CH - 1:S:CH], ACT.Exp, scale=-KAPPA).then_inc(s.exps, 1)
                act.wait_ge(s.exps, 3 * c + 2)
                A(St[:, R_, c, :], St[:, R_, c, :], ACT.Exp, scale=-KAPPA).then_inc(s.exps, 1)

            def diag_copies(q):
                if q >= 1:
                    act.wait_ge(s.tr_mm, 3 * (q - 1) + 2)
                for dst, kind in ((Bbd, A_), (Kbd, K_)):
                    for h in range(2):
                        A(dst[64 * h:64 * h + 64, :, 64 * h:64 * h + 64],
                          St[64 * h:64 * h + 64, kind, q // 2, (q % 2) * QUAD * CH:(q % 2 + 1) * QUAD * CH]
                          .rearrange("p (u t) -> p u t", t=CH), ACT.Copy).then_inc(s.bd_a, 1)

            for t in range(12):
                n = N_K + t
                if t == 11:
                    act.wait_ge(s.prep, 1)
                    act.wait_ge(s.bd_zero, 3)
                    diag_copies(0)
                if t == 3:
                    kk_root(0)
                    mixes(4, 8 * (N_K + 3))
                if t == 7:
                    mixes(5, 8 * (N_R + 3))
                if t < 4 or t >= 8:
                    kind, c = (K_, 2 * t) if t < 4 else (V_, 2 * (t - 8))
                    act.wait_ge(s.pe_step, 8 * (n + 1))
                    for m in range(2):
                        A(St[:, kind, c + m, :], pb[2 * (1 - t % 2) + m][:, :], ACT.Copy).then_inc(s.dense_a, 1)
                if t < 4:
                    kk_square(2 * t)
                    kk_square(2 * t + 1)
                if n + 2 < N_G2:
                    high(n + 2, t % 2)
                if t < 4:
                    if t == 0:
                        for c in range(CT):
                            decay_before(c)
                    if t == 3:
                        decays(0)
                        decays(1)
                elif t == 4:
                    decays(2)
                    decays(3)
                elif t == 5:
                    kk_root(1)
                    decays(4)
                    decays(5)
                elif t == 6:
                    decays(6)
                    decays(7)

            def flat(t):
                return t[:, :, :].rearrange("p u t -> p (u t)")

            def turned(q, i):
                act.wait_ge(s.tr_mm, 3 * q + i + 1)
                if q >= 3:
                    act.wait_ge(s.y_mm, 4 * (q - 2))
                A(flat(set_of(q)[i]), pb[2][:, :], ACT.Copy).then_inc(s.tr_ev, 1)

            def take_p(q, lv):
                par, n = q % 2, q // 2
                act.wait_ge(s.pt_tr[par], 6 * n + lv + 1)
                A(flat(Pb[par]), pb[3 + 2 * par][:, :], ACT.Copy).then_inc(s.pb_ev[par], 1)

            def take_inverse(q):
                par, n = q % 2, q // 2
                act.wait_ge(s.w_mm[par], 6 * n + 6)
                if q < 3:
                    act.wait_ge(s.set_zero, 2 * q + 2)
                for h in range(2):
                    r = slice(64 * h, 64 * h + 64)
                    A(set_of(q)[6][r, :, r], pb[4 + 2 * par][r, :].rearrange("p (u t) -> p u t", t=P)[:, :, CH:P], ACT.Copy)\
                        .then_inc(s.tt_ev[par], 1)

            def decayed(o, j):
                J = 4 * o + j
                if J % 8:
                    act.wait_ge(s.h_ev, J)
                    A(Hg[:, :], Hs[:, J % 2, :], ACT.Copy, scale=gC[:, (o // 2) * 8 + J % 8:(o // 2) * 8 + J % 8 + 1])\
                        .then_inc(s.hg, 1)

            def take_z(o, j):
                act.wait_ge(s.ch, 3 * (4 * o + j) + 1)
                A(Zs[:, :], pb[0][:, 0:P], ACT.Copy).then_inc(s.z_ev, 1)

            def take_u(o, j):
                J = 4 * o + j
                act.wait_ge(s.ch, 3 * J + 2)
                if J >= 1:
                    act.wait_ge(s.y_mm, J)
                A(Us[:, :], pb[0][:, 0:P], ACT.Copy).then_inc(s.z_ev, 1)

            def centred(c):
                act.wait_ge(s.mu_mm, c + 1)
                A(X[:, c, 4:4 + S], pb[3][:, :], ACT.Copy).then_inc(s.yc_rdy, 1)
                if c == 0:
                    act.wait_ge(s.tr_mm, 3 * NQ)
                if c >= 2:
                    act.wait_ge(s.gn_ps, c - 1)
                A(tmp[:, c % 2, :], pb[3][:, :], ACT.Square).then_inc(s.gn_sq, 1)

            act.wait_ge(s.prep, CT)
            act.wait_ge(s.dense_v, 8)
            for i in range(NQ + 2):
                a, b, o = i, i - 1, i - 2
                first, second, chain = a < NQ, 0 <= b < NQ, o >= 0
                tile = 4 * (i - NQ) if i >= NQ else None
                if chain:
                    take_z(o, 0)
                    decayed(o, 0)
                if second:
                    take_p(b, 3)
                if chain:
                    take_u(o, 0)
                if tile is not None:
                    centred(tile)
                if i == NQ + 1:
                    act.wait_ge(s.y_mm, 4 * (NQ - 1))
                    high(N_G2, 0)
                if first:
                    turned(a, 0)
                if second:
                    take_p(b, 4)
                if chain:
                    take_z(o, 1)
                    decayed(o, 1)
                if first:
                    take_p(a, 0)
                if chain:
                    take_u(o, 1)
                if tile is not None:
                    centred(tile + 1)
                if i == NQ + 1:
                    high(N_WO, 1)
                if first:
                    turned(a, 1)
                if second:
                    take_p(b, 5)
                if chain:
                    take_z(o, 2)
                    decayed(o, 2)
                if first:
                    take_p(a, 1)
                if chain:
                    take_u(o, 2)
                if tile is not None:
                    centred(tile + 2)
                if second:
                    take_inverse(b)
                if chain:
                    take_z(o, 3)
                    decayed(o, 3)
                if first:
                    turned(a, 2)
                    take_p(a, 2)
                if chain:
                    take_u(o, 3)
                if tile == 0:
                    centred(tile + 3)
                if a + 1 < NQ:
                    diag_copies(a + 1)
                if chain:
                    act.wait_ge(s.y_mm, 4 * (o + 1))
                    t0 = 4 + (o % 2) * QUAD * CH
                    A(X[:, o // 2, t0:t0 + QUAD * CH], pb[1][:, 0:QUAD * CH], ACT.Copy).then_inc(s.y_ev, 1)

            for t in range(TT):
                act.dma_start(xtok2[:, t, :], x[0, t * P:(t + 1) * P, :]).then_inc(s.x2_in, 16)
            centred(CT - 1)
            act.wait_ge(s.gn_ps, CT)
            act.wait_ge(s.rows_0, 1)
            A(rstd[0:16, :], pb[7][0:16, :], ACT.Sqrt, bias=eps_g[0:16, :], scale=1.0 / HD).then_inc(s.gn_rt, 1)
            act.wait_ge(s.pr_rdy, CT)
            for c in range(CT):
                act.wait_ge(s.x2_tr, c + 1)
                A(St[:, K_, c, :], pb[2 + c % 2][:, :], ACT.Copy).then_inc(s.x2_cp, 1)
                act.wait_ge(s.y_fin, c + 1)
                split_high(c, tmp[:, 2 + c % 2, :], None, None)

            squares = [0]

            def square(c, slot, src_sem, src_count):
                i = squares[0]
                squares[0] += 1
                act.wait_ge(src_sem, src_count)
                if i >= 2:
                    act.wait_ge(s.acc, i if slot == 2 else i - 1)
                A(tmp[:, slot, :], X[:, c, 0:S], ACT.Square).then_inc(s.sq_rdy, 1)

            def splits(gain, free, k0=0, k1=CT):
                for k in range(k0, k1):
                    split_high(k, X[:, k, 0:S], vec(k, gain), free)

            def proj(n0, ev0, gain):
                for b in range(4):
                    if n0 == N_WO or b:
                        high(n0 + b + 1, (n0 + b + 1) % 2)
                    if b == 3:
                        splits(gain, 8 * (n0 + 3), 0, 6)
                        act.wait_ge(s.dense_v, ev0 + 8)
                        splits(gain, 8 * (n0 + 3), 6)
                    for m in range(2):
                        square(2 * b + m, m, s.dense_v, ev0 + 2 * b + m + 1)

            def mlp(layer, n0, ev0, ni, gain):
                for half in range(2):
                    m0 = n0 + 16 * half
                    h0 = 32 * layer + 16 * half

                    def two_blocks(i, first):
                        for h in range(2):
                            high(m0 + 2 * i + h + 1, (m0 + h + 1) % 2)
                            if first and h == 0 and half == 0:
                                norm_root(ni)
                            for m in range(2):
                                act.wait_ge(s.hid_f, h0 + 4 * i + 2 * h + m + 1)
                                A(hid_h[:, bass.ds(4 * i + 2 * h + m, 1), :], tmp[:, 2 + m:3 + m, :], ACT.Copy)\
                                    .then_inc(s.hid_hi, 1)
                    two_blocks(0, True)
                    with act.Fori(1, 4) as i:
                        two_blocks(i, False)
                    m0 += 8
                    if half == 1:
                        for k in range(2):
                            act.wait_ge(s.p_tr, 2 * layer + k + 1)
                            A(lora_h[:, k, :], pb[5 + k][:, :], ACT.Copy).then_inc(s.p_hi, 1)
                    if half == 0:
                        with act.Fori(0, 4) as i:
                            for h in range(2):
                                high(m0 + 2 * i + h + 1, (m0 + h + 1) % 2)
                    else:
                        for b in range(8):
                            high(m0 + b + 1, (m0 + b + 1) % 2)
                            if b == 7:
                                splits(gain, None, 0, 6)
                                act.wait_ge(s.dense_v, ev0 + 48)
                                splits(gain, None, 6)
                            if b % 2:
                                for m in range(2):
                                    square(b - 1 + m, m, s.dense_v, ev0 + 40 + b + m)

            def ple(layer, n, ni):
                high(n + 1, (n + 1) % 2)
                if layer == 0:
                    act.wait_ge(s.pe_step, 8 * n)
                    act.dma_start(hot[:, :], consts[:, C_HOT:C_HOT + 640]).then_inc(s.hot_in, 16)
                    act.dma_start(relb[0:BUCKETS, :], rel_bias).then_inc(s.rel_in, 16)
                for m in range(CT):
                    act.wait_ge(s.pe_step, 8 * n + m + 1)
                    A(UP[:, m, :], pb[m % 4][:, :], ACT.Copy).then_inc(s.dense_a, 1)
                norm_root(ni)
                high(n + 2, n % 2)
                for b in range(4):
                    if layer == 0 and b == 3:
                        splits(V_KV, 8 * (n + 4), 0, 6)
                    for m in range(2):
                        c = 2 * b + m
                        act.wait_ge(s.dense_v, 64 + 88 * layer + c + 1)
                        A(tmp[:, m, :], tmp[:, m, :], ACT.Sigmoid).then_inc(s.sig, 1)
                    if layer == 0 and b == 3:
                        act.wait_ge(s.upd, 8)
                        splits(V_KV, 8 * (n + 4), 6)
                    if n + 3 + b < N_ALL:
                        high(n + 3 + b, (n + 1 + b) % 2)
                    if layer == 0:
                        for m in range(2):
                            square(2 * b + m, 2, s.upd, 2 * b + m + 1)

            proj(N_WO, 8, V_N01)
            mlp(0, L_MLP[0], 16, 1, V_N02)
            ple(0, L_MLP[0] + 32, 2)

            act.wait_ge(s.upd, 8)

            def head_square(i):
                src = KT[:, i, :] if i < 8 else q_raw(i)
                act.wait_ge(s.dense_v, 72 + i + 1 if i < 8 else 88 + i - 8 + 1)
                if 2 <= i < 14:
                    act.wait_ge(s.qk_n, i - 1)
                if 10 <= i < 14:
                    act.wait_ge(s.q1_n, i - 9)
                if i >= 14:
                    act.wait_ge(s.qk_ps, i - 1)
                A(tmp[:, i % 2, :], src, ACT.Square).then_inc(s.qk_sq, 1)

            def head_root(i):
                act.wait_ge(s.qk_ps, i + 1)
                A(tmp[:, i % 2, :], pb[4 + i % 2][:, :], ACT.Sqrt, bias=eps_n, scale=1.0 / HD).then_inc(s.qk_rt, 1)

            def v_copy(i):
                act.wait_ge(s.v_tr, i + 1)
                A(VT[:, i, :, :].rearrange("p t v -> p (t v)"), pb[6 + i % 2][:, :], ACT.Copy).then_inc(s.v_ev, 1)

            for b in range(4):
                if b == 0:
                    norm_root(3)
                else:
                    high(N_KS + b + 1, (b + 1) % 2)
                    head_root(2 * b - 2)
                    head_root(2 * b - 1)
                head_square(2 * b)
                head_square(2 * b + 1)
            for b in range(4):
                high(N_VS + b + 1, (b + 1) % 2)
                if b:
                    v_copy(2 * b - 2)
                    v_copy(2 * b - 1)
                else:
                    head_root(6)
                    head_root(7)
            splits(V_N10, 8 * (N_VS + 3))
            for b in range(4):
                high(N_Q + b + 1, (b + 1) % 2)
                if b == 0:
                    v_copy(6)
                    v_copy(7)
                elif b < 3:
                    head_root(8 + 2 * b - 2)
                    head_root(8 + 2 * b - 1)
                head_square(8 + 2 * b)
                head_square(8 + 2 * b + 1)

            def exps(i):
                w = (i % 4 + 1) * P
                act.wait_ge(s.lg, 2 * i + 2)
                if i >= 2:
                    act.wait_ge(s.at_rdy, i - 1)
                for m in range(2):
                    k = 2 * (i % 2) + m
                    A(Pr[i % 2][:, m, 0:w], Lg[i % 2][:, m, 0:w], ACT.Exp, bias=st_n[:, k:k + 1], scale=-1.0,
                      accum_out=st_l[:, k:k + 1]).then_inc(s.pexp, 1)

            def attn_copy(i):
                w = (i % 4 + 1) * P
                act.wait_ge(s.at_tr, i + 1)
                if i >= 2:
                    act.wait_ge(s.o_mm, i - 1)
                A(ATt[:, i % 2, 0:w], pb[4][:, 0:w], ACT.Copy).then_inc(s.at_ev, 1)

            def head_take(h):
                act.wait_ge(s.o_mm, 4 * h + 4)
                if h == 0:
                    act.wait_ge(s.q1_n, 4)
                    act.wait_ge(s.qk_n, 20)
                A(QZ[0][:, h, :], pb[5 + h % 2][:, :], ACT.Copy).then_inc(s.o_cp, 1)
                if h >= 2:
                    act.wait_ge(s.o_ps, h - 1)
                A(tmp[:, h % 2, :], pb[5 + h % 2][:, :], ACT.Square).then_inc(s.o_sq, 1)

            high(N_DO + 1, 1)
            for i in range(1, 32 + 4):
                if i - 1 < 32:
                    exps(i - 1)
                if i == 2:
                    act.wait_ge(s.qk_ps, 16)
                    A(rstd[:, :], pb[6][:, :], ACT.Sqrt, bias=eps_n, scale=1.0 / HD).then_inc(s.qk_rt, 1)
                if 0 <= i - 3 < 32:
                    attn_copy(i - 3)
                if i >= 8 and i % 4 == 0:
                    head_take((i - 8) // 4)
            head_take(7)
            act.wait_ge(s.o_ps, 8)
            act.wait_ge(s.rows_0, 2)
            A(rstd[0:8, :], pb[7][0:8, :], ACT.Sqrt, bias=eps_n[0:8, :], scale=1.0 / P).then_inc(s.o_rt, 1)
            act.wait_ge(s.pe_step, 8 * N_DO)
            for h in range(8):
                act.wait_ge(s.o_f, h + 1)
                split_high(h, tmp[:, 2 + h % 2, :], None, None)
            proj(N_DO, 96, V_N11)
            mlp(1, L_MLP[1], 104, 4, V_N12)
            ple(1, L_MLP[1] + 32, 5)
            for c in range(CT):
                act.wait_ge(s.fin_tr, c + 1)
                A(OT[:, :, c * P:(c + 1) * P], pb[4 + c % 4][:, :].rearrange("p (t d) -> p t d", d=P), ACT.Copy)\
                    .then_inc(s.fin_ev, 1)

        @block.vector
        def _(dve):
            link = Link(dve, s.vec_link)
            tt, stt, ts = dve.tensor_tensor, dve.scalar_tensor_tensor, dve.tensor_scalar

            dve.memset(eps_n, NORM_EPS).then_inc(s.vec_link, 1)
            dve.memset(eps_g, GN_EPS).then_inc(s.vec_link, 1)
            link.n = 2
            dve.wait_ge(s.vec_link, 2)
            dve.memset(eps_0, 0.0).then_inc(s.small_set, 1)
            dve.memset(X[:, :, 0:4], 0.0).then_inc(s.x_edge, 1)
            link(dve.memset(one_col, 0.0))
            link(dve.memset(one_col[:, 8:9], 1.0))

            dve.wait_ge(s.x_rt, 1)
            dve.reciprocal(x_rms, x_rms).then_inc(s.x_rs, 1)
            dve.wait_ge(s.x_rs, 1)
            dve.wait_ge(s.cst_in, 16)
            for t in range(TT):
                ts(rstd[:, t * P:(t + 1) * P], ident, x_rms[:, t:t + 1], None, ALU.mult).then_inc(s.x_dg, 1)
            dve.wait_ge(s.par_tr, 1)
            dve.tensor_copy(PV[:, :, :], pb[7][:, 0:CT * NV].rearrange("p (c v) -> p c v", v=NV)).then_inc(s.par_ev, 1)
            dve.tensor_copy(hv[:, 0:3], pb[7][:, CT * NV:CT * NV + 3]).then_inc(s.par_ev, 1)
            dve.wait_ge(s.par_ev, 2)
            link(ts(omka, PV[:, :, V_KA], -1.0, 1.0, ALU.mult, ALU.add))
            link(ts(qk_gain, hv[:, 1:2], HD ** -0.5, hv[:, 0:1], ALU.mult, ALU.mult))
            link(ts(subg, hv[:, 2:3], 1.0 - LAMBDA_INIT, None, ALU.mult))

            def norm_finish(i):
                dve.wait_ge(s.norm_rt, i)
                link(dve.reciprocal(rstd[:, :], rstd[:, :]))

            def low(k, src, n):
                dve.wait_ge(s.x_hi, n + 1)
                tt(xl[:, k, :], src, xh[:, k, :].bitcast(F32), ALU.subtract).then_inc(s.x_ready, 1)

            def mixes(i, mix):
                ahead = 2 if i != 4 else 1

                def mixed(k):
                    if i == 0:
                        dve.wait_ge(s.dx, k + 1)
                    if 8 * i + k - 2 * ahead >= 0:
                        dve.wait_ge(s.x_ready, 8 * i + max(k - 2 * ahead, -1) + 1)
                    stt(tmp[:, mix_place(i, k), :], St[:, V_, k, :], vec(k, V_MIX + mix), X[:, k, 4:4 + S], ALU.mult, ALU.add)\
                        .then_inc(s.mix_b, 1)
                for k in range(ahead):
                    mixed(k)
                for k in range(CT):
                    if k + ahead < CT:
                        mixed(k + ahead)
                    dve.wait_ge(s.mix_b, 8 * i + k + 1)
                    low(k, tmp[:, mix_place(i, k), :], 8 * i + k)

            def lora_low(dst, high, src, r):
                z = slice(64, 128) if r == slice(0, 64) else slice(0, r.start)
                tt(dst[r], src[r], high[r].bitcast(F32), ALU.subtract).then_inc(s.lora_rdy, 1)
                if z.stop:
                    ts(dst[z], src[z], 0.0, None, ALU.mult).then_inc(s.lora_rdy, 1)

            mixes(0, MIX_W)
            dve.wait_ge(s.lam_in, 16)
            link(tt(lrow[:, 0:2, :], lrow[:, 0:4:2, :], lrow[:, 1:4:2, :], ALU.mult))
            dve.tensor_reduce(lamw[:, 0:2], lrow[:, 0:2, :], AX.X, ALU.add).then_inc(s.lam_s, 1)
            dve.wait_ge(s.lam_e, 1)
            link(tt(lamf, lamw[:, 2:3], lamw[:, 3:4], ALU.subtract))
            link(ts(lamf, lamf, LAMBDA_INIT, None, ALU.add))

            mixes(1, MIX_A)
            mixes(2, MIX_G)
            dve.wait_ge(s.lora_hi, 4)
            lora_low(lora_l[:, 0, :], lora_h[:, 0, :], rstd[:, :], slice(0, 64))
            lora_low(rate_l[:, :], rate_h[:, :], rstd[:, :], slice(64, 128))
            dve.wait_ge(s.lora_hi, 5)
            lora_low(lora_l[:, 1, :], lora_h[:, 1, :], St[:, K_, 0, :], slice(0, 128))
            dve.wait_ge(s.lora_hi, 7)
            lora_low(lora_l[:, 2, :], lora_h[:, 2, :], St[:, K_, 1, :], slice(96, 128))
            mixes(3, MIX_K)

            def log_decays(c):
                if c == 0:
                    dve.wait_ge(s.cst2_in, 16)
                    dve.wait_ge(s.lora_rdy, 7)
                    dve.wait_ge(s.pe_step, 8 * N_K)
                dve.wait_ge(s.dense_a, 4 + c + 1)
                dve.tensor_tensor_scan(St[:, R_, c, :], cst[:, C_SEG:C_SEG + S], St[:, LW, c, :], 0.0, ALU.mult, ALU.add)\
                    .then_inc(s.g_cum, 1)
                dve.wait_ge(s.g_cum, 2 * c + 1)
                if c >= 2:
                    dve.wait_ge(s.dec, c - 1)
                tt((prep_a, prep_b)[c % 2][:, :], St[:, R_, c, :], St[:, LW, c, :], ALU.subtract).then_inc(s.g_cum, 1)

            def kk_invert(i):
                dve.wait_ge(s.kk_rt, i + 1)
                link(ts(rstd[:, :], rstd[:, :], 1e-12, None, ALU.max))
                dve.reciprocal(rstd[:, :], rstd[:, :]).then_inc(s.kk_rs, 1)

            def prep(c):
                lw, k, a = (St[:, kind, c, :] for kind in (LW, K_, A_))
                kn, pa, inv = tmp[:, 0, :], tmp[:, 1, :], (prep_a, prep_b)[c % 2][:, :]
                if c == 0:
                    dve.wait_ge(s.dense_a, 28)
                    dve.wait_ge(s.kk_ps, 8)
                else:
                    dve.wait_ge(s.prep, c)
                if c == 6:
                    dve.wait_ge(s.x_ready, X_V + CT)
                dve.wait_ge(s.kb_ps, c + 1)
                stt(kn, k, vec(c, V_KK), pb[(6, 7, 4)[c % 3]][:, :], ALU.mult, ALU.mult).then_inc(s.kn, 1)
                link.mark(ts(pa, a, vec(c, V_KA), omka[:, c:c + 1], ALU.mult, ALU.add))
                dve.wait_ge(s.kn, c + 1)
                link.mark(stt(lw, kn, -1.0, lw, ALU.mult, ALU.mult))
                link.wait()
                link.mark(tt(k, k, pa, ALU.mult))
                link(tt(a, a, kn, ALU.mult))
                dve.wait_ge(s.exps, 3 * c + 3)
                link.mark(tt(a, a, inv, ALU.mult))
                tt(k, k, inv, ALU.mult).then_inc(s.prep, 1)

            def r_tiles(b):
                dve.wait_ge(s.pe_step, 8 * (N_R + b + 1))
                for m in range(2):
                    c = 2 * b + m
                    dve.wait_ge(s.exps, 3 * c + 3)
                    tt(St[:, R_, c, :], St[:, R_, c, :], pb[2 * (1 - b % 2) + m][:, :], ALU.mult).then_inc(s.dense_v, 1)

            for c in range(CT):
                log_decays(c)
            mixes(4, MIX_R)
            kk_invert(0)
            prep(0)
            prep(1)
            r_tiles(0)
            prep(2)
            prep(3)
            kk_invert(1)
            r_tiles(1)
            prep(4)
            prep(5)
            r_tiles(2)
            mixes(5, MIX_V)
            r_tiles(3)
            prep(6)
            prep(7)
            dve.wait_ge(s.prep, 8)
            dve.wait_ge(s.vec_link, link.n)

            dve.wait_ge(s.pe_step, 8 * N_G2)
            tri = cst[:, C_TRS:C_TRS + CH]
            tri_in = cst[:, C_TRS + CH:C_TRS + 2 * CH]

            def scored(q, i):
                dve.wait_ge(s.sc_mm, 2 * q + i + 1)
                if q >= 3:
                    dve.wait_ge(s.y_mm, 4 * (q - 2))
                Lak, Lrb, Lrk = set_of(q)[3:6]
                bank = pb[3 + 2 * (q % 2) + i][:, :].rearrange("p (u t) -> p u t", t=P)
                if i == 0:
                    tt(Wq[q % 2][:, :, 0:CH], bank[:, :, 0:CH], tri[:, None, :].to_broadcast([P, QUAD, CH]), ALU.mult)\
                        .then_inc(s.sc_ev, 1)
                else:
                    for h in range(2):
                        r = slice(64 * h, 64 * h + 64)
                        tt(Lak[r, :, r], bank[r, :, 0:CH], tri[r, None, :].to_broadcast([64, QUAD, CH]), ALU.mult)\
                            .then_inc(s.sc_ev, 1)
                tt((Lrb, Lrk)[i][:, :, :], bank[:, :, CH:P], tri_in[:, None, :].to_broadcast([P, QUAD, CH]), ALU.mult)\
                    .then_inc(s.sc_ev, 1)

            def masked(q, lv):
                par, n = q % 2, q // 2
                if lv:
                    dve.wait_ge(s.w_mm[par], 6 * n + lv)
                    src = pb[4 + 2 * par][:, :].rearrange("p (u t) -> p u t", t=P)
                else:
                    dve.wait_ge(s.mn_rdy, 2 * q + 1)
                    src = Wq[par]
                tt(PT[par][:, :, :].rearrange("p u (h t) -> p u h t", h=2),
                   src[:, :, None, 0:CH].to_broadcast([P, QUAD, 2, CH]),
                   cst[:, None, C_LVL + lv * P:C_LVL + (lv + 1) * P].rearrange("p o (h t) -> p o h t", h=2)
                   .to_broadcast([P, QUAD, 2, CH]), ALU.mult).then_inc(s.pt_ev[par], 1)

            def next_level(q, lv):
                masked(q, lv)
                dve.tensor_copy(Wq[q % 2][:, :, :].rearrange("p u t -> p (u t)"), pb[4 + 2 * (q % 2)][:, :])\
                    .then_inc(s.w_ev[q % 2], 1)

            def state(o, j):
                J = 4 * o + j
                dve.wait_ge(s.ch, 3 * J + 3)
                if J:
                    dve.wait_ge(s.y_mm, J)
                g = gC[:, (o // 2) * 8 + J % 8:(o // 2) * 8 + J % 8 + 1]
                if J % 8 == 0:
                    ts(Hs[:, (J + 1) % 2, :], pb[0][:, 0:P], g, None, ALU.mult).then_inc(s.h_ev, 1)
                else:
                    dve.wait_ge(s.hg, J - J // 8)
                    stt(Hs[:, (J + 1) % 2, :], pb[0][:, 0:P], g, Hg[:, :], ALU.mult, ALU.add).then_inc(s.h_ev, 1)

            def bonus_product(c):
                if c == 0:
                    dve.wait_ge(s.tr_mm, 3 * NQ)
                if c >= 2:
                    dve.wait_ge(s.bon_ps, c - 1)
                stt(tmp[:, 2 + c % 2, :], St[:, R_, c, :], vec(c, V_RK), St[:, K_, c, :], ALU.mult, ALU.mult)\
                    .then_inc(s.pr_rdy, 1)

            def bonus_sum(c):
                if c + 1 < CT:
                    bonus_product(c + 1)
                dve.wait_ge(s.bon_ps, c + 1)
                if c == 0:
                    dve.wait_ge(s.bd_p, 4 * NQ)
                tt(St[:, V_, c, :], St[:, V_, c, :], pb[4][:, :], ALU.mult).then_inc(s.bon_v, 1)

            for i in range(NQ + 2):
                a, b, o = i, i - 1, i - 2
                first, second, chain = a < NQ, 0 <= b < NQ, o >= 0
                tile = 4 * (i - NQ) if i >= NQ else None
                if i == NQ:
                    bonus_product(0)
                if i < 3:
                    for k in (3, 6):
                        dve.memset(set_of(i)[k][:, :, :], 0.0).then_inc(s.set_zero, 1)
                    dve.wait_ge(s.set_zero, 2 * i + 2)
                if first:
                    scored(a, 0)
                    scored(a, 1)
                if second:
                    next_level(b, 4)
                if chain:
                    state(o, 0)
                if tile is not None:
                    bonus_sum(tile)
                if first:
                    masked(a, 0)
                if second:
                    next_level(b, 5)
                if chain:
                    state(o, 1)
                if tile is not None:
                    bonus_sum(tile + 1)
                if first:
                    next_level(a, 1)
                if chain:
                    state(o, 2)
                if tile is not None:
                    bonus_sum(tile + 2)
                if first:
                    next_level(a, 2)
                    next_level(a, 3)
                if chain:
                    state(o, 3)
                if tile == 0:
                    bonus_sum(tile + 3)

            bonus_sum(CT - 1)
            dve.memset(rstd[:, :], 0.0).then_inc(s.rows_0, 1)
            dve.wait_ge(s.gn_rt, 1)
            dve.wait_ge(s.vec_link, link.n)
            dve.reciprocal(rstd[0:16, :], rstd[0:16, :]).then_inc(s.gn_rs, 1)
            dve.wait_ge(s.yc_rdy, CT)
            dve.wait_ge(s.bon_v, CT)
            for c in range(CT):
                t = tmp[:, c % 2, :]
                dve.wait_ge(s.rb_ps, c + 1)
                if c >= 2:
                    dve.wait_ge(s.y_fin, c - 1)
                link(stt(t, X[:, c, 4:4 + S], vec(c, V_LNW), pb[4 + c % 2][:, :], ALU.mult, ALU.mult))
                link(stt(t, t, vec(c, V_LNB), St[:, V_, c, :], ALU.add, ALU.add))
                dve.wait_ge(s.pe_step, 8 * N_G2 + c + 1)
                if c >= 2:
                    dve.wait_ge(s.x_hi, X_Y + c - 1)
                    dve.wait_ge(s.x_ready, X_Y + c - 1)
                tt(tmp[:, 2 + c % 2, :], t, pb[6 + c % 2][:, :], ALU.mult).then_inc(s.y_fin, 1)
                if c:
                    low(c - 1, tmp[:, 2 + (c - 1) % 2, :], X_Y + c - 1)
            dve.wait_ge(s.y_fin, CT)
            low(CT - 1, tmp[:, 3, :], X_Y + CT - 1)

            squares = [0]

            def clear_acc(i):
                if i > 1:
                    dve.wait_ge(s.norm_ps, i - 1)
                link(dve.memset(tmp[:, 3, :], 0.0))

            def add_square(slot):
                i = squares[0]
                squares[0] += 1
                dve.wait_ge(s.sq_rdy, i + 1)
                if i:
                    dve.wait_ge(s.acc, i)
                tt(tmp[:, 3, :], tmp[:, 3, :], tmp[:, slot, :], ALU.add).then_inc(s.acc, 1)

            def residual(c, b, sem=s.dense_v, old=None):
                tt(X[:, c, 0:S], X[:, c, 0:S] if old is None else old, b, ALU.add).then_inc(sem, 1)

            def splits(gain, base, k0=0, k1=CT):
                for k in range(k0, k1):
                    dve.wait_ge(s.x_hi, base + k + 1)
                    stt(xl[:, k, :], X[:, k, 0:S], vec(k, gain), xh[:, k, :].bitcast(F32), ALU.mult, ALU.subtract)\
                        .then_inc(s.x_ready, 1)

            def proj(n0, i, gain, base):
                dve.wait_ge(s.x_ready, (X_Y if i == 1 else X_O) + CT)
                clear_acc(i)
                for b in range(4):
                    if b == 3:
                        splits(gain, base, 0, 6)
                    dve.wait_ge(s.pe_step, 8 * (n0 + b + 1))
                    for m in range(2):
                        residual(2 * b + m, pb[2 * (b % 2) + m][:, :], old=St[:, K_, 2 * b + m, :] if i == 1 else None)
                    if b == 3:
                        splits(gain, base, 6)
                    for m in range(2):
                        add_square(m)

            def mlp(layer, n0, ev0, gain, base):
                for half in range(2):
                    m0 = n0 + 16 * half
                    e = ev0 + 24 * half
                    h0 = 32 * layer + 16 * half
                    with dve.Fori(0, 4) as i:
                        for h in range(2):
                            done = 4 * i + 2 * h
                            dve.wait_ge(s.pe_step, 8 * (m0 + 2 * i + h + 1))
                            for m in range(2):
                                tt(tmp[:, m, :], pb[2 * h + m][:, :], rstd[:, :], ALU.mult).then_inc(s.dense_v, 1)
                            dve.wait_ge(s.hid_rdy, h0 + done)
                            for m in range(2):
                                dve.wait_ge(s.dense_v, e + done + m + 1)
                                stt(tmp[:, 2 + m, :], tmp[:, m, :], 0.0, tmp[:, m, :], ALU.max, ALU.mult)\
                                    .then_inc(s.hid_f, 1)
                            for m in range(2):
                                dve.wait_ge(s.hid_hi, h0 + done + m + 1)
                                tt(hid_l[:, bass.ds(done + m, 1), :], tmp[:, 2 + m:3 + m, :],
                                   hid_h[:, bass.ds(done + m, 1), :].bitcast(F32), ALU.subtract).then_inc(s.hid_rdy, 1)
                    m0 += 8
                    e += 16
                    if half == 1:
                        for k in range(2):
                            dve.wait_ge(s.p_hi, 2 * layer + k + 1)
                            tt(lora_l[:, k, :], pb[5 + k][:, :], lora_h[:, k, :].bitcast(F32), ALU.subtract).then_inc(s.p_rdy, 1)
                        dve.wait_ge(s.hid_rdy, h0 + 16)
                        clear_acc(2 + 3 * layer)
                    for g in range(4):
                        if half == 1 and g == 3:
                            splits(gain, base, 0, 6)
                        dve.wait_ge(s.pe_step, 8 * (m0 + 2 * g + 2))
                        for m in range(2):
                            residual(2 * g + m, pb[2 * (g % 2) + m][:, :])
                        if half == 1 and g == 3:
                            splits(gain, base, 6)
                        if half == 1:
                            for m in range(2):
                                add_square(m)

            def ple(layer, n, ni):
                norm_finish(ni)
                if layer == 0:
                    clear_acc(3)
                    dve.wait_ge(s.pe_step, 8 * n)
                    dve.memset(relb[BUCKETS:BUCKETS + 1, :], NEG).then_inc(s.far_row, 1)
                for b in range(4):
                    if layer == 0 and b == 3:
                        splits(V_KV, X_KV, 0, 6)
                        dve.wait_ge(s.bv_mm, 1)
                        dve.tensor_copy(bvec[:, 0:S], pb[5][0:8, 0:S]).then_inc(s.bv_ev, 1)
                        dve.tensor_copy(bvec[:, S:640], pb[6][0:8, 0:128]).then_inc(s.bv_ev, 1)
                    dve.wait_ge(s.pe_step, 8 * (n + 2 + b))
                    for m in range(2):
                        tt(tmp[:, m, :], pb[2 * (b % 2) + m][:, :], rstd[:, :], ALU.mult).then_inc(s.dense_v, 1)
                    for m in range(2):
                        c = 2 * b + m
                        dve.wait_ge(s.sig, 8 * layer + c + 1)
                        dve.wait_ge(s.dense_a, 36 + 8 * layer + c + 1)
                        link(tt(tmp[:, m, :], tmp[:, m, :], UP[:, c, :], ALU.mult))
                        residual(c, tmp[:, m, :], s.upd)
                        if layer == 0 and b < 3:
                            add_square(2)
                    if layer == 0 and b == 3:
                        splits(V_KV, X_KV, 6)
                        add_square(2)
                        add_square(2)
                    dve.wait_ge(s.upd, 8 * layer + 2 * b + 2)

            dve.wait_ge(s.x2_cp, 8)
            proj(N_WO, 1, V_N01, X_M0)
            norm_finish(1)
            mlp(0, L_MLP[0], 16, V_N02, X_P0)
            ple(0, L_MLP[0] + 32, 2)
            norm_finish(3)

            def head_norm(i):
                dve.wait_ge(s.qk_rt, i + 1)
                dve.reciprocal(tmp[:, i % 2, :], tmp[:, i % 2, :]).then_inc(s.qk_rs, 1)
                dve.wait_ge(s.qk_rs, i + 1)
                if i < 8:
                    stt(KT[:, i, :], KT[:, i, :], qk_gain, tmp[:, i % 2, :], ALU.mult, ALU.mult).then_inc(s.qk_n, 1)
                else:
                    a = slice(0, 64)
                    if i == 8:
                        dve.wait_ge(s.q0_zero, 1)
                    tt(QZ[0][a, i % 8, :], q_raw(i)[a, :], tmp[a, i % 2, :], ALU.mult).then_inc(s.qk_n, 1)

            def last_q(i):
                dve.wait_ge(s.q_ps, i - 12 + 1)
                if i == 12:
                    dve.wait_ge(s.q1_zero, 1)
                for m in range(2):
                    r = slice(64 * m, 64 * m + 64)
                    tt(QZ[m][r, i % 8, :], q_raw(i)[r, :], pb[7 - i % 2][r, :], ALU.mult).then_inc(s.qk_n, 1)

            def times_rstd(n, b, dsts, sem=s.dense_v):
                dve.wait_ge(s.pe_step, 8 * (n + 1))
                for m in range(2):
                    tt(dsts[m], pb[2 * (b % 2) + m][:, :], rstd[:, :], ALU.mult).then_inc(sem, 1)

            for b in range(4):
                if b:
                    head_norm(2 * b - 2)
                    head_norm(2 * b - 1)
                times_rstd(N_KS + b, b, [KT[:, 2 * b + m, :] for m in range(2)])
            for b in range(4):
                if b == 0:
                    head_norm(6)
                    head_norm(7)
                else:
                    dve.wait_ge(s.v_tr, 2 * b)
                dve.wait_ge(s.pe_step, 8 * (N_VS + b + 1))
                for m in range(2):
                    tt(tmp[:, 2 + m, :], pb[2 * (b % 2) + m][:, :], rstd[:, :], ALU.mult).then_inc(s.dense_v, 1)
            splits(V_N10, X_Q)
            for b in range(4):
                if b == 0:
                    dve.wait_ge(s.v_tr, 8)
                elif b < 3:
                    head_norm(8 + 2 * b - 2)
                    head_norm(8 + 2 * b - 1)
                    dve.wait_ge(s.q1_n, 2 * b)
                    dve.wait_ge(s.qk_n, 8 + 2 * b)
                times_rstd(N_Q + b, b, [q_raw(8 + 2 * b + m) for m in range(2)])
            dve.wait_ge(s.strip_in, 128)

            def logits(i):
                h, w = i // 4, (i % 4 + 1) * P
                if i >= 2:
                    dve.wait_ge(s.pexp, 2 * (i - 1))
                bias = strip[:, h, 0:w]
                bias = bass.AP(bias.tensor, bias.offset + w - 1, [bias.ap[0], [-1, w]])
                for m in range(2):
                    k = 2 * (i % 2) + m
                    dve.wait_ge(s.s_mm, 2 * i + m + 1)
                    dve.tensor_tensor_reduce(out=Lg[i % 2][:, m, 0:w], in0=pb[2 * (i % 2) + m][:, 0:w], in1=bias,
                                             scale=-1.0, scalar=3.0e38, op0=ALU.add, op1=ALU.min,
                                             accum_out=st_n[:, k:k + 1]).then_inc(s.lg, 1)

            def combine(i):
                w, k, pr = (i % 4 + 1) * P, 2 * (i % 2), Pr[i % 2]
                dve.wait_ge(s.scaled, i + 1)
                dve.wait_ge(s.rec, i + 1)
                if i >= 2:
                    dve.wait_ge(s.at_tr, i - 1)
                stt(At[:, i % 2, 0:w], pr[:, 0, 0:w], st_r[:, k:k + 1], pr[:, 1, 0:w], ALU.mult, ALU.subtract)\
                    .then_inc(s.at_rdy, 1)

            def invert_sums(i):
                k = 2 * (i % 2)
                dve.wait_ge(s.pexp, 2 * i + 2)
                dve.reciprocal(st_r[:, k:k + 2], st_l[:, k:k + 2]).then_inc(s.rec, 1)

            dve.wait_ge(s.pe_step, 8 * N_DO)
            dve.wait_ge(s.dense_v, 96)
            for i in range(32 + 2):
                if i < 32:
                    logits(i)
                if i >= 2:
                    combine(i - 2)
                if i == 3:
                    dve.wait_ge(s.qk_rt, 13)
                    dve.reciprocal(rstd[:, :], rstd[:, :]).then_inc(s.qk_rs, 1)
                if i in (6, 7):
                    last_q(2 * i)
                    last_q(2 * i + 1)
                if i == 10:
                    dve.memset(rstd[:, :], 0.0).then_inc(s.rows_0, 1)
                if 1 <= i <= 32:
                    invert_sums(i - 1)
            dve.wait_ge(s.o_rt, 1)
            dve.reciprocal(rstd[0:8, :], rstd[0:8, :]).then_inc(s.o_rs, 1)
            for h in range(8):
                dve.wait_ge(s.ob_ps, h + 1)
                if h == 0:
                    dve.wait_ge(s.o_cp, 8)
                if h >= 2:
                    dve.wait_ge(s.x_ready, X_O + h - 1)
                stt(tmp[:, 2 + h % 2, :], QZ[0][:, h, :], subg, pb[4 + h % 4][:, :], ALU.mult, ALU.mult).then_inc(s.o_f, 1)
                if h:
                    low(h - 1, tmp[:, 2 + (h - 1) % 2, :], X_O + h - 1)
            dve.wait_ge(s.o_f, 8)
            low(7, tmp[:, 3, :], X_O + 7)
            proj(N_DO, 4, V_N11, X_M1)
            norm_finish(4)
            mlp(1, L_MLP[1], 104, V_N12, X_P1)
            ple(1, L_MLP[1] + 32, 5)


_INS = ["x", "p", "norm_g", "mlp_w1", "mlp_w2", "ple_w_up", "ple_w_gate", "rwkv_mix", "rwkv_w_rkvo", "rwkv_w0",
        "rwkv_w1", "rwkv_w2", "rwkv_a0", "rwkv_a1", "rwkv_a2", "rwkv_g1", "rwkv_g2", "rwkv_k_k", "rwkv_k_a",
        "rwkv_r_k", "rwkv_ln_w", "rwkv_ln_b", "kv_norm_g", "w_k_shared", "w_v_shared", "k_norm_g", "diff_w_q",
        "diff_q_norm_g", "diff_lam", "diff_subln_g", "diff_w_o", "rel_bias"]


def build(nc, shapes):
    args = [nc.dram_tensor(f"in_{n}_dram", shape, F32, kind="ExternalInput").ap() for n, shape in shapes]
    out = nc.dram_tensor("out_0_dram", (1, S, D), F32, kind="ExternalOutput").ap()
    trunk(nc, *args, out)


def kernel(**inputs):
    import numpy as _np
    import concourse.bacc as _bacc
    from concourse.bass_utils import run_bass_kernel_spmd as _run

    nc = _bacc.Bacc("TRN2", target_bir_lowering=False, num_devices=1)
    arrays = {f"in_{n}_dram": _np.ascontiguousarray(inputs[n]) for n in _INS}
    arrays["in_consts_dram"] = shape_constants()
    build(nc, [(n, arrays[f"in_{n}_dram"].shape) for n in _INS + ["consts"]])
    r = _run(nc, [arrays], core_ids=[0])
    return r.results[0]["out_0_dram"]
```
